# Optimizing a Trainium2 kernel written in Bass

```python
import math
import jax, jax.numpy as jnp
from jax import lax
import numpy as np

D_MODEL = 1024
BATCH = 1
SEQ = 128
DEPTH = 2
DEC_BATCH = 1
DEC_SEQ = 512
PAST_LEN = 128

GRID_W = 64
MIX_WIDTH = D_MODEL
HEAD_DIM = 64
ATTN_HEADS = 4
KV_HEADS = 2
Q_PER_KV = ATTN_HEADS // KV_HEADS
ATTN_WIDTH = ATTN_HEADS * HEAD_DIM
WINDOW = 128
ATTN_BLOCK = 128
ROPE_THETA = 10000.0
SSD_HEAD_DIM = 64
SSD_WIDTH = MIX_WIDTH // 2
SSD_HEADS = SSD_WIDTH // SSD_HEAD_DIM
SSD_GROUPS = 2
SSD_STATE = 64
SSD_CONV = 5
SSD_CHUNK = 128
SSD_XBC = SSD_WIDTH + 2 * SSD_GROUPS * SSD_STATE
CONV_WIDTH = MIX_WIDTH - ATTN_WIDTH - SSD_WIDTH
CONV_KERNEL = 31
CONV_GROUPS = 4
IN_SIZES = (ATTN_WIDTH, KV_HEADS * HEAD_DIM, KV_HEADS * HEAD_DIM, SSD_WIDTH, SSD_XBC, SSD_HEADS, 2 * CONV_WIDTH)
IN_COLS = sum(IN_SIZES)
N_EXPERT_GROUPS = 4
EXPERTS_PER_GROUP = 8
N_EXPERTS = N_EXPERT_GROUPS * EXPERTS_PER_GROUP
TOP_K = 2
EXPERT_FF = 256
MOE_BLOCK = 128
EPS = 1e-6

kernel_name = 'hybrid_diffusion_prefix_trunk_step'

def rms_norm(x, w):
    xf = x.astype(jnp.float32)
    y = xf * lax.rsqrt(jnp.mean(xf * xf, axis=-1, keepdims=True) + EPS)
    return (y * w.astype(jnp.float32)).astype(x.dtype)

def group_layer_norm(x, w, b):
    shp = x.shape
    xg = x.reshape(*shp[:-1], CONV_GROUPS, shp[-1] // CONV_GROUPS).astype(jnp.float32)
    xc = xg - jnp.mean(xg, axis=-1, keepdims=True)
    y = (xc * lax.rsqrt(jnp.mean(xc * xc, axis=-1, keepdims=True) + EPS)).reshape(shp)
    return (y * w.astype(jnp.float32) + b.astype(jnp.float32)).astype(x.dtype)

def depthwise_conv(x, w, b):
    half = (w.shape[0] - 1) // 2
    y = lax.conv_general_dilated(x, w[:, None, :].astype(x.dtype), window_strides=(1,),
                                 padding=[(half, half)], dimension_numbers=('NWC', 'WIO', 'NWC'),
                                 feature_group_count=x.shape[-1])
    return y + b

def modulation(cond, w, b):
    m = jax.nn.silu(cond) @ w + b
    return jnp.split(m[..., None, :], 6, axis=-1)

def axial_rope(n_tokens):
    rows = n_tokens // GRID_W
    row = jnp.repeat(jnp.arange(rows, dtype=jnp.float32), GRID_W)
    col = jnp.tile(jnp.arange(GRID_W, dtype=jnp.float32), rows)
    n_freq = HEAD_DIM // 4
    inv = ROPE_THETA ** (-jnp.arange(n_freq, dtype=jnp.float32) / n_freq)
    ang = jnp.stack([row[:, None] * inv, col[:, None] * inv], axis=1)
    return jnp.cos(ang), jnp.sin(ang)

def apply_axial_rope(x, cos, sin):
    shp = x.shape
    xr = x.reshape(*shp[:-1], 2, 2, HEAD_DIM // 4)
    x1, x2 = xr[..., 0, :], xr[..., 1, :]
    c = cos[:, None].astype(x.dtype)
    s = sin[:, None].astype(x.dtype)
    return jnp.stack([x1 * c - x2 * s, x2 * c + x1 * s], axis=-2).reshape(shp)

def block_attention(q, k_ctx, v_ctx, sink, k_lat=None, v_lat=None):
    bsz, s_len = q.shape[0], q.shape[1]
    n_blk = s_len // ATTN_BLOCK
    c_len = k_ctx.shape[1]
    qb = q.reshape(bsz, n_blk, ATTN_BLOCK, KV_HEADS, Q_PER_KV, HEAD_DIM) * (HEAD_DIM ** -0.5)
    sink_logit = jnp.broadcast_to(sink.astype(jnp.float32).reshape(1, KV_HEADS, Q_PER_KV, 1, 1),
                                  (bsz, KV_HEADS, Q_PER_KV, ATTN_BLOCK, 1))
    local = k_lat is not None
    if local:
        zpad = jnp.zeros((bsz, ATTN_BLOCK, KV_HEADS, HEAD_DIM), k_lat.dtype)
        k_pad = jnp.concatenate([zpad, k_lat, zpad], axis=1)
        v_pad = jnp.concatenate([zpad.astype(v_lat.dtype), v_lat, zpad.astype(v_lat.dtype)], axis=1)
        q_off = jnp.arange(ATTN_BLOCK)
        k_off = jnp.arange(3 * ATTN_BLOCK) - ATTN_BLOCK
        band = jnp.abs(k_off[None, :] - q_off[:, None]) <= WINDOW

    def one_block(b):
        qblk = lax.dynamic_index_in_dim(qb, b, axis=1, keepdims=False)
        parts = [jnp.einsum('bqkgd,bckd->bkgqc', qblk, k_ctx).astype(jnp.float32)]
        if local:
            k_blk = lax.dynamic_slice_in_dim(k_pad, b * ATTN_BLOCK, 3 * ATTN_BLOCK, axis=1)
            v_blk = lax.dynamic_slice_in_dim(v_pad, b * ATTN_BLOCK, 3 * ATTN_BLOCK, axis=1)
            pos = b * ATTN_BLOCK + k_off
            valid = band & ((pos >= 0) & (pos < s_len))[None, :]
            s_loc = jnp.einsum('bqkgd,bskd->bkgqs', qblk, k_blk).astype(jnp.float32)
            parts.append(jnp.where(valid, s_loc, -jnp.inf))
        p = jax.nn.softmax(jnp.concatenate(parts + [sink_logit], axis=-1), axis=-1).astype(v_ctx.dtype)
        out = jnp.einsum('bkgqc,bckd->bqkgd', p[..., :c_len], v_ctx)
        if local:
            out = out + jnp.einsum('bkgqs,bskd->bqkgd', p[..., c_len:c_len + 3 * ATTN_BLOCK], v_blk)
        return out

    out = lax.map(one_block, jnp.arange(n_blk))
    return jnp.moveaxis(out, 0, 1).reshape(bsz, s_len, ATTN_WIDTH)

def ssd_scan(x, log_a, bm, cm, h0):
    bsz, l_len, n_h, p_dim = x.shape
    t = SSD_CHUNK
    nc = l_len // t
    xc = x.reshape(bsz, nc, t, n_h, p_dim)
    bc = bm.reshape(bsz, nc, t, n_h, SSD_STATE)
    cc = cm.reshape(bsz, nc, t, n_h, SSD_STATE)
    a_cum = jnp.cumsum(log_a.reshape(bsz, nc, t, n_h).transpose(0, 3, 1, 2), axis=-1)
    tri = jnp.tril(jnp.ones((t, t), dtype=bool))
    seg = a_cum[..., :, None] - a_cum[..., None, :]
    l_mat = jnp.exp(jnp.where(tri, seg, -jnp.inf)).astype(x.dtype)
    scores = jnp.einsum('bclhn,bcshn->bhcls', cc, bc) * l_mat
    y_diag = jnp.einsum('bhcls,bcshp->bclhp', scores, xc)
    decay_to_end = jnp.exp(a_cum[..., -1:] - a_cum).astype(x.dtype)
    chunk_states = jnp.einsum('bclhn,bhcl,bclhp->bchpn', bc, decay_to_end, xc)
    chunk_decay = jnp.exp(a_cum[..., -1])

    def step(h, inp):
        s_c, d_c = inp
        return h * d_c[..., None, None] + s_c.astype(jnp.float32), h

    h_final, h_starts = lax.scan(step, h0.astype(jnp.float32),
                                 (jnp.moveaxis(chunk_states, 1, 0), jnp.moveaxis(chunk_decay, 2, 0)))
    decay_in = jnp.exp(a_cum).astype(x.dtype)
    y_off = jnp.einsum('bclhn,cbhpn,bhcl->bclhp', cc, h_starts.astype(x.dtype), decay_in)
    return (y_diag + y_off).reshape(bsz, l_len, n_h, p_dim), h_final.astype(h0.dtype)

def ssd_direction(xh, dt_raw, bm, cm, dt_bias, a_log, d_skip, h0):
    dt = jax.nn.softplus(dt_raw.astype(jnp.float32) + dt_bias.astype(jnp.float32))
    log_a = dt * (-jnp.exp(a_log.astype(jnp.float32)))
    y, h_t = ssd_scan(xh * dt[..., None].astype(xh.dtype), log_a, bm, cm, h0)
    return y + d_skip[:, None] * xh, h_t

def grouped_expert_mlp(x, idx, w, wg, wu, wd):
    n_tok, k = idx.shape
    n_assign = n_tok * k
    flat = idx.reshape(-1)
    order = jnp.argsort(flat)
    sorted_e = flat[order]
    counts = jnp.bincount(flat, length=N_EXPERTS)
    padded = (counts + MOE_BLOCK - 1) // MOE_BLOCK * MOE_BLOCK
    pad_end = jnp.cumsum(padded)
    pad_start = pad_end - padded
    start = jnp.cumsum(counts) - counts
    slot_sorted = pad_start[sorted_e] + (jnp.arange(n_assign) - start[sorted_e])
    n_blocks = -(-n_assign // MOE_BLOCK) + N_EXPERTS
    src_token = jnp.full((n_blocks * MOE_BLOCK,), n_tok, jnp.int32).at[slot_sorted].set((order // k).astype(jnp.int32))
    x_pad = jnp.concatenate([x, jnp.zeros((1, x.shape[1]), x.dtype)], axis=0)
    xs = x_pad[src_token].reshape(n_blocks, MOE_BLOCK, x.shape[1])
    block_e = jnp.minimum(jnp.searchsorted(pad_end, jnp.arange(n_blocks) * MOE_BLOCK, side='right'), N_EXPERTS - 1)

    def run(args):
        xb, e = args
        return (jax.nn.silu(xb @ wg[e]) * (xb @ wu[e])) @ wd[e]

    ys = lax.map(run, (xs, block_e)).reshape(n_blocks * MOE_BLOCK, x.shape[1])
    slot = jnp.zeros((n_assign,), slot_sorted.dtype).at[order].set(slot_sorted).reshape(n_tok, k)
    return jnp.einsum('nk,nkd->nd', w, ys[slot])

def hierarchical_moe(x, lp):
    bsz, l_len, d = x.shape
    xt = x.reshape(-1, d)
    g_logits = (xt @ lp['rg_w'] + lp['rg_b']).astype(jnp.float32)
    _, g_idx = lax.top_k(g_logits, 1)
    p_grp = jnp.take_along_axis(jax.nn.softmax(g_logits, axis=-1), g_idx, axis=-1)
    e_logits = (xt @ lp['re_w'] + lp['re_b']).astype(jnp.float32).reshape(-1, N_EXPERT_GROUPS, EXPERTS_PER_GROUP)
    e_logits = jnp.take_along_axis(e_logits, g_idx[:, :, None], axis=1)[:, 0]
    top_v, top_i = lax.top_k(e_logits, TOP_K)
    weights = (p_grp * jax.nn.softmax(top_v, axis=-1)).astype(x.dtype)
    expert_idx = g_idx * EXPERTS_PER_GROUP + top_i
    y = grouped_expert_mlp(xt, expert_idx, weights, lp['e_wg'], lp['e_wu'], lp['e_wd'])
    return y.reshape(bsz, l_len, d)

def mixer(h, lp, ctx_k, ctx_v, ctx_state, rope):
    bsz, l_len, _ = h.shape
    proj = h @ lp['w_in']
    q, k, v, z, xbc, dt_raw, glu = jnp.split(proj, np.cumsum(IN_SIZES)[:-1].tolist(), axis=-1)
    q = rms_norm(q.reshape(bsz, l_len, ATTN_HEADS, HEAD_DIM), lp['q_norm'])
    k = rms_norm(k.reshape(bsz, l_len, KV_HEADS, HEAD_DIM), lp['k_norm'])
    v = v.reshape(bsz, l_len, KV_HEADS, HEAD_DIM)
    if ctx_k is None:
        attn = block_attention(q, k, v, lp['sink'])
        h0 = jnp.zeros((bsz, 2, SSD_HEADS, SSD_HEAD_DIM, SSD_STATE), h.dtype)
    else:
        cos, sin = rope
        attn = block_attention(apply_axial_rope(q, cos, sin), ctx_k, ctx_v, lp['sink'],
                               apply_axial_rope(k, cos, sin), v)
        h0 = ctx_state
    xbc = jax.nn.silu(depthwise_conv(xbc, lp['ssd_conv_w'], lp['ssd_conv_b']))
    xs, bm, cm = jnp.split(xbc, [SSD_WIDTH, SSD_WIDTH + SSD_GROUPS * SSD_STATE], axis=-1)
    xs = xs.reshape(bsz, l_len, SSD_HEADS, SSD_HEAD_DIM)
    hpg = SSD_HEADS // SSD_GROUPS
    bm = jnp.repeat(bm.reshape(bsz, l_len, SSD_GROUPS, SSD_STATE), hpg, axis=2)
    cm = jnp.repeat(cm.reshape(bsz, l_len, SSD_GROUPS, SSD_STATE), hpg, axis=2)
    y_f, h_f = ssd_direction(xs, dt_raw, bm, cm, lp['dt_bias'][0], lp['a_log'][0], lp['d_skip'][0], h0[:, 0])
    y_b, h_b = ssd_direction(jnp.flip(xs, 1), jnp.flip(dt_raw, 1), jnp.flip(bm, 1), jnp.flip(cm, 1),
                             lp['dt_bias'][1], lp['a_log'][1], lp['d_skip'][1], h0[:, 1])
    y = (y_f + jnp.flip(y_b, 1)).reshape(bsz, l_len, SSD_WIDTH) * jax.nn.silu(z)
    y = rms_norm(y.reshape(bsz, l_len, SSD_GROUPS, -1), lp['ssd_norm'].reshape(SSD_GROUPS, -1)).reshape(bsz, l_len, SSD_WIDTH)
    a, g = jnp.split(glu, 2, axis=-1)
    u = depthwise_conv(a * jax.nn.sigmoid(g), lp['cm_conv_w'], lp['cm_conv_b'])
    u = jax.nn.silu(group_layer_norm(u, lp['cm_norm_w'], lp['cm_norm_b']))
    out = jnp.concatenate([attn, y, u], axis=-1) @ lp['w_out']
    return out, k, v, jnp.stack([h_f, h_b], axis=1)

def trunk_layer(x, cond, lp, ctx_k=None, ctx_v=None, ctx_state=None, rope=None):
    sh1, sc1, g1, sh2, sc2, g2 = modulation(cond, lp['mod_w'], lp['mod_b'])
    mix, k, v, st = mixer(rms_norm(x, lp['norm1']) * (1 + sc1) + sh1, lp, ctx_k, ctx_v, ctx_state, rope)
    x = x + g1 * mix
    x = x + g2 * hierarchical_moe(rms_norm(x, lp['norm2']) * (1 + sc2) + sh2, lp)
    return x, k, v, st

def setup_inputs(seed: int = 0) -> dict:
    key = jax.random.key(seed)
    keys = list(jax.random.split(key, 40))

    def nrm(shape, scale):
        return jax.random.normal(keys.pop(), shape, jnp.float32) * scale

    dt0 = jnp.exp(jax.random.uniform(keys.pop(), (DEPTH, 2, SSD_HEADS), jnp.float32,
                                     minval=math.log(1e-3), maxval=math.log(1e-1)))
    a0 = jax.random.uniform(keys.pop(), (DEPTH, 2, SSD_HEADS), jnp.float32, minval=1.0, maxval=16.0)
    d = D_MODEL
    return {
        'x_prompt': nrm((BATCH, SEQ, d), 1.0),
        'x_sample': nrm((DEC_BATCH, DEC_SEQ, d), 1.0),
        'c': nrm((DEC_BATCH, d), 1.0),
        'cache_k': nrm((DEC_BATCH, DEPTH, PAST_LEN, KV_HEADS, HEAD_DIM), 1.0),
        'cache_v': nrm((DEC_BATCH, DEPTH, PAST_LEN, KV_HEADS, HEAD_DIM), 1.0),
        'state_ssm': nrm((DEC_BATCH, DEPTH, 2, SSD_HEADS, SSD_HEAD_DIM, SSD_STATE), 0.3),
        'c_ctx': nrm((d,), 1.0),
        'mod_w': nrm((DEPTH, d, 6 * d), 0.5 * d ** -0.5),
        'mod_b': nrm((DEPTH, 6 * d), 0.02),
        'norm1_w': 1.0 + nrm((DEPTH, d), 0.02),
        'norm2_w': 1.0 + nrm((DEPTH, d), 0.02),
        'w_in': nrm((DEPTH, d, IN_COLS), d ** -0.5),
        'q_norm_w': 1.0 + nrm((DEPTH, HEAD_DIM), 0.02),
        'k_norm_w': 1.0 + nrm((DEPTH, HEAD_DIM), 0.02),
        'attn_sink': nrm((DEPTH, ATTN_HEADS), 0.5),
        'ssd_conv_w': nrm((DEPTH, SSD_CONV, SSD_XBC), SSD_CONV ** -0.5),
        'ssd_conv_b': nrm((DEPTH, SSD_XBC), 0.02),
        'ssd_dt_bias': dt0 + jnp.log(-jnp.expm1(-dt0)),
        'ssd_a_log': jnp.log(a0),
        'ssd_d': 1.0 + nrm((DEPTH, 2, SSD_HEADS), 0.1),
        'ssd_norm_w': 1.0 + nrm((DEPTH, SSD_WIDTH), 0.02),
        'cm_conv_w': nrm((DEPTH, CONV_KERNEL, CONV_WIDTH), CONV_KERNEL ** -0.5),
        'cm_conv_b': nrm((DEPTH, CONV_WIDTH), 0.02),
        'cm_norm_w': 1.0 + nrm((DEPTH, CONV_WIDTH), 0.02),
        'cm_norm_b': nrm((DEPTH, CONV_WIDTH), 0.02),
        'w_out': nrm((DEPTH, MIX_WIDTH, d), MIX_WIDTH ** -0.5),
        'router_group_w': nrm((DEPTH, d, N_EXPERT_GROUPS), d ** -0.5),
        'router_group_b': nrm((DEPTH, N_EXPERT_GROUPS), 0.01),
        'router_expert_w': nrm((DEPTH, d, N_EXPERTS), d ** -0.5),
        'router_expert_b': nrm((DEPTH, N_EXPERTS), 0.01),
        'expert_w_gate': nrm((DEPTH, N_EXPERTS, d, EXPERT_FF), d ** -0.5),
        'expert_w_up': nrm((DEPTH, N_EXPERTS, d, EXPERT_FF), d ** -0.5),
        'expert_w_down': nrm((DEPTH, N_EXPERTS, EXPERT_FF, d), EXPERT_FF ** -0.5),
    }

def reference(x_prompt, x_sample, c, cache_k, cache_v, state_ssm, c_ctx, mod_w, mod_b, norm1_w, norm2_w,
              w_in, q_norm_w, k_norm_w, attn_sink, ssd_conv_w, ssd_conv_b, ssd_dt_bias, ssd_a_log, ssd_d,
              ssd_norm_w, cm_conv_w, cm_conv_b, cm_norm_w, cm_norm_b, w_out, router_group_w, router_group_b,
              router_expert_w, router_expert_b, expert_w_gate, expert_w_up, expert_w_down):
    rope = axial_rope(x_sample.shape[1])
    y_prompt, y_sample = x_prompt, x_sample
    ks, vs, sts = [], [], []
    for l in range(DEPTH):
        lp = {
            'mod_w': mod_w[l], 'mod_b': mod_b[l], 'norm1': norm1_w[l], 'norm2': norm2_w[l],
            'w_in': w_in[l], 'q_norm': q_norm_w[l], 'k_norm': k_norm_w[l], 'sink': attn_sink[l],
            'ssd_conv_w': ssd_conv_w[l], 'ssd_conv_b': ssd_conv_b[l], 'dt_bias': ssd_dt_bias[l],
            'a_log': ssd_a_log[l], 'd_skip': ssd_d[l], 'ssd_norm': ssd_norm_w[l],
            'cm_conv_w': cm_conv_w[l], 'cm_conv_b': cm_conv_b[l], 'cm_norm_w': cm_norm_w[l],
            'cm_norm_b': cm_norm_b[l], 'w_out': w_out[l],
            'rg_w': router_group_w[l], 'rg_b': router_group_b[l],
            're_w': router_expert_w[l], 're_b': router_expert_b[l],
            'e_wg': expert_w_gate[l], 'e_wu': expert_w_up[l], 'e_wd': expert_w_down[l],
        }
        y_prompt, k_l, v_l, st_l = trunk_layer(y_prompt, c_ctx, lp)
        ks.append(k_l)
        vs.append(v_l)
        sts.append(st_l)
        y_sample, _, _, _ = trunk_layer(y_sample, c, lp, cache_k[:, l], cache_v[:, l], state_ssm[:, l], rope)
    new_cache_k = jnp.stack(ks, axis=1)
    new_cache_v = jnp.stack(vs, axis=1)
    new_state_ssm = jnp.stack(sts, axis=1)
    return (y_prompt, y_sample, new_cache_k, new_cache_v, new_state_ssm)


_drawn_inputs = setup_inputs


def setup_inputs(seed=0):
    import zlib

    import numpy as np

    out = dict(_drawn_inputs(seed))
    spreads = {}
    factors = {'cache_k': 5.104,
     'cache_v': 3.817,
     'norm2_w': 3.897,
     'q_norm_w': 8.0,
     'k_norm_w': 2.944,
     'attn_sink': 8.0,
     'ssd_d': 3.178,
     'ssd_norm_w': 5.265,
     'cm_conv_b': 7.826,
     'cm_norm_w': 8.0,
     'cm_norm_b': 8.0,
     'router_group_b': 6.928,
     'router_expert_b': 8.0}
    for name, (base, spread) in spreads.items():
        noise = np.random.default_rng([zlib.crc32(name.encode()), seed]).standard_normal(out[name].shape)
        drawn = base * np.exp(spread * noise) if base else spread * noise
        out[name] = __import__('jax').numpy.asarray(drawn.astype(out[name].dtype))
    for name, factor in factors.items():
        out[name] = (out[name] * factor).astype(out[name].dtype)
    return out
```

```python
from contextlib import ExitStack

import numpy as np

import concourse.bass as bass
from concourse import mybir

ALU = mybir.AluOpType
ACT = mybir.ActivationFunctionType
F32 = mybir.dt.float32
I32 = mybir.dt.int32
AX = mybir.AxisListType.X

P = 128
D = 1024
KD = D // P
DEPTH = 2
CTX, LAT = 128, 512
NTOK = CTX + LAT
NT = NTOK // P
NLT = LAT // P
HD = 64
NH = 8
QH, KVH = 4, 2
EPS = 1e-6
BIG = 1e30

NE, EPG, NG = 32, 8, 4
FF = 256
NOVF = (2 * NTOK - NE) // P
NBLK = NE + NOVF
NOROW = 100000

SLOT = 2048
RING = 6
MODN = 6 * D // 256
INN = 9
OUTN = 4
LAYERN = INN + OUTN + 3 * NE

PAR = {}
PARN = 0
for _name, _n in (("norm1", KD), ("qw", HD), ("kw", HD), ("sink", QH), ("cw", 6 * 5), ("cb", 6),
                  ("gw", 2 * 31), ("gb", 2), ("dtb", 16), ("alog", 16), ("dskip", 16),
                  ("snorm", 512), ("lnw", 256), ("lnb", 256), ("rw", KD * 36), ("rb", 36),
                  ("wdt", KD * 8), ("kctx", P), ("vctx", P), ("h0", 512)):
    PAR[_name] = (PARN, _n)
    PARN += _n
XPAD, GPAD = 2, 15
XLEN, GLEN = NTOK + 3 * XPAD, NTOK + 3 * GPAD
XOUT, GOUT = NTOK + XPAD, NTOK + GPAD


def build(nc, x, stream, par, cond, modb, n2row, rope, y_out, k_out, v_out, st_out):
    with ExitStack() as ctx:
        def sb(name, shape, dt=F32):
            return ctx.enter_context(nc.sbuf_tensor(name, shape, dt))

        def sem(name):
            return ctx.enter_context(nc.semaphore(name))

        PS = [ctx.enter_context(nc.psum_tensor(f"bank{i}", [P, 512], F32)) for i in range(8)]
        mod_dram = nc.dram_tensor("mod_rows", (DEPTH, 2, 6 * D), F32, kind="Internal").ap()
        h2_dram = nc.dram_tensor("moe_in", (NTOK, D), F32, kind="Internal").ap()
        slot_dram = nc.dram_tensor("slot_rows", (P * NBLK, 1), I32, kind="Internal").ap()
        yk_dram = nc.dram_tensor("moe_out", (2 * NTOK, D), F32, kind="Internal").ap()

        X = sb("X", [P, NT, D])
        HT = sb("HT", [P, KD, NTOK])
        CAT = sb("CAT", [P, NT, D])
        ring = sb("ring", [P, RING, SLOT])
        RA = sb("RA", [P, 2, D])
        RB = sb("RB", [P, 2, D])
        prm = sb("prm", [P, PARN])
        ident = sb("ident", [P, P])
        triF = sb("triF", [P, P])
        triB = sb("triB", [P, P])
        triS = sb("triS", [P, P])
        ones = sb("ones", [P, P])
        negF = sb("negF", [P, P])
        negB = sb("negB", [P, P])
        iota = sb("iota", [P, NE])
        ropeT = sb("ropeT", [P, 2, NLT, HD])
        condT = sb("condT", [P, KD, 2])
        modc = sb("modc", [P, 2, 2, KD])
        sm = sb("sm", [P, 1700])

        UW = 15400
        U = sb("U", [P, UW])

        def view(off, *shape, parts=P):
            n = int(np.prod(shape))
            assert off + n <= UW, (off, n)
            a = U[0:parts, off:off + n]
            if len(shape) == 1:
                return a
            names = "abcd"[:len(shape)]
            return a.rearrange(f"p ({' '.join(names)}) -> p {' '.join(names)}", **dict(zip(names[1:], shape[1:])))

        def small(off, *shape):
            n = int(np.prod(shape))
            assert off + n <= 1700
            a = sm[:, off:off + n]
            if len(shape) == 1:
                return a
            names = "abcd"[:len(shape)]
            return a.rearrange(f"p ({' '.join(names)}) -> p {' '.join(names)}", **dict(zip(names[1:], shape[1:])))

        def pr(name, *shape):
            o, n = PAR[name]
            a = prm[:, o:o + n]
            if not shape:
                return a
            names = "abcd"[:len(shape)]
            return a.rearrange(f"p ({' '.join(names)}) -> p {' '.join(names)}", **dict(zip(names[1:], shape[1:])))

        qkv = view(0, NT, 512)
        xp = view(2560, 6, XLEN)
        xs = view(2560, NT, 512)
        btok = view(2560 + NT * 512, NT, P)
        o = 2560 + 6 * XLEN
        gp = view(o, 2, GLEN)
        uc = view(o + 2 * GLEN, 2, GOUT)
        hs = view(o, 2, NLT, 256)
        o += 2 * GLEN + 2 * GOUT
        qkT = view(o, 3, NTOK)
        o += 3 * NTOK
        TMP = o
        xn = view(TMP, 2, D)
        sqs = view(TMP + 2 * D, D)
        sg = view(TMP + 3 * D, 2, NTOK)
        t1 = view(TMP, NT, 384)
        t2 = view(TMP + NT * 384, NLT, 384)
        Pm = view(TMP, QH, 512)
        PTs = view(TMP + 2048, 2, 4, P)
        LW = view(TMP, 4, 4, P)
        xdt = view(TMP + 2048, 2, 512)
        xw = view(TMP + 3072, 2, 512)
        gts = view(TMP + 4096, 2, P)
        off1, off2 = RB[:, 0, 0:512], RB[:, 0, 512:1024]
        hsc, stc = RB[:, 1, 0:256], RB[:, 1, 512:1024].rearrange("p (a b) -> p a b", a=2)
        big = view(TMP, NT, 512)
        wtmp = view(TMP, 2, 512)
        mrow = view(0, DEPTH, 6 * D, parts=2)
        xg = view(0, 2, D)
        xgT = view(2 * D, 2, KD, P)
        hh = view(4 * D, 2, FF)
        sgate = view(4 * D + 512, 2, FF)
        hhT = view(4 * D + 1024, 2, 2, P)
        yb = view(4 * D + 1536, 2, D)
        yl = view(6 * D + 1536, 2, 2, D)
        mt = view(10 * D + 1536, 2, D)
        nrow2 = view(12 * D + 1536, D)
        cidx = sb("cidx", [P, 1], I32)
        slots = sb("slots", [P, NBLK], I32)
        gidx = sb("gidx", [P, NBLK], I32)
        svi = sb("svi", [P, 2, NT], I32)
        ovn = sb("ovn", [P, 1 + NOVF], I32)
        gcur, scur = sb("gcur", [P, 1], I32), sb("scur", [P, 1], I32)
        wov_gu = CAT[:].rearrange("p a b -> p (a b)")[:, 0:2 * SLOT].rearrange("p (j k n) -> p j k n", j=2, k=KD)
        wov_d = HT[:].rearrange("p a b -> p (a b)")[:, 0:SLOT].rearrange("p (k n) -> p k n", k=2)
        sai = sb("sai", [P, 2, NT], I32)

        names = ("ld0 ld_par ld_rows ld_modc cst bar silu_c mod_ps mod_sb mod_st xn_ready xT_ps hT_a hT_d "
                 "pj_ps pj_sb ch_ps ch_sb ch_a sg_rd conv_rdy convs_rdy xt_ps xt_sb uconv qk_rdy qkT_ps qkT_sb "
                 "att_s att_m att_exp att_es att_pt ptc_a ptc_d att_pv att_o kv_st st_st dt_x dt_e la_rdy cum_ps "
                 "cum_sb dec_rdy gt_ps gt_sb r_ps l_rdy w_rdy xd_rdy y_ps s_ps y_sb off_ps off_sb hs_rdy st_rdy "
                 "ut_ps ut_sb ct_ps ct_sb_a ct_sb_d wo_ps wo_sb cat_a cat_b h2_rdy h2_st h2T_ps h2T_a h2T_d lg_ps lg_sb "
                 "ge_x ge_y te_x te_y m_rdy rank_ps slot_rdy slot_init slot_st slot_ld gidx_rdy "
                 "xgT_ps xgT_sb gu_ps sgate_rdy hh_rdy hhT_ps hhT_sb y2_ps y2_sb_a y2_sb_d yg_used yst ov_go y_ld0 y_ld1 y_used out_st")
        S = {n: sem(n) for n in names.split()}
        for l in range(DEPTH):
            for n in "seen w gather pe x gate h hT y scatter".split():
                S[f"ov_{n}{l}"] = sem(f"ov_{n}{l}")
        full = [sem(f"ring_full{i}") for i in range(RING)]
        free = [sem(f"ring_free{i}") for i in range(RING)]
        gfull = [sem(f"gather_full{i}") for i in range(2)]
        yfree = [sem(f"scatter_done{i}") for i in range(2)]
        block = ctx.enter_context(nc.Block())

        def base(l):
            return DEPTH * MODN + l * LAYERN

        class Bars:
            def __init__(self, e):
                self.e, self.n = e, 0

            def __call__(self):
                self.n += 1
                self.e.drain().then_inc(S["bar"], 1)
                self.e.wait_ge(S["bar"], 4 * self.n)

        def cnd(t):
            return 0 if t == 0 else 1

        @block.sync
        def _(e):
            def load(q):
                if q >= RING:
                    e.wait_ge(free[q % RING], q // RING)
                e.dma_start(ring[:, q % RING, :], stream[q]).then_inc(full[q % RING], 16)

            e.dma_start(condT[:], cond).then_inc(S["ld0"], 16)
            e.dma_start(X[:], x).then_inc(S["ld0"], 16)
            e.dma_start(ropeT[:], rope).then_inc(S["ld0"], 16)
            e.dma_start(mrow, modb).then_inc(S["ld0"], 16)
            for q in range(DEPTH * MODN):
                load(q)
            for l in range(DEPTH):
                b = base(l)
                for q in range(b, b + INN + OUTN):
                    load(q)
                b += INN + OUTN
                for q in range(b, b + RING):
                    load(q)
                b += RING
                e.wait_ge(S["ov_go"], l + 1)
                some = e.value_load(ovn[0:1, 0:1], min_val=0, max_val=NOVF)
                with e.If(some > 0):
                    with e.Fori(0, NOVF) as i:
                        tile0 = e.value_load(ovn[0:1, bass.ds(i + 1, 1)], min_val=0, max_val=DEPTH * (MODN + LAYERN) - 3)
                        e.wait_ge(S[f"ov_pe{l}"], 4 * i + 1)
                        for j in range(2):
                            e.dma_start(wov_gu[:, j].rearrange("p k n -> p (k n)"),
                                        stream[bass.ds(tile0 + j, 1)].rearrange("a p n -> (a p) n")).then_inc(S[f"ov_w{l}"], 16)
                        e.dma_start(wov_d.rearrange("p k n -> p (k n)"),
                                    stream[bass.ds(tile0 + 2, 1)].rearrange("a p n -> (a p) n")).then_inc(S[f"ov_w{l}"], 16)
                with e.Fori(0, 3 * NE // RING - 1) as i:
                    for j in range(RING):
                        q = b + j
                        at = e.snap(i * RING + q)
                        e.wait_ge(free[q % RING], q // RING + i)
                        e.dma_start(ring[:, q % RING, :], stream[bass.ds(at, 1)].rearrange("a p n -> (a p) n")
                                    ).then_inc(full[q % RING], 16)

        @block.gpsimd
        def _(e):
            bar = Bars(e)
            c = S["cst"]
            for m in (ident, triF, triB, triS, ones):
                e.memset(m[:], 0.0 if m is ident else 1.0).then_inc(c, 1)
            e.memset(negF[:], 0.0).then_inc(c, 1)
            e.memset(negB[:], 0.0).then_inc(c, 1)
            e.iota(iota[:], [[1, NE]], base=0, channel_multiplier=0, allow_small_or_imprecise_dtypes=True).then_inc(c, 1)
            e.iota(svi[:], [[NTOK, 2], [P, NT]], base=0, channel_multiplier=1).then_inc(c, 1)
            e.wait_ge(c, 9)
            e.affine_select(out=ident[:], in_=ident[:], compare_op=ALU.not_equal, fill=1.0, base=0,
                            pattern=[[-1, P]], channel_multiplier=1).then_inc(c, 1)
            e.affine_select(out=triF[:], in_=triF[:], compare_op=ALU.is_ge, fill=0.0, base=0,
                            pattern=[[1, P]], channel_multiplier=-1).then_inc(c, 1)
            e.affine_select(out=triB[:], in_=triB[:], compare_op=ALU.is_ge, fill=0.0, base=0,
                            pattern=[[-1, P]], channel_multiplier=1).then_inc(c, 1)
            e.affine_select(out=triS[:], in_=triS[:], compare_op=ALU.is_gt, fill=0.0, base=0,
                            pattern=[[1, P]], channel_multiplier=-1).then_inc(c, 1)
            e.affine_select(out=negF[:], in_=negF[:], compare_op=ALU.is_ge, fill=-BIG, base=0,
                            pattern=[[1, P]], channel_multiplier=-1).then_inc(c, 1)
            e.affine_select(out=negB[:], in_=negB[:], compare_op=ALU.is_ge, fill=-BIG, base=0,
                            pattern=[[-1, P]], channel_multiplier=1).then_inc(c, 1)
            e.wait_ge(S["mod_sb"], DEPTH * 12)
            e.dma_start(mod_dram.rearrange("l c n -> c l n"), mrow).then_inc(S["mod_st"], 16)
            e.wait_ge(S["mod_st"], 16)
            bar()
            for l in range(DEPTH):
                e.dma_start(prm[:], par[l]).then_inc(S["ld_par"], 16)
                for cc in range(2):
                    for j in range(2):
                        e.dma_start(modc[:, cc, j, :], mod_dram[l, cc, j * D:(j + 1) * D].rearrange("(p k) -> p k", p=P)
                                    ).then_inc(S["ld_modc"], 16)
                    e.dma_start(RA[:, cc, :], mod_dram[l, cc:cc + 1, 2 * D:3 * D].to_broadcast((P, D))
                                ).then_inc(S["ld_rows"], 16)
                for v, h in ((xp, XPAD), (gp, GPAD)):
                    for a in (0, h + CTX, 2 * h + NTOK):
                        e.memset(v[:, :, a:a + h], 0.0)
                bar()
                e.wait_ge(S["qk_rdy"], 2 * l + 1)
                e.dma_start(k_out[l], qkv[:, 0, 256:384]).then_inc(S["kv_st"], 16)
                e.dma_start(v_out[l], qkv[:, 0, 384:512]).then_inc(S["kv_st"], 16)
                e.wait_ge(S["kv_st"], 32 * (l + 1))
                bar()
                e.wait_ge(S["st_rdy"], l + 1)
                e.dma_start(st_out[l], stc).then_inc(S["st_st"], 16)
                e.wait_ge(S["st_st"], 16 * (l + 1))
                bar()
                bar()
                for cc in range(2):
                    for j, dst in ((3, RB), (4, RA)):
                        e.dma_start(dst[:, cc, :], mod_dram[l, cc:cc + 1, j * D:(j + 1) * D].to_broadcast((P, D))
                                    ).then_inc(S["ld_rows"], 16)
                e.dma_start(nrow2, n2row[l:l + 1].to_broadcast((P, D))).then_inc(S["ld_rows"], 16)
                e.memset(slots[:], NOROW)
                e.drain()
                e.memset(xg, 0.0)
                e.dma_start(slot_dram.rearrange("(p n) a -> p (n a)", p=P), slots[:]).then_inc(S["slot_init"], 16)
                for t in range(NT):
                    e.wait_ge(S["h2_rdy"], NT * l + t + 1)
                    e.dma_start(h2_dram[t * P:(t + 1) * P, :], CAT[:, t, :]).then_inc(S["h2_st"], 16)
                e.wait_ge(S["slot_init"], 16 * (l + 1))
                e.wait_ge(S["slot_rdy"], l + 1)
                for k in range(2):
                    for t in range(NT):
                        e.indirect_dma_start(slot_dram, bass.IndirectOffsetOnAxis(sai[:, k, t:t + 1], 0),
                                             svi[:, k, t:t + 1], None, bounds_check=P * NBLK - 1, oob_is_err=False
                                             ).then_inc(S["slot_st"], 16)
                e.wait_ge(S["slot_st"], 160 * (l + 1))
                e.dma_start(slots[:], slot_dram.rearrange("(p n) a -> p (n a)", p=P)).then_inc(S["slot_ld"], 16)
                e.wait_ge(S["h2_st"], 16 * NT * (l + 1))
                e.wait_ge(S["gidx_rdy"], l + 1)
                bar()
                e.drain().then_inc(S["ov_go"], 1)
                for cc in range(2):
                    e.dma_start(RA[:, cc, :], mod_dram[l, cc:cc + 1, 5 * D:6 * D].to_broadcast((P, D))
                                ).then_inc(S["ld_rows"], 16)

                def gather(n, first):
                    if not first:
                        e.wait_ge(S["xgT_ps"], 32 * l + n - 1)
                    e.indirect_dma_start(xg[:, n % 2, :], None, h2_dram, bass.IndirectOffsetOnAxis(gidx[:, n:n + 1], 0),
                                         bounds_check=NTOK - 1, oob_is_err=False).then_inc(gfull[n % 2], 16)

                some = e.value_load(ovn[0:1, 0:1], min_val=0, max_val=NOVF)
                with e.If(some > 0):
                    with e.Fori(0, NOVF) as i:
                        n = i
                        e.tensor_copy(gcur[:], gidx[:, bass.ds(i + NE, 1)])
                        e.tensor_copy(scur[:], slots[:, bass.ds(i + NE, 1)])
                        e.drain()
                        e.indirect_dma_start(xg[:, 0, :], None, h2_dram, bass.IndirectOffsetOnAxis(gcur[:, 0:1], 0),
                                             bounds_check=NTOK - 1, oob_is_err=False).then_inc(S[f"ov_gather{l}"], 16)
                        e.wait_ge(S[f"ov_y{l}"], n + 2)
                        e.sem_inc(S[f"ov_seen{l}"], 1)
                        e.indirect_dma_start(yk_dram, bass.IndirectOffsetOnAxis(scur[:, 0:1], 0), yb[:, 0, :], None,
                                             bounds_check=2 * NTOK - 1, oob_is_err=False).then_inc(S[f"ov_scatter{l}"], 16)
                        e.wait_ge(S[f"ov_scatter{l}"], 16 * (n + 1))
                gather(0, True)
                gather(1, True)
                for n in range(NE):
                    e.wait_ge(S["y2_sb_a"], 32 * l + n + 1)
                    e.wait_ge(S["y2_sb_d"], 32 * l + n + 1)
                    e.indirect_dma_start(yk_dram, bass.IndirectOffsetOnAxis(slots[:, n:n + 1], 0), yb[:, n % 2, :], None,
                                         bounds_check=2 * NTOK - 1, oob_is_err=False).then_inc(yfree[n % 2], 16)
                    if n + 2 < NE:
                        gather(n + 2, False)
                for i in range(2):
                    e.wait_ge(yfree[i], 16 * (NE // 2) * (l + 1))
                for t in range(NT):
                    if t >= 2:
                        e.wait_ge(S["y_used"], NT * l + t - 1)
                    for k in range(2):
                        e.dma_start(yl[:, t % 2, k, :], yk_dram[k * NTOK + t * P:k * NTOK + (t + 1) * P, :]
                                    ).then_inc(S[f"y_ld{t % 2}"], 16)
                bar()
            e.dma_start(y_out, X[:]).then_inc(S["out_st"], 16)
            e.wait_ge(S["out_st"], 16)

        @block.scalar
        def _(e):
            bar = Bars(e)
            A = e.activation
            e.wait_ge(S["ld0"], 64)
            A(condT[:], condT[:], ACT.Silu).then_inc(S["silu_c"], 1)
            bar()
            for l in range(DEPTH):
                e.sem_inc(S[f"ov_y{l}"], 1)
            for l in range(DEPTH):
                for t in range(NT):
                    e.wait_ge(S["xT_ps"], NT * l + t + 1)
                    if t == 0:
                        e.wait_ge(S["m_rdy"], 2 * l + 1)
                    for k in range(4):
                        ins = A(HT[:, k, t * P:(t + 1) * P], PS[2 * (t % 2)][:, k * P:(k + 1) * P], ACT.Identity,
                                scale=modc[:, cnd(t), 1, k:k + 1], bias=modc[:, cnd(t), 0, k:k + 1])
                    ins.then_inc(S["hT_a"], 1)
                dtr = small(0, NT, 8)
                for n in range(15):
                    e.wait_ge(S["pj_ps"], 15 * l + n + 1)
                    t, b = n % NT, PS[4 + n % 2]
                    if n < 5:
                        ins = A(qkv[:, t, :], b[:], ACT.Copy)
                    elif n < 10:
                        ins = A(CAT[:, t, 256:768], b[:], ACT.Silu)
                    else:
                        ins = A(dtr[:, t, :], b[:, 0:8], ACT.Copy)
                    ins.then_inc(S["pj_sb"], 1)
                for n in range(8):
                    e.wait_ge(S["ch_ps"], 10 * l + n + 1)
                    a, b = PS[2 * (n % 2)], PS[2 * (n % 2) + 1]
                    if n < 6:
                        A(xp[:, n, 2 * XPAD + CTX:2 * XPAD + NTOK], a[:], ACT.Copy)
                        ins = A(xp[:, n, XPAD:XPAD + CTX], b[:, 0:CTX], ACT.Copy)
                    else:
                        A(sg[:, n - 6, CTX:NTOK], a[:], ACT.Sigmoid)
                        ins = A(sg[:, n - 6, 0:CTX], b[:, 0:CTX], ACT.Sigmoid)
                    ins.then_inc(S["ch_sb"], 1)
                bar()
                cv = HT[:].rearrange("p a b -> p (a b)")[:, 0:6 * XOUT].rearrange("p (a b) -> p a b", b=XOUT)
                for n in range(6):
                    e.wait_ge(S["conv_rdy"], 6 * l + n + 1)
                    A(cv[:, n, :], cv[:, n, :], ACT.Silu).then_inc(S["convs_rdy"], 1)
                for n in range(7):
                    e.wait_ge(S["xt_ps"], 7 * l + n + 1)
                    b = PS[n % 2]
                    if n < 5:
                        ins = A(xs[:, n, :], b[:], ACT.Copy)
                    elif n == 5:
                        ins = A(btok[:, 0:4, :], b[:].rearrange("p (a b) -> p a b", a=4), ACT.Copy)
                    else:
                        ins = A(btok[:, 4, :], b[:, 0:P], ACT.Copy)
                    ins.then_inc(S["xt_sb"], 1)
                for t in range(NT):
                    e.wait_ge(S["qkT_ps"], NT * l + t + 1)
                    A(qkT[:, :, t * P:(t + 1) * P], PS[2 + t % 2][:, 0:384].rearrange("p (a b) -> p a b", a=3), ACT.Copy
                      ).then_inc(S["qkT_sb"], 1)
                nm, es, sums = small(44, NT, QH), small(64, NT, QH), small(84, NT, QH)
                for t in range(NT):
                    w = P if t == 0 else P * (1 + len(near(t)))
                    e.wait_ge(S["att_m"], NT * l + t + 1)
                    for h in range(QH):
                        if t:
                            e.wait_ge(S["att_pt"], 20 * l + 4 * (t - 1) + h + 1)
                        A(Pm[:, h, 0:w], PS[h][:, 0:w], ACT.Exp, bias=nm[:, t, h:h + 1], accum_out=sums[:, t, h:h + 1]
                          ).then_inc(S["att_exp"], 1)
                    A(es[:, t, :], es[:, t, :], ACT.Exp).then_inc(S["att_es"], 1)
                    for h in (0, 2):
                        n = 4 * t + h
                        e.wait_ge(S["att_pt"], 20 * l + n + 1)
                        if n >= 2:
                            e.wait_ge(S["att_pv"], 20 * l + n - 1)
                        A(PTs[:, 0, :, :].rearrange("p a b -> p (a b)")[:, 0:w], PS[4][:, 0:w], ACT.Copy).then_inc(S["ptc_a"], 1)
                bar()
                e.wait_ge(S["cat_a"], l + 1)
                A(CAT[:, :, 768:1024], CAT[:, :, 768:1024], ACT.Silu).then_inc(S["cat_b"], 1)
                e.wait_ge(S["dt_x"], l + 1)
                A(small(220, 80), small(140, 80), ACT.Exp, scale=-1.0)
                A(small(300, 16), pr("alog"), ACT.Exp).then_inc(S["dt_e"], 1)
                e.wait_ge(S["cum_sb"], l + 1)
                A(small(700, 240), small(460, 240), ACT.Exp).then_inc(S["dec_rdy"], 1)
                ncum = small(380, 2, NT, 8)
                for c in range(NT):
                    e.wait_ge(S["gt_ps"], NT * l + c + 1)
                    if c:
                        e.wait_ge(S["w_rdy"], 20 * l + 4 * c)
                    A(gts[:, 0], PS[6][:, 0:P], ACT.Copy)
                    A(gts[:, 1], PS[7][:, 0:P], ACT.Copy).then_inc(S["gt_sb"], 1)
                    for u in range(4):
                        d, g = u // 2, u % 2
                        e.wait_ge(S["r_ps"], 20 * l + 4 * c + u + 1)
                        if c and u == 0:
                            e.wait_ge(S["y_ps"], NT * l + c)
                        for j in range(4):
                            ins = A(LW[:, u, j, :], PS[u][:, j * P:(j + 1) * P], ACT.Exp, bias=ncum[:, d, c, 4 * g + j:4 * g + j + 1])
                        ins.then_inc(S["l_rdy"], 1)
                bar()
                for t in range(NT):
                    e.wait_ge(S["ct_ps"], NT * l + t + 1)
                    A(HT[:, 0:4, t * P:(t + 1) * P], PS[2 * (t % 2)][:].rearrange("p (a b) -> p a b", a=4), ACT.Copy
                      ).then_inc(S["ct_sb_a"], 1)
                bar()
                for t in range(NT):
                    e.wait_ge(S["h2T_ps"], NT * l + t + 1)
                    A(HT[:, 0:4, t * P:(t + 1) * P], PS[2 * (t % 2)][:].rearrange("p (a b) -> p a b", a=4), ACT.Copy
                      ).then_inc(S["h2T_a"], 1)
                e.wait_ge(S["ge_x"], l + 1)
                A(small(1200, NT, NG), small(1200, NT, NG), ACT.Exp).then_inc(S["ge_y"], 1)
                e.wait_ge(S["te_x"], l + 1)
                A(small(1220, NT), small(1220, NT), ACT.Exp).then_inc(S["te_y"], 1)
                bar()
                some = e.value_load(ovn[0:1, 0:1], min_val=0, max_val=NOVF)
                with e.If(some > 0):
                    with e.Fori(0, NOVF) as i:
                        n = i
                        e.wait_ge(S[f"ov_pe{l}"], 4 * n + 2)
                        for j in range(2):
                            ins = A(xgT[:, 0, 4 * j:4 * j + 4, :], PS[j][:].rearrange("p (a b) -> p a b", a=4), ACT.Copy)
                        ins.then_inc(S[f"ov_x{l}"], 1)
                        e.wait_ge(S[f"ov_pe{l}"], 4 * n + 3)
                        A(sgate[:, 0, :], PS[2][:, 0:FF], ACT.Silu).then_inc(S[f"ov_gate{l}"], 1)
                        e.wait_ge(S[f"ov_pe{l}"], 4 * n + 5)
                        for j in range(2):
                            ins = A(yb[:, 0, 512 * j:512 * j + 512], PS[5 + j][:], ACT.Copy)
                        ins.then_inc(S[f"ov_y{l}"], 1)
                for n in range(NE):
                    m = 32 * l + n
                    e.wait_ge(S["xgT_ps"], m + 1)
                    if n >= 2:
                        e.wait_ge(S["gu_ps"], m - 1)
                    A(xgT[:, n % 2, 0:4, :], PS[0][:].rearrange("p (a b) -> p a b", a=4), ACT.Copy).then_inc(S["xgT_sb"], 1)
                    e.wait_ge(S["gu_ps"], m + 1)
                    if n >= 2:
                        e.wait_ge(S["hh_rdy"], m - 1)
                    A(sgate[:, n % 2, :], PS[2 + n % 2][:, 0:FF], ACT.Silu).then_inc(S["sgate_rdy"], 1)
                    e.wait_ge(S["y2_ps"], m + 1)
                    if n >= 2:
                        e.wait_ge(yfree[n % 2], 16 * ((NE // 2) * l + n // 2))
                    A(yb[:, n % 2, 0:512], PS[5][:], ACT.Copy).then_inc(S["y2_sb_a"], 1)
                bar()

        @block.vector
        def _(e):
            bar = Bars(e)
            dr = e.drain

            def rsqrt(v, a, y, yi, vi):
                e.tensor_scalar(yi, vi, 1, None, ALU.logical_shift_right); dr()
                e.tensor_scalar(yi, yi, -1.0, 1597463007.0, ALU.mult, ALU.add); dr()
                for _ in range(3):
                    e.tensor_tensor(a, y, y, ALU.mult); dr()
                    e.scalar_tensor_tensor(out=a, in0=a, scalar=-0.5, in1=v, op0=ALU.mult, op1=ALU.mult); dr()
                    e.scalar_tensor_tensor(out=y, in0=a, scalar=1.5, in1=y, op0=ALU.add, op1=ALU.mult); dr()

            def rs(n, scale, vo=1400):
                v, a, y = small(vo, n), small(vo + 50, n), small(vo + 100, n)
                e.tensor_scalar(v, v, scale, EPS, ALU.mult, ALU.add); dr()
                rsqrt(v, a, y, y.bitcast(I32), v.bitcast(I32))
                return y

            e.wait_ge(S["ld0"], 64)
            for n in range(DEPTH * 12):
                l, j = divmod(n, 12)
                e.wait_ge(S["mod_ps"], n + 1)
                m = mrow[:, l, j * 512:(j + 1) * 512]
                e.tensor_tensor(m, PS[n % 2][0:2, :], m, ALU.add).then_inc(S["mod_sb"], 1)
            bar()
            for l in range(DEPTH):
                for t in range(NT):
                    e.tensor_tensor_reduce(sqs, X[:, t, :], X[:, t, :], 1.0, 0.0, ALU.mult, ALU.add, small(1400 + t, 1))
                    dr()
                y = rs(NT, 1.0 / D)
                e.wait_ge(S["ld_par"], 16 * (l + 1))
                e.wait_ge(S["ld_modc"], 64 * (l + 1))
                for cc in range(2):
                    ins = e.scalar_tensor_tensor(out=modc[:, cc, 1, :], in0=modc[:, cc, 1, :], scalar=1.0, in1=pr("norm1"),
                                                 op0=ALU.add, op1=ALU.mult)
                dr()
                e.drain().then_inc(S["m_rdy"], 1)

                def evac1(t):
                    e.wait_ge(S["xT_ps"], NT * l + t + 1)
                    for k in range(4):
                        ins = e.tensor_scalar(HT[:, 4 + k, t * P:(t + 1) * P], PS[2 * (t % 2) + 1][:, k * P:(k + 1) * P],
                                              modc[:, cnd(t), 1, 4 + k:5 + k], modc[:, cnd(t), 0, 4 + k:5 + k], ALU.mult, ALU.add)
                    ins.then_inc(S["hT_d"], 1)

                for t in range(NT):
                    if t >= 2:
                        e.wait_ge(S["xT_ps"], NT * l + t - 1)
                    e.tensor_scalar(xn[:, t % 2, :], X[:, t, :], y[:, t:t + 1], None, ALU.mult).then_inc(S["xn_ready"], 1)
                    if t:
                        evac1(t - 1)
                evac1(NT - 1)
                e.wait_ge(S["ch_sb"], 8 * (l + 1))
                for j in range(2):
                    n = 8 + j
                    e.wait_ge(S["ch_ps"], 10 * l + n + 1)
                    a, b = PS[2 * (n % 2)], PS[2 * (n % 2) + 1]
                    e.tensor_tensor(gp[:, j, 2 * GPAD + CTX:2 * GPAD + NTOK], a[:], sg[:, j, CTX:NTOK], ALU.mult)
                    e.tensor_tensor(gp[:, j, GPAD:GPAD + CTX], b[:, 0:CTX], sg[:, j, 0:CTX], ALU.mult)
                bar()
                cv = HT[:].rearrange("p a b -> p (a b)")[:, 0:6 * XOUT].rearrange("p (a b) -> p a b", b=XOUT)
                cw, cb = pr("cw", 6, 5), pr("cb")
                for n in range(6):
                    e.tensor_scalar(cv[:, n, :], xp[:, n, 0:XOUT], cw[:, n, 0:1], cb[:, n:n + 1], ALU.mult, ALU.add); dr()
                    for k in range(1, 5):
                        ins = e.scalar_tensor_tensor(out=cv[:, n, :], in0=xp[:, n, k:k + XOUT], scalar=cw[:, n, k:k + 1],
                                                     in1=cv[:, n, :], op0=ALU.mult, op1=ALU.add)
                        if k < 4:
                            dr()
                    ins.then_inc(S["conv_rdy"], 1)
                qk = qkv[:, :, 0:384]
                e.tensor_tensor(t1, qk, qk, ALU.mult); dr()
                e.tensor_reduce(small(1400, 30), t1.rearrange("p t (h d) -> p (t h) d", d=HD), AX, ALU.add); dr()
                y = rs(30, 1.0 / HD)
                for t in range(NT):
                    yt = y[:, 6 * t:6 * t + 6].unsqueeze(2).to_broadcast((P, 6, HD))
                    e.tensor_tensor(t1[:, t, :].rearrange("p (h d) -> p h d", d=HD), qkv[:, t, 0:384].rearrange("p (h d) -> p h d", d=HD),
                                    yt, ALU.mult)
                dr()
                for t in range(NT):
                    for g in range(2):
                        e.scalar_tensor_tensor(out=qkv[:, t, 128 * g:128 * g + 128].rearrange("p (k d) -> p k d", k=2),
                                               in0=t1[:, t, 0:256].rearrange("p (k g d) -> p g k d", g=2, d=HD)[:, g],
                                               scalar=HD ** -0.5,
                                               in1=pr("qw").unsqueeze(1).to_broadcast((P, 2, HD)), op0=ALU.mult, op1=ALU.mult)
                    e.tensor_tensor(qkv[:, t, 256:384].rearrange("p (k d) -> p k d", k=2),
                                    t1[:, t, 256:384].rearrange("p (k d) -> p k d", k=2),
                                    pr("kw").unsqueeze(1).to_broadcast((P, 2, HD)), ALU.mult)
                dr()
                e.drain().then_inc(S["qk_rdy"], 1)
                for t in range(1, NT):
                    q6 = qkv[:, t, 0:384].rearrange("p (h d) -> p h d", d=HD)
                    e.tensor_tensor(t1[:, t, :].rearrange("p (h d) -> p h d", d=HD), q6,
                                    ropeT[:, 0, t - 1, :].unsqueeze(1).to_broadcast((P, 6, HD)), ALU.mult)
                    halves = "p (h a b f) -> p b h a f"
                    qh = qkv[:, t, 0:384].rearrange(halves, a=2, b=2, f=16)
                    th = t2[:, t - 1, :].rearrange(halves, a=2, b=2, f=16)
                    sn = ropeT[:, 1, t - 1, :].rearrange("p (a b f) -> p b a f", b=2, f=16)
                    for b in range(2):
                        e.tensor_tensor(th[:, b], qh[:, 1 - b], sn[:, b].unsqueeze(1).to_broadcast((P, 6, 2, 16)), ALU.mult)
                dr()
                e.tensor_tensor(qkv[:, 1:NT, 0:384], t1[:, 1:NT, :], t2, ALU.add).then_inc(S["qk_rdy"], 1)

                mx, nm, es, sums, den = small(40, QH), small(44, NT, QH), small(64, NT, QH), small(84, NT, QH), small(104, QH)

                def att_max(t):
                    w = P if t == 0 else P * (1 + len(near(t)))
                    for h in range(QH):
                        e.wait_ge(S["att_s"], 20 * l + 4 * t + h + 1)
                        e.tensor_reduce(mx[:, h:h + 1], PS[h][:, 0:w], AX, ALU.max)
                    dr()
                    e.tensor_tensor(mx, mx, pr("sink"), ALU.max); dr()
                    e.tensor_scalar(nm[:, t, :], mx, -1.0, None, ALU.mult); dr()
                    e.tensor_tensor(es[:, t, :], nm[:, t, :], pr("sink"), ALU.add).then_inc(S["att_m"], 1)
                    dr()

                att_max(0)
                for t in range(NT):
                    if t + 1 < NT:
                        att_max(t + 1)
                    w = P if t == 0 else P * (1 + len(near(t)))
                    for h in (1, 3):
                        n = 4 * t + h
                        e.wait_ge(S["att_pt"], 20 * l + n + 1)
                        if n >= 2:
                            e.wait_ge(S["att_pv"], 20 * l + n - 1)
                        e.tensor_copy(PTs[:, 1, :, :].rearrange("p a b -> p (a b)")[:, 0:w], PS[5][:, 0:w]).then_inc(S["ptc_d"], 1)
                    e.wait_ge(S["att_es"], NT * l + t + 1)
                    e.tensor_tensor(den, sums[:, t, :], es[:, t, :], ALU.add); dr()
                    e.reciprocal(den, den); dr()
                    e.wait_ge(S["att_pv"], 20 * l + 4 * t + 4)
                    e.tensor_tensor(CAT[:, t, 0:256].rearrange("p (h d) -> p h d", d=HD),
                                    PS[6 + t % 2][:, 0:256].rearrange("p (h d) -> p h d", d=HD),
                                    den.unsqueeze(2).to_broadcast((P, QH, HD)), ALU.mult).then_inc(S["att_o"], 1)
                    dr()
                gw, gb = pr("gw", 2, 31), pr("gb")
                for ct in range(2):
                    e.tensor_scalar(uc[:, ct, :], gp[:, ct, 0:GOUT], gw[:, ct, 0:1], gb[:, ct:ct + 1], ALU.mult, ALU.add); dr()
                    for k in range(1, 31):
                        ins = e.scalar_tensor_tensor(out=uc[:, ct, :], in0=gp[:, ct, k:k + GOUT], scalar=gw[:, ct, k:k + 1],
                                                     in1=uc[:, ct, :], op0=ALU.mult, op1=ALU.add)
                        if k < 30:
                            dr()
                    ins.then_inc(S["uconv"], 1)
                for t in range(NT):
                    e.wait_ge(S["ut_ps"], NT * l + t + 1)
                    e.tensor_copy(CAT[:, t, 768:1024], PS[6 + t % 2][:, 256:512]).then_inc(S["ut_sb"], 1)
                e.wait_ge(S["att_pt"], 20 * (l + 1))
                e.wait_ge(S["att_pv"], 20 * (l + 1))
                dr()
                lt = view(TMP, NT, 256)
                cu = CAT[:, :, 768:1024]
                mean = small(1200, NT, 4)
                for t in range(NT):
                    e.tensor_reduce(mean[:, t, :], CAT[:, t, 768:1024].rearrange("p (g d) -> p g d", d=HD), AX, ALU.add)
                dr()
                for t in range(NT):
                    c4 = CAT[:, t, 768:1024].rearrange("p (g d) -> p g d", d=HD)
                    e.scalar_tensor_tensor(out=c4, in0=mean[:, t, :].unsqueeze(2).to_broadcast((P, 4, HD)), scalar=-1.0 / HD, in1=c4,
                                           op0=ALU.mult, op1=ALU.add)
                dr()
                e.tensor_tensor(lt, cu, cu, ALU.mult); dr()
                e.tensor_reduce(small(1400, 20), lt.rearrange("p t (g d) -> p (t g) d", d=HD), AX, ALU.add); dr()
                y = rs(20, 1.0 / HD)
                for t in range(NT):
                    c4 = CAT[:, t, 768:1024].rearrange("p (g d) -> p g d", d=HD)
                    e.tensor_tensor(c4, c4, y[:, 4 * t:4 * t + 4].unsqueeze(2).to_broadcast((P, 4, HD)), ALU.mult)
                dr()
                e.tensor_tensor(cu, cu, pr("lnw").unsqueeze(1).to_broadcast((P, NT, 256)), ALU.mult); dr()
                e.tensor_tensor(cu, cu, pr("lnb").unsqueeze(1).to_broadcast((P, NT, 256)), ALU.add).then_inc(S["cat_a"], 1)
                bar()
                xdir, ax, ee = small(1240, 80), small(140, 80), small(220, 80)
                x4 = small(1240, 2, NT, 8)
                dtr = small(0, NT, 8)
                for d in range(2):
                    e.tensor_tensor(x4[:, d], dtr, pr("dtb")[:, 8 * d:8 * d + 8].unsqueeze(1).to_broadcast((P, NT, 8)), ALU.add)
                dr()
                e.tensor_scalar(ax, xdir, -1.0, None, ALU.mult); dr()
                e.tensor_tensor(ax, ax, xdir, ALU.max).then_inc(S["dt_x"], 1)
                e.tensor_scalar(xdir, xdir, 0.0, None, ALU.max)
                e.wait_ge(S["dt_e"], l + 1)
                dr()
                s_, z_, p_ = small(940, 80), small(1020, 80), small(1100, 80)
                e.tensor_scalar(s_, ee, 2.0, None, ALU.add); dr()
                e.reciprocal(s_, s_); dr()
                e.tensor_tensor(s_, s_, ee, ALU.mult); dr()
                e.tensor_tensor(z_, s_, s_, ALU.mult); dr()
                e.tensor_scalar(p_, z_, 1.0 / 17, None, ALU.mult); dr()
                for k in (15, 13, 11, 9, 7, 5, 3):
                    e.scalar_tensor_tensor(out=p_, in0=p_, scalar=1.0 / k, in1=z_, op0=ALU.add, op1=ALU.mult); dr()
                e.scalar_tensor_tensor(out=p_, in0=p_, scalar=1.0, in1=s_, op0=ALU.add, op1=ALU.mult); dr()
                dt, la = small(1320, 80), small(1020, 80)
                e.scalar_tensor_tensor(out=dt, in0=p_, scalar=2.0, in1=xdir, op0=ALU.mult, op1=ALU.add); dr()
                dt4, la4 = small(1320, 2, NT, 8), small(1020, 2, NT, 8)
                for d in range(2):
                    ins = e.scalar_tensor_tensor(out=la4[:, d], in0=dt4[:, d], scalar=-1.0,
                                                 in1=small(300, 2, 8)[:, d].unsqueeze(1).to_broadcast((P, NT, 8)),
                                                 op0=ALU.mult, op1=ALU.mult)
                ins.then_inc(S["la_rdy"], 1)
                e.wait_ge(S["cum_ps"], l + 1)
                e.tensor_copy(small(460, 160), PS[7][:, 0:160]); dr()
                e.tensor_scalar(small(380, 80), small(460, 80), -1.0, None, ALU.mult)
                e.tensor_tensor(small(620, 80), small(540, 80), small(460, 80), ALU.subtract).then_inc(S["cum_sb"], 1)
                e.wait_ge(S["dec_rdy"], l + 1)
                dec, cd, dte = small(700, 2, NT, 8), small(780, 2, NT, 8), small(860, 2, NT, 8)
                dsum = small(320, 8)
                e.tensor_tensor(dsum, pr("dskip")[:, 0:8], pr("dskip")[:, 8:16], ALU.add)
                e.tensor_copy(hs[:, 0, 0, :], pr("h0")[:, 0:256])
                e.tensor_copy(hs[:, 1, NLT - 1, :], pr("h0")[:, 256:512])
                dr()

                def h3(a, n=8):
                    return a.rearrange("p (h d) -> p h d", d=HD)

                def decayed(out, src, d, c):
                    for g in range(2):
                        r = slice(64 * g, 64 * g + 64)
                        e.tensor_tensor(h3(out[r]), h3(src[r]),
                                        cd[r, d, c, 4 * g:4 * g + 4].unsqueeze(2).to_broadcast((64, 4, HD)), ALU.mult)

                for c in range(NT):
                    if c:
                        e.wait_ge(S["s_ps"], NT * l + c)
                    for d in range(2):
                        e.tensor_tensor(h3(xdt[:, d, :]), h3(xs[:, c, :]), dt4[:, d, c, :].unsqueeze(2).to_broadcast((P, 8, HD)), ALU.mult)
                    dr()
                    for d in range(2):
                        ins = e.tensor_tensor(h3(xw[:, d, :]), h3(xdt[:, d, :]), dte[:, d, c, :].unsqueeze(2).to_broadcast((P, 8, HD)), ALU.mult)
                    ins.then_inc(S["xd_rdy"], 1)
                    e.tensor_tensor(h3(xs[:, c, :]), h3(xs[:, c, :]), dsum.unsqueeze(2).to_broadcast((P, 8, HD)), ALU.mult)
                    e.wait_ge(S["gt_sb"], NT * l + c + 1)
                    for u in range(4):
                        e.wait_ge(S["l_rdy"], 20 * l + 4 * c + u + 1)
                        e.tensor_tensor(LW[:, u], LW[:, u], gts[:, u % 2].unsqueeze(1).to_broadcast((P, 4, P)), ALU.mult
                                        ).then_inc(S["w_rdy"], 1)
                    e.wait_ge(S["s_ps"], NT * l + c + 1)
                    sp = PS[5]
                    if c == 0:
                        e.tensor_copy(stc.rearrange("p a b -> p (a b)"), sp[:]).then_inc(S["st_rdy"], 1)
                    else:
                        i = c - 1
                        if i < NLT - 1:
                            decayed(hsc, hs[:, 0, i, :], 0, c); dr()
                            e.tensor_tensor(hs[:, 0, i + 1, :], sp[:, 0:256], hsc, ALU.add)
                        if i:
                            e.tensor_copy(hs[:, 1, i - 1, :], sp[:, 256:512])
                    dr()
                    e.tensor_tensor(xs[:, c, :], PS[4][:], xs[:, c, :], ALU.add).then_inc(S["y_sb"], 1)
                for i in range(NLT - 1, 0, -1):
                    decayed(hsc, hs[:, 1, i, :], 1, i + 1); dr()
                    e.tensor_tensor(hs[:, 1, i - 1, :], hs[:, 1, i - 1, :], hsc, ALU.add); dr()
                e.drain().then_inc(S["hs_rdy"], 1)
                for i in range(NLT):
                    c = i + 1
                    e.wait_ge(S["off_ps"], NLT * l + i + 1)
                    for d, dst in ((0, off1), (1, off2)):
                        for g in range(2):
                            ins = e.tensor_tensor(h3(dst[:, 256 * g:256 * g + 256]), h3(PS[2 * (i % 2) + g][:, 256 * d:256 * d + 256]),
                                                  dec[:, d, c, 4 * g:4 * g + 4].unsqueeze(2).to_broadcast((P, 4, HD)), ALU.mult)
                    ins.then_inc(S["off_sb"], 1)
                    dr()
                    e.tensor_tensor(xs[:, c, :], xs[:, c, :], off1, ALU.add); dr()
                    e.tensor_tensor(xs[:, c, :], xs[:, c, :], off2, ALU.add); dr()
                cz = CAT[:, :, 256:768]
                e.wait_ge(S["st_st"], 16 * (l + 1))
                e.tensor_tensor(xs, xs, cz, ALU.mult); dr()
                e.tensor_tensor(big, xs, xs, ALU.mult); dr()
                e.tensor_reduce(small(1400, 10), big.rearrange("p t (g d) -> p (t g) d", d=256), AX, ALU.add); dr()
                y = rs(10, 1.0 / 256)
                for t in range(NT):
                    for g in range(2):
                        e.scalar_tensor_tensor(out=CAT[:, t, 256 + 256 * g:512 + 256 * g], in0=xs[:, t, 256 * g:256 * g + 256],
                                               scalar=y[:, 2 * t + g:2 * t + g + 1], in1=pr("snorm")[:, 256 * g:256 * g + 256],
                                               op0=ALU.mult, op1=ALU.mult)
                bar()
                for t in range(NT):
                    e.wait_ge(S["ct_ps"], NT * l + t + 1)
                    e.tensor_copy(HT[:, 4:8, t * P:(t + 1) * P], PS[2 * (t % 2) + 1][:].rearrange("p (a b) -> p a b", a=4)
                                  ).then_inc(S["ct_sb_d"], 1)
                e.wait_ge(S["ld_rows"], 16 * (9 * l + 2))
                for n in range(2 * NT):
                    t, hf = n % NT, n // NT
                    e.wait_ge(S["wo_ps"], 10 * l + n + 1)
                    e.tensor_tensor(wtmp[:, n % 2, :], PS[4 + n % 2][:], RA[:, cnd(t), 512 * hf:512 * hf + 512], ALU.mult
                                    ).then_inc(S["wo_sb"], 1)
                    dr()
                    e.tensor_tensor(X[:, t, 512 * hf:512 * hf + 512], X[:, t, 512 * hf:512 * hf + 512], wtmp[:, n % 2, :], ALU.add)
                bar()
                for t in range(NT):
                    e.tensor_tensor_reduce(mt[:, 0, :], X[:, t, :], X[:, t, :], 1.0, 0.0, ALU.mult, ALU.add, small(1400 + t, 1))
                    dr()
                y = rs(NT, 1.0 / D)
                e.wait_ge(S["ld_rows"], 16 * (9 * l + 7))
                for cc in range(2):
                    e.scalar_tensor_tensor(out=RA[:, cc, :], in0=RA[:, cc, :], scalar=1.0, in1=nrow2, op0=ALU.add, op1=ALU.mult)
                dr()
                e.drain().then_inc(S["m_rdy"], 1)

                def evac2(t):
                    e.wait_ge(S["h2T_ps"], NT * l + t + 1)
                    e.tensor_copy(HT[:, 4:8, t * P:(t + 1) * P], PS[2 * (t % 2) + 1][:].rearrange("p (a b) -> p a b", a=4)
                                  ).then_inc(S["h2T_d"], 1)

                for t in range(NT):
                    e.scalar_tensor_tensor(out=mt[:, t % 2, :], in0=X[:, t, :], scalar=y[:, t:t + 1], in1=RA[:, cnd(t), :],
                                           op0=ALU.mult, op1=ALU.mult); dr()
                    e.tensor_tensor(CAT[:, t, :], mt[:, t % 2, :], RB[:, cnd(t), :], ALU.add).then_inc(S["h2_rdy"], 1)
                    if t:
                        evac2(t - 1)
                evac2(NT - 1)
                lg = small(0, NT, 36)
                for t in range(NT):
                    e.wait_ge(S["lg_ps"], NT * l + t + 1)
                    e.tensor_tensor(lg[:, t, :], PS[4 + t % 2][:, 0:36], pr("rb"), ALU.add).then_inc(S["lg_sb"], 1)
                dr()
                gl, el = lg[:, :, 0:NG], lg[:, :, NG:36]

                def first_max(src, n, m, i, oh, tmp):
                    io = iota[:, 0:n].unsqueeze(1).to_broadcast((P, NT, n))
                    e.tensor_reduce(m, src, AX, ALU.max); dr()
                    e.tensor_tensor(tmp, src, m.unsqueeze(2).to_broadcast((P, NT, n)), ALU.is_equal); dr()
                    e.scalar_tensor_tensor(out=tmp, in0=tmp, scalar=-64.0, in1=io, op0=ALU.mult, op1=ALU.add); dr()
                    e.tensor_reduce(i, tmp, AX, ALU.min); dr()
                    e.tensor_scalar(i, i, 64.0, None, ALU.add); dr()
                    e.tensor_tensor(oh, i.unsqueeze(2).to_broadcast((P, NT, n)), io, ALU.is_equal); dr()

                gm, gi, m1, i1, m2, i2 = (small(180 + 5 * j, NT) for j in range(6))
                goh, gt = small(210, NT, NG), small(230, NT, NG)
                o1, o2, tm, es8 = (small(250 + 40 * j, NT, EPG) for j in range(4))
                first_max(gl, NG, gm, gi, goh, gt)
                gx = small(1200, NT, NG)
                e.tensor_tensor(gx, gl, gm.unsqueeze(2).to_broadcast((P, NT, NG)), ALU.subtract).then_inc(S["ge_x"], 1)
                tm32 = small(420, NT, NG, EPG)
                for t in range(NT):
                    e.tensor_tensor(tm32[:, t], el[:, t, :].rearrange("p (g x) -> p g x", g=NG),
                                    goh[:, t, :].unsqueeze(2).to_broadcast((P, NG, EPG)), ALU.mult)
                dr()
                for t in range(NT):
                    e.tensor_reduce(es8[:, t, :], tm32[:, t].rearrange("p g x -> p x g"), AX, ALU.add)
                dr()
                first_max(es8, EPG, m1, i1, o1, tm)
                e.scalar_tensor_tensor(out=es8, in0=o1, scalar=-BIG, in1=es8, op0=ALU.mult, op1=ALU.add); dr()
                first_max(es8, EPG, m2, i2, o2, tm)
                dx = small(1220, NT)
                e.tensor_tensor(dx, m2, m1, ALU.subtract).then_inc(S["te_x"], 1)
                M1, M2, MM = small(580, NT, NE), small(740, NT, NE), small(900, NT, NE)
                for t in range(NT):
                    for Mk, ok in ((M1, o1), (M2, o2)):
                        e.tensor_tensor(Mk[:, t, :].rearrange("p (g x) -> p g x", g=NG),
                                        goh[:, t, :].unsqueeze(2).to_broadcast((P, NG, EPG)),
                                        ok[:, t, :].unsqueeze(1).to_broadcast((P, NG, EPG)), ALU.mult)
                dr()
                e.tensor_tensor(MM, M1, M2, ALU.add).then_inc(S["lg_sb"], 1)
                e.wait_ge(S["ge_y"], l + 1)
                pg, wd = small(1225, NT), small(1230, NT)
                W1, W2 = small(1235, NT), small(1240, NT)
                e.tensor_reduce(pg, gx, AX, ALU.add); dr()
                e.wait_ge(S["te_y"], l + 1)
                e.scalar_tensor_tensor(out=wd, in0=dx, scalar=1.0, in1=pg, op0=ALU.add, op1=ALU.mult); dr()
                e.reciprocal(W1, wd); dr()
                e.tensor_tensor(W2, W1, dx, ALU.mult)
                e.wait_ge(S["rank_ps"], l + 1)
                rk, cnt = small(420, NT, NE), small(1245, NE)
                e.tensor_copy(rk, PS[6][:, 0:NT * NE].rearrange("p (t n) -> p t n", t=NT))
                e.tensor_copy(cnt, PS[6][:, NT * NE:NT * NE + NE]); dr()
                nov, cs, cs2 = small(1280, NE), small(1320, 16 + NE), small(1370, 16 + NE)
                e.tensor_scalar(nov, cnt, float(P), None, ALU.is_gt); dr()
                for j in range(2, 5):
                    e.scalar_tensor_tensor(out=nov, in0=cnt, scalar=float(P * j), in1=nov, op0=ALU.is_gt, op1=ALU.add); dr()
                e.memset(cs[:, 0:16], 0.0)
                e.memset(cs2[:, 0:16], 0.0)
                e.tensor_copy(cs[:, 16:16 + NE], nov); dr()
                a_, b_ = cs, cs2
                for j in (1, 2, 4, 8, 16):
                    e.tensor_tensor(b_[:, 16:16 + NE], a_[:, 16:16 + NE], a_[:, 16 - j:16 - j + NE], ALU.add); dr()
                    a_, b_ = b_, a_
                ovs = small(1630, NE)
                e.tensor_tensor(ovs, a_[:, 16:16 + NE], nov, ALU.subtract); dr()
                ovf, cmp = small(1662, 1 + NOVF), small(1060, 4, NE)
                for i in range(NOVF):
                    e.tensor_scalar(cmp[:, i % 4, :], a_[:, 16:16 + NE], float(i), None, ALU.is_le); dr()
                    e.tensor_reduce(ovf[:, 1 + i:2 + i], cmp[:, i % 4, :], AX, ALU.add); dr()
                e.tensor_copy(ovf[:, 0:1], a_[:, 16 + NE - 1:16 + NE])
                e.tensor_scalar(ovf[:, 1:], ovf[:, 1:], float(NE - 1), None, ALU.min); dr()
                e.tensor_scalar(ovf[:, 1:], ovf[:, 1:], 3.0, float(base(l) + INN + OUTN), ALU.mult, ALU.add); dr()
                e.tensor_copy(ovn[:], ovf)
                for k, Mk in ((0, M1), (1, M2)):
                    tt = small(0, NT, NE)
                    rk_, ek, ok_, mk, sl = (small(160 + 5 * j, NT) for j in range(5))
                    for dst, src in ((rk_, rk), (ek, iota[:].unsqueeze(1).to_broadcast((P, NT, NE))),
                                     (ok_, ovs.unsqueeze(1).to_broadcast((P, NT, NE)))):
                        e.tensor_tensor(tt, Mk, src, ALU.mult); dr()
                        e.tensor_reduce(dst, tt, AX, ALU.add); dr()
                    e.tensor_scalar(mk, rk_, float(P), None, ALU.is_ge); dr()
                    for j in range(2, 5):
                        e.scalar_tensor_tensor(out=mk, in0=rk_, scalar=float(P * j), in1=mk, op0=ALU.is_ge, op1=ALU.add); dr()
                    e.tensor_scalar(sl, mk, 0.0, None, ALU.is_gt)
                    e.tensor_tensor(ok_, ok_, ek, ALU.subtract); dr()
                    e.scalar_tensor_tensor(out=ok_, in0=ok_, scalar=float(NE - 1), in1=mk, op0=ALU.add, op1=ALU.add); dr()
                    e.tensor_tensor(ok_, ok_, sl, ALU.mult); dr()
                    e.tensor_tensor(ek, ek, ok_, ALU.add)
                    e.scalar_tensor_tensor(out=rk_, in0=mk, scalar=float(-P), in1=rk_, op0=ALU.mult, op1=ALU.add); dr()
                    e.scalar_tensor_tensor(out=rk_, in0=rk_, scalar=float(NBLK), in1=ek, op0=ALU.mult, op1=ALU.add); dr()
                    e.tensor_copy(sai[:, k, :], rk_); dr()
                e.drain().then_inc(S["slot_rdy"], 1)
                e.wait_ge(S["slot_ld"], 16 * (l + 1))
                sf, sf2 = small(0, NBLK), small(50, NBLK)
                e.tensor_copy(sf, slots[:]); dr()
                e.tensor_scalar(sf2, sf, float(NTOK), float(-NTOK), ALU.is_ge, ALU.mult); dr()
                e.tensor_tensor(sf, sf, sf2, ALU.add); dr()
                e.tensor_copy(gidx[:], sf).then_inc(S["gidx_rdy"], 1)
                bar()
                some = e.value_load(ovn[0:1, 0:1], min_val=0, max_val=NOVF)
                with e.If(some > 0):
                    with e.Fori(0, NOVF) as i:
                        n = i
                        e.wait_ge(S[f"ov_gate{l}"], n + 1)
                        e.tensor_tensor(hh[:, 0, :], PS[2][:, FF:2 * FF], sgate[:, 0, :], ALU.mult).then_inc(S[f"ov_h{l}"], 1)
                        e.wait_ge(S[f"ov_pe{l}"], 4 * n + 4)
                        e.tensor_copy(hhT[:, 0], PS[4][:, 0:256].rearrange("p (a b) -> p a b", a=2)).then_inc(S[f"ov_hT{l}"], 1)
                for n in range(NE):
                    m = 32 * l + n
                    e.wait_ge(S["xgT_ps"], m + 1)
                    if n >= 2:
                        e.wait_ge(S["gu_ps"], m - 1)
                    e.tensor_copy(xgT[:, n % 2, 4:8, :], PS[1][:].rearrange("p (a b) -> p a b", a=4)).then_inc(S["xgT_sb"], 1)
                    e.wait_ge(S["sgate_rdy"], m + 1)
                    if n >= 2:
                        e.wait_ge(S["hhT_ps"], m - 1)
                    e.tensor_tensor(hh[:, n % 2, :], PS[2 + n % 2][:, FF:2 * FF], sgate[:, n % 2, :], ALU.mult).then_inc(S["hh_rdy"], 1)
                    e.wait_ge(S["hhT_ps"], m + 1)
                    if n >= 2:
                        e.wait_ge(S["y2_ps"], m - 1)
                    e.tensor_copy(hhT[:, n % 2], PS[4][:, 0:256].rearrange("p (a b) -> p a b", a=2)).then_inc(S["hhT_sb"], 1)
                    e.wait_ge(S["y2_ps"], m + 1)
                    if n >= 2:
                        e.wait_ge(yfree[n % 2], 16 * ((NE // 2) * l + n // 2))
                    e.tensor_copy(yb[:, n % 2, 512:1024], PS[6][:]).then_inc(S["y2_sb_d"], 1)
                e.wait_ge(S["ld_rows"], 16 * 9 * (l + 1))
                for t in range(NT):
                    uses = (3 * l + t // 2 + 1) if t % 2 == 0 else (2 * l + t // 2 + 1)
                    e.wait_ge(S[f"y_ld{t % 2}"], 32 * uses)
                    e.tensor_scalar(mt[:, t % 2, :], yl[:, t % 2, 0, :], W1[:, t:t + 1], None, ALU.mult); dr()
                    e.scalar_tensor_tensor(out=mt[:, t % 2, :], in0=yl[:, t % 2, 1, :], scalar=W2[:, t:t + 1], in1=mt[:, t % 2, :],
                                           op0=ALU.mult, op1=ALU.add).then_inc(S["y_used"], 1)
                    dr()
                    e.tensor_tensor(mt[:, t % 2, :], mt[:, t % 2, :], RA[:, cnd(t), :], ALU.mult); dr()
                    e.tensor_tensor(X[:, t, :], X[:, t, :], mt[:, t % 2, :], ALU.add); dr()
                bar()

        @block.tensor
        def _(e):
            bar = Bars(e)

            def arrived(q):
                e.wait_ge(full[q % RING], 16 * (q // RING + 1))

            def wt(q):
                return ring[:, q % RING, :].rearrange("p (k n) -> p k n", k=KD)

            e.wait_ge(S["silu_c"], 1)
            for n in range(DEPTH * 12):
                if n >= 2:
                    e.wait_ge(S["mod_sb"], n - 1)
                for h in range(2):
                    q = 2 * n + h
                    arrived(q)
                    for k in range(KD):
                        ins = e.matmul(PS[n % 2][0:2, 256 * h:256 * h + 256], condT[:, k, :], wt(q)[:, k, :], start=(k == 0), stop=(k == KD - 1))
                        if k == KD - 1:
                            ins.then_inc(free[q % RING], 1)
                e.drain().then_inc(S["mod_ps"], 1)
            e.wait_ge(S["cst"], 15)
            bar()
            for l in range(DEPTH):
                e.sem_inc(S[f"ov_pe{l}"], 1)
            for l in range(DEPTH):
                b = base(l)
                for t in range(NT):
                    e.wait_ge(S["xn_ready"], NT * l + t + 1)
                    if t >= 2:
                        e.wait_ge(S["hT_a"], NT * l + t - 1)
                        e.wait_ge(S["hT_d"], NT * l + t - 1)
                    for k in range(KD):
                        ins = e.transpose(PS[2 * (t % 2) + k // 4][:, (k % 4) * P:(k % 4 + 1) * P], xn[:, t % 2, k * P:(k + 1) * P], ident[:])
                    ins.then_inc(S["xT_ps"], 1)
                e.wait_ge(S["hT_a"], NT * (l + 1))
                e.wait_ge(S["hT_d"], NT * (l + 1))
                e.wait_ge(S["ld_par"], 16 * (l + 1))
                wdt = pr("wdt", KD, 8)
                for n in range(15):
                    t, bank = n % NT, PS[4 + n % 2]
                    if n >= 2:
                        e.wait_ge(S["pj_sb"], 15 * l + n - 1)
                    if n < 10:
                        q = b + 2 * (n // NT)
                        arrived(q)
                        arrived(q + 1)
                        for h in range(2):
                            for k in range(KD):
                                ins = e.matmul(bank[:, 256 * h:256 * h + 256], HT[:, k, t * P:(t + 1) * P], wt(q + h)[:, k, :],
                                               start=(k == 0), stop=(k == KD - 1))
                            if t == NT - 1:
                                e.drain().then_inc(free[(q + h) % RING], 1)
                        e.drain().then_inc(S["pj_ps"], 1)
                    else:
                        for k in range(KD):
                            ins = e.matmul(bank[:, 0:8], HT[:, k, t * P:(t + 1) * P], wdt[:, k, :], start=(k == 0), stop=(k == KD - 1))
                        ins.then_inc(S["pj_ps"], 1)
                for n in range(10):
                    q = b + 4 + n // 2
                    arrived(q)
                    if n >= 2:
                        e.wait_ge(S["ch_sb"], 8 * l + n - 1)
                    elif l:
                        pass
                    lat, cx = PS[2 * (n % 2)], PS[2 * (n % 2) + 1]
                    for out, lo, w in ((lat[:], CTX, LAT), (cx[:, 0:CTX], 0, CTX)):
                        for k in range(KD):
                            ins = e.matmul(out, wt(q)[:, k, P * (n % 2):P * (n % 2) + P], HT[:, k, lo:lo + w], start=(k == 0), stop=(k == KD - 1))
                    ins.then_inc(S["ch_ps"], 1)
                    if n % 2:
                        e.drain().then_inc(free[q % RING], 1)
                bar()
                cv = HT[:].rearrange("p a b -> p (a b)")[:, 0:6 * XOUT].rearrange("p (a b) -> p a b", b=XOUT)

                def at(n, t):
                    s = t * P + (0 if t == 0 else XPAD)
                    return cv[:, n, s:s + P]

                e.wait_ge(S["convs_rdy"], 6 * (l + 1))
                for n in range(7):
                    if n >= 2:
                        e.wait_ge(S["xt_sb"], 7 * l + n - 1)
                    src = [(j, n) for j in range(4)] if n < 5 else [(4, t) for t in (range(4) if n == 5 else (4,))]
                    for i, (j, t) in enumerate(src):
                        ins = e.transpose(PS[n % 2][:, i * P:(i + 1) * P], at(j, t), ident[:])
                    ins.then_inc(S["xt_ps"], 1)
                e.wait_ge(S["qk_rdy"], 2 * (l + 1))
                for t in range(NT):
                    if t >= 2:
                        e.wait_ge(S["qkT_sb"], NT * l + t - 1)
                    for j in range(3):
                        ins = e.transpose(PS[2 + t % 2][:, j * P:(j + 1) * P], qkv[:, t, j * P:(j + 1) * P], ident[:])
                    ins.then_inc(S["qkT_ps"], 1)
                e.wait_ge(S["xt_sb"], 7 * (l + 1))
                e.wait_ge(S["qkT_sb"], NT * (l + 1))

                def att_scores(t):
                    for h in range(QH):
                        if t:
                            e.wait_ge(S["att_exp"], 20 * l + 4 * (t - 1) + h + 1)
                        kv, g = h // 2, h % 2
                        r = slice(64 * kv, 64 * kv + 64)
                        q = qkT[r, g, t * P:(t + 1) * P]
                        if t == 0:
                            ins = e.matmul(PS[h][:, 0:P], q, qkT[r, 2, 0:P], start=True, stop=True)
                        else:
                            nb = near(t)
                            w = P * len(nb)
                            e.matmul(PS[h][:, 0:P], q, pr("kctx")[r, :], start=True, stop=False, skip_group_check=True)
                            ins = e.matmul(PS[h][:, P:P + w], q, qkT[r, 2, nb[0] * P:nb[0] * P + w], start=False, stop=True, skip_group_check=True)
                            for i, j in enumerate(nb):
                                if j != t:
                                    ins = e.matmul(PS[h][:, P + i * P:P + i * P + P], ident[:], (negF if j < t else negB)[:],
                                                   start=False, stop=True, skip_group_check=True)
                        ins.then_inc(S["att_s"], 1)

                att_scores(0)
                for t in range(NT):
                    if t + 1 < NT:
                        att_scores(t + 1)
                    nb = [0] if t == 0 else [-1] + near(t)

                    def pv(h):
                        n = 4 * t + h
                        kv = h // 2
                        if h % 2 == 0:
                            e.wait_ge(S["ptc_a"], 10 * l + n // 2 + 1)
                        else:
                            e.wait_ge(S["ptc_d"], 10 * l + n // 2 + 1)
                        if t >= 2 and h == 0:
                            e.wait_ge(S["att_o"], NT * l + t - 1)
                        for i, j in enumerate(nb):
                            v = pr("vctx")[:, 64 * kv:64 * kv + 64] if j < 0 else qkv[:, j, 384 + 64 * kv:448 + 64 * kv]
                            ins = e.matmul(PS[6 + t % 2][:, 64 * h:64 * h + 64], PTs[:, h % 2, i, :], v, start=(i == 0), stop=(i == len(nb) - 1))
                        ins.then_inc(S["att_pv"], 1)

                    for h in range(QH):
                        n = 4 * t + h
                        e.wait_ge(S["att_exp"], 20 * l + n + 1)
                        if n >= 2:
                            if h % 2 == 0:
                                e.wait_ge(S["ptc_a"], 10 * l + n // 2)
                            else:
                                e.wait_ge(S["ptc_d"], 10 * l + n // 2)
                        for i in range(len(nb)):
                            ins = e.transpose(PS[4 + h % 2][:, i * P:(i + 1) * P], Pm[:, h, i * P:(i + 1) * P], ident[:])
                        ins.then_inc(S["att_pt"], 1)
                        if h:
                            pv(h - 1)
                    pv(3)
                e.wait_ge(S["uconv"], 2 * (l + 1))
                e.wait_ge(S["att_o"], NT * (l + 1))
                for t in range(NT):
                    if t >= 2:
                        e.wait_ge(S["ut_sb"], NT * l + t - 1)
                    s = t * P + (0 if t == 0 else GPAD)
                    for j in range(2):
                        ins = e.transpose(PS[6 + t % 2][:, 256 + j * P:256 + (j + 1) * P], uc[:, j, s:s + P], ident[:])
                    ins.then_inc(S["ut_ps"], 1)
                bar()
                la4 = small(1020, 2, NT, 8)
                e.wait_ge(S["la_rdy"], l + 1)
                e.matmul(PS[7][:, 0:40], triF[:], small(1020, 40), start=True, stop=True)
                e.matmul(PS[7][:, 40:80], triB[:], small(1060, 40), start=True, stop=True)
                e.matmul(PS[7][:, 80:160], ones[:], small(1020, 80), start=True, stop=True).then_inc(S["cum_ps"], 1)

                def ssd_pre(c):
                    if c:
                        e.wait_ge(S["gt_sb"], NT * l + c)
                    for g in range(2):
                        r = slice(64 * g, 64 * g + 64)
                        ins = e.matmul(PS[6 + g][:, 0:P], at(4, c)[r], at(5, c)[r], start=True, stop=True)
                    ins.then_inc(S["gt_ps"], 1)
                    for u in range(4):
                        d, g = u // 2, u % 2
                        if c:
                            e.wait_ge(S["l_rdy"], 20 * l + 4 * (c - 1) + u + 1)
                        e.matmul(PS[u][:], ident[:], (negB if d else negF)[:].unsqueeze(1).to_broadcast((P, 4, P)),
                                 start=True, stop=False, skip_group_check=True)
                        for j in range(4):
                            ins = e.matmul(PS[u][:, j * P:(j + 1) * P], la4[:, d, c, 4 * g + j:4 * g + j + 1].to_broadcast((P, P)),
                                           (triB if d else triF)[:], start=False, stop=True, skip_group_check=True)
                        ins.then_inc(S["r_ps"], 1)

                e.wait_ge(S["cum_sb"], l + 1)
                ssd_pre(0)
                for c in range(NT):
                    if c + 1 < NT:
                        ssd_pre(c + 1)
                    e.wait_ge(S["xd_rdy"], NT * l + c + 1)
                    if c:
                        e.wait_ge(S["y_sb"], NT * l + c)
                    for d in range(2):
                        for g in range(2):
                            ins = e.matmul(PS[5][64 * g:64 * g + 64, 256 * d:256 * d + 256], btok[:, c, 64 * g:64 * g + 64],
                                           xw[:, d, 256 * g:256 * g + 256], start=True, stop=True)
                    e.wait_ge(S["w_rdy"], 20 * l + 4 * c + 4)
                    for h in range(NH):
                        for d in range(2):
                            ins = e.matmul(PS[4][:, 64 * h:64 * h + 64], LW[:, 2 * d + h // 4, h % 4, :], xdt[:, d, 64 * h:64 * h + 64],
                                           start=(d == 0), stop=(d == 1))
                    e.drain().then_inc(S["y_ps"], 1)
                    e.drain().then_inc(S["s_ps"], 1)
                e.wait_ge(S["hs_rdy"], l + 1)
                for i in range(NLT):
                    if i >= 2:
                        e.wait_ge(S["off_sb"], NLT * l + i - 1)
                    for d in range(2):
                        for g in range(2):
                            r = slice(64 * g, 64 * g + 64)
                            ins = e.matmul(PS[2 * (i % 2) + g][:, 256 * d:256 * d + 256], at(5, i + 1)[r], hs[r, d, i, :], start=True, stop=True)
                    ins.then_inc(S["off_ps"], 1)
                bar()
                e.wait_ge(S["cat_b"], l + 1)

                def to_channels(signal, a, d_, src):
                    for t in range(NT):
                        if t >= 2:
                            e.wait_ge(S[a], NT * l + t - 1)
                            e.wait_ge(S[d_], NT * l + t - 1)
                        if src == "h2":
                            e.wait_ge(S["h2_rdy"], NT * l + t + 1)
                        for k in range(KD):
                            ins = e.transpose(PS[2 * (t % 2) + k // 4][:, (k % 4) * P:(k % 4 + 1) * P], CAT[:, t, k * P:(k + 1) * P], ident[:])
                        ins.then_inc(S[signal], 1)
                    e.wait_ge(S[a], NT * (l + 1))
                    e.wait_ge(S[d_], NT * (l + 1))

                to_channels("ct_ps", "ct_sb_a", "ct_sb_d", "cat")
                for n in range(2 * NT):
                    t, hf = n % NT, n // NT
                    q = b + INN + 2 * hf
                    arrived(q)
                    arrived(q + 1)
                    if n >= 2:
                        e.wait_ge(S["wo_sb"], 10 * l + n - 1)
                    for j in range(2):
                        for k in range(KD):
                            ins = e.matmul(PS[4 + n % 2][:, 256 * j:256 * j + 256], HT[:, k, t * P:(t + 1) * P], wt(q + j)[:, k, :],
                                           start=(k == 0), stop=(k == KD - 1))
                    ins.then_inc(S["wo_ps"], 1)
                    if t == NT - 1:
                        for j in range(2):
                            e.drain().then_inc(free[(q + j) % RING], 1)
                bar()
                to_channels("h2T_ps", "h2T_a", "h2T_d", "h2")
                rw = pr("rw", KD, 36)
                for t in range(NT):
                    if t >= 2:
                        e.wait_ge(S["lg_sb"], 6 * l + t - 1)
                    for k in range(KD):
                        ins = e.matmul(PS[4 + t % 2][:, 0:36], HT[:, k, t * P:(t + 1) * P], rw[:, k, :], start=(k == 0), stop=(k == KD - 1))
                    ins.then_inc(S["lg_ps"], 1)
                MM = small(900, NT, NE)
                e.wait_ge(S["lg_sb"], 6 * (l + 1))
                for t in range(NT):
                    for j in range(t + 1):
                        e.matmul(PS[6][:, NE * t:NE * t + NE], (triS if j == t else ones)[:], MM[:, j, :], start=(j == 0), stop=(j == t))
                for j in range(NT):
                    ins = e.matmul(PS[6][:, NE * NT:NE * NT + NE], ones[:], MM[:, j, :], start=(j == 0), stop=(j == NT - 1))
                ins.then_inc(S["rank_ps"], 1)
                bar()
                b2 = b + INN + OUTN

                def moe_in(n):
                    m = 32 * l + n
                    e.wait_ge(gfull[n % 2], 16 * ((NE // 2) * l + n // 2 + 1))
                    if n:
                        e.wait_ge(S["xgT_sb"], 2 * m)
                    for k in range(KD):
                        ins = e.transpose(PS[k // 4][:, (k % 4) * P:(k % 4 + 1) * P], xg[:, n % 2, k * P:(k + 1) * P], ident[:])
                    ins.then_inc(S["xgT_ps"], 1)

                def moe_up(n):
                    m = 32 * l + n
                    q = b2 + 3 * n
                    e.wait_ge(S["xgT_sb"], 2 * (m + 1))
                    if n >= 2:
                        e.wait_ge(S["hh_rdy"], m - 1)
                    for j in range(2):
                        arrived(q + j)
                        for k in range(KD):
                            ins = e.matmul(PS[2 + n % 2][:, FF * j:FF * j + FF], xgT[:, n % 2, k, :], wt(q + j)[:, k, :],
                                           start=(k == 0), stop=(k == KD - 1))
                        ins.then_inc(free[(q + j) % RING], 1)
                    e.drain().then_inc(S["gu_ps"], 1)

                def moe_down(n):
                    m = 32 * l + n
                    q = b2 + 3 * n + 2
                    e.wait_ge(S["hh_rdy"], m + 1)
                    if n:
                        e.wait_ge(S["hhT_sb"], m)
                    for k in range(2):
                        ins = e.transpose(PS[4][:, k * P:(k + 1) * P], hh[:, n % 2, k * P:(k + 1) * P], ident[:])
                    ins.then_inc(S["hhT_ps"], 1)
                    e.wait_ge(S["hhT_sb"], m + 1)
                    arrived(q)
                    if n:
                        e.wait_ge(S["y2_sb_a"], m)
                        e.wait_ge(S["y2_sb_d"], m)
                    wd = ring[:, q % RING, :].rearrange("p (k n) -> p k n", k=2)
                    for j in range(2):
                        for k in range(2):
                            ins = e.matmul(PS[5 + j][:], hhT[:, n % 2, k, :], wd[:, k, 512 * j:512 * j + 512], start=(k == 0), stop=(k == 1))
                    ins.then_inc(free[q % RING], 1)
                    e.drain().then_inc(S["y2_ps"], 1)

                some = e.value_load(ovn[0:1, 0:1], min_val=0, max_val=NOVF)
                with e.If(some > 0):
                    with e.Fori(0, NOVF) as i:
                        n = i
                        e.wait_ge(S[f"ov_gather{l}"], 16 * (n + 1))
                        for k in range(KD):
                            ins = e.transpose(PS[k // 4][:, (k % 4) * P:(k % 4 + 1) * P], xg[:, 0, k * P:(k + 1) * P], ident[:])
                        ins.then_inc(S[f"ov_pe{l}"], 1)
                        e.wait_ge(S[f"ov_x{l}"], n + 1)
                        e.wait_ge(S[f"ov_w{l}"], 48 * (n + 1))
                        for j in range(2):
                            for k in range(KD):
                                ins = e.matmul(PS[2][:, FF * j:FF * j + FF], xgT[:, 0, k, :], wov_gu[:, j, k, :],
                                               start=(k == 0), stop=(k == KD - 1))
                        ins.then_inc(S[f"ov_pe{l}"], 1)
                        e.wait_ge(S[f"ov_h{l}"], n + 1)
                        for k in range(2):
                            ins = e.transpose(PS[4][:, k * P:(k + 1) * P], hh[:, 0, k * P:(k + 1) * P], ident[:])
                        ins.then_inc(S[f"ov_pe{l}"], 1)
                        e.wait_ge(S[f"ov_hT{l}"], n + 1)
                        e.wait_ge(S[f"ov_y{l}"], n + 1)
                        for j in range(2):
                            for k in range(2):
                                ins = e.matmul(PS[5 + j][:], hhT[:, 0, k, :], wov_d[:, k, 512 * j:512 * j + 512],
                                               start=(k == 0), stop=(k == 1))
                        ins.then_inc(S[f"ov_pe{l}"], 1)
                moe_in(0)
                for n in range(NE):
                    moe_up(n)
                    if n + 1 < NE:
                        moe_in(n + 1)
                    moe_down(n)
                bar()


def near(t):
    return [j for j in (t - 1, t, t + 1) if 1 <= j < NT]


def _tiles(w):
    n = w.shape[1] // 256
    return w.reshape(KD, P, n, 256).transpose(2, 1, 0, 3).reshape(n, P, SLOT)


def _cols(v):
    return v.reshape(-1, P).T


def _rows(v):
    return np.broadcast_to(v.reshape(1, -1), (P, v.size))


def kernel(**inputs):
    import concourse.bacc as _bacc
    from concourse.bass_utils import run_bass_kernel_spmd as _run

    a = {k: np.asarray(v) for k, v in inputs.items()}
    f = np.float32
    x = np.concatenate([a["x_prompt"][0], a["x_sample"][0]]).reshape(NT, P, D).transpose(1, 0, 2)
    stream = np.empty((DEPTH * (MODN + LAYERN), P, SLOT), f)
    par = np.empty((DEPTH, P, PARN), f)
    order = np.arange(6 * D)
    order[:2 * D] = order[:2 * D].reshape(2, KD, P).transpose(0, 2, 1).ravel()
    for l in range(DEPTH):
        stream[l * MODN:(l + 1) * MODN] = _tiles(a["mod_w"][l][:, order])
        b = DEPTH * MODN + l * LAYERN
        w = a["w_in"][l]
        w = np.concatenate([w[:, :1792], w[:, 2056:2312], w[:, 1800:2056]], 1)
        stream[b:b + INN] = _tiles(w)
        stream[b + INN:b + INN + OUTN] = _tiles(a["w_out"][l])
        ex = stream[b + INN + OUTN:b + LAYERN].reshape(NE, 3, P, SLOT)
        for j, n in enumerate(("expert_w_gate", "expert_w_up")):
            ex[:, j] = a[n][l].reshape(NE, KD, P, FF).transpose(0, 2, 1, 3).reshape(NE, P, SLOT)
        ex[:, 2] = a["expert_w_down"][l].reshape(NE, 2, P, D).transpose(0, 2, 1, 3).reshape(NE, P, SLOT)

        def put(name, v):
            o, n = PAR[name]
            par[l, :, o:o + n] = v.reshape(P, n)

        put("norm1", _cols(a["norm1_w"][l]))
        put("qw", _rows(a["q_norm_w"][l]))
        put("kw", _rows(a["k_norm_w"][l]))
        put("sink", _rows(a["attn_sink"][l]))
        put("cw", a["ssd_conv_w"][l].reshape(5, 6, P).transpose(2, 1, 0))
        put("cb", _cols(a["ssd_conv_b"][l]))
        put("gw", a["cm_conv_w"][l].reshape(31, 2, P).transpose(2, 1, 0))
        put("gb", _cols(a["cm_conv_b"][l]))
        put("dtb", _rows(a["ssd_dt_bias"][l]))
        put("alog", _rows(a["ssd_a_log"][l]))
        put("dskip", _rows(a["ssd_d"][l]))
        put("snorm", _rows(a["ssd_norm_w"][l]))
        put("lnw", _rows(a["cm_norm_w"][l]))
        put("lnb", _rows(a["cm_norm_b"][l]))
        put("rw", np.concatenate([a["router_group_w"][l], a["router_expert_w"][l]], 1).reshape(KD, P, 36).transpose(1, 0, 2))
        put("rb", _rows(np.concatenate([a["router_group_b"][l], a["router_expert_b"][l]])))
        put("wdt", a["w_in"][l][:, 1792:1800].reshape(KD, P, 8).transpose(1, 0, 2))
        put("kctx", a["cache_k"][0, l].reshape(P, P).T)
        put("vctx", a["cache_v"][0, l].reshape(P, P))
        put("h0", a["state_ssm"][0, l].reshape(2, 2, 4, HD, HD).transpose(1, 4, 0, 2, 3))
    cond = np.stack([a["c_ctx"], a["c"][0]]).reshape(2, KD, P).transpose(2, 1, 0)
    modb = np.broadcast_to(a["mod_b"][:, order], (2, DEPTH, 6 * D))
    pos = np.arange(LAT)
    inv = (f(10000.0) ** (-np.arange(16, dtype=f) / f(16))).astype(f)
    ang = np.stack([(pos // 64).astype(f)[:, None] * inv, (pos % 64).astype(f)[:, None] * inv], 1)
    cs, sn = np.cos(ang), np.sin(ang)
    rope = np.stack([np.stack([cs, cs], 2), np.stack([-sn, sn], 2)]).reshape(2, NLT, P, HD).transpose(2, 0, 1, 3)

    nc = _bacc.Bacc("TRN2", target_bir_lowering=False, num_devices=1)
    arrays, args = {}, []
    for name, v in (("x", x), ("stream", stream), ("par", par), ("cond", cond), ("modb", modb),
                    ("n2row", a["norm2_w"]), ("rope", rope)):
        v = np.ascontiguousarray(v, dtype=f)
        arrays[f"in_{name}"] = v
        args.append(nc.dram_tensor(f"in_{name}", v.shape, F32, kind="ExternalInput").ap())
    outs = (("y", (P, NT, D)), ("k", (DEPTH, P, 128)), ("v", (DEPTH, P, 128)), ("st", (DEPTH, P, 2, 256)))
    for name, shape in outs:
        args.append(nc.dram_tensor(f"out_{name}", shape, F32, kind="ExternalOutput").ap())
    build(nc, *args)
    r = _run(nc, [arrays], core_ids=[0]).results[0]
    y = r["out_y"].transpose(1, 0, 2).reshape(NTOK, D)
    st = r["out_st"].reshape(DEPTH, 2, HD, 2, 4, HD).transpose(0, 3, 1, 4, 5, 2).reshape(1, DEPTH, 2, NH, HD, HD)
    return (y[None, :CTX].copy(), y[None, CTX:].copy(), r["out_k"].reshape(1, DEPTH, CTX, KVH, HD),
            r["out_v"].reshape(1, DEPTH, CTX, KVH, HD), np.ascontiguousarray(st))
```

```python
from contextlib import ExitStack

import numpy as np

import concourse.bass as bass
from concourse import mybir

ALU = mybir.AluOpType
ACT = mybir.ActivationFunctionType
F32 = mybir.dt.float32
I32 = mybir.dt.int32
AX = mybir.AxisListType.X

P = 128
D = 1024
KD = D // P
DEPTH = 2
CTX, LAT = 128, 512
NTOK = CTX + LAT
NT = NTOK // P
NLT = LAT // P
HD = 64
NH = 8
QH, KVH = 4, 2
EPS = 1e-6
BIG = 1e30

NE, EPG, NG = 32, 8, 4
FF = 256
NOVF = (2 * NTOK - NE) // P
NBLK = NE + NOVF
NOROW = 100000

SLOT = 2048
RING = 6
MODN = 6 * D // 256
INN = 9
OUTN = 4
LAYERN = INN + OUTN + 3 * NE

PAR = {}
PARN = 0
for _name, _n in (("norm1", KD), ("qw", HD), ("kw", HD), ("sink", QH), ("cw", 6 * 5), ("cb", 6),
                  ("gw", 2 * 31), ("gb", 2), ("dtb", 16), ("alog", 16), ("dskip", 16),
                  ("snorm", 512), ("lnw", 256), ("lnb", 256), ("rw", KD * 36), ("rb", 36),
                  ("wdt", KD * 8), ("kctx", P), ("vctx", P), ("h0", 512)):
    PAR[_name] = (PARN, _n)
    PARN += _n
XPAD, GPAD = 2, 15
XLEN, GLEN = NTOK + 3 * XPAD, NTOK + 3 * GPAD
XOUT, GOUT = NTOK + XPAD, NTOK + GPAD


def build(nc, x, stream, par, cond, modb, n2row, rope, y_out, k_out, v_out, st_out):
    with ExitStack() as ctx:
        def sb(name, shape, dt=F32):
            return ctx.enter_context(nc.sbuf_tensor(name, shape, dt))

        def sem(name):
            return ctx.enter_context(nc.semaphore(name))

        PS = [ctx.enter_context(nc.psum_tensor(f"bank{i}", [P, 512], F32)) for i in range(8)]
        mod_dram = nc.dram_tensor("mod_rows", (DEPTH, 2, 6 * D), F32, kind="Internal").ap()
        h2_dram = nc.dram_tensor("moe_in", (NTOK, D), F32, kind="Internal").ap()
        slot_dram = nc.dram_tensor("slot_rows", (P * NBLK, 1), I32, kind="Internal").ap()
        yk_dram = nc.dram_tensor("moe_out", (2 * NTOK, D), F32, kind="Internal").ap()

        X = sb("X", [P, NT, D])
        HT = sb("HT", [P, KD, NTOK])
        CAT = sb("CAT", [P, NT, D])
        ring = sb("ring", [P, RING, SLOT])
        RAB = sb("RAB", [P, 4, D])
        RA = RAB[:, 0:2, :]
        RB = RAB[:, 2:4, :]
        cv = RAB[:].rearrange("p a b -> p (a b)")[:, 0:6 * XOUT].rearrange("p (a b) -> p a b", b=XOUT)
        prm = sb("prm", [P, PARN])
        ident = sb("ident", [P, P])
        triF = sb("triF", [P, P])
        triB = sb("triB", [P, P])
        triS = sb("triS", [P, P])
        ones = sb("ones", [P, P])
        negF = sb("negF", [P, P])
        negB = sb("negB", [P, P])
        iota = sb("iota", [P, NE])
        ropeT = sb("ropeT", [P, 2, NLT, HD])
        condT = sb("condT", [P, KD, 2])
        modc = sb("modc", [P, 2, 2, KD])
        sm = sb("sm", [P, 1700])

        UW = 15400
        U = sb("U", [P, UW])

        def view(off, *shape, parts=P):
            n = int(np.prod(shape))
            assert off + n <= UW, (off, n)
            a = U[0:parts, off:off + n]
            if len(shape) == 1:
                return a
            names = "abcd"[:len(shape)]
            return a.rearrange(f"p ({' '.join(names)}) -> p {' '.join(names)}", **dict(zip(names[1:], shape[1:])))

        def small(off, *shape):
            n = int(np.prod(shape))
            assert off + n <= 1700
            a = sm[:, off:off + n]
            if len(shape) == 1:
                return a
            names = "abcd"[:len(shape)]
            return a.rearrange(f"p ({' '.join(names)}) -> p {' '.join(names)}", **dict(zip(names[1:], shape[1:])))

        def pr(name, *shape):
            o, n = PAR[name]
            a = prm[:, o:o + n]
            if not shape:
                return a
            names = "abcd"[:len(shape)]
            return a.rearrange(f"p ({' '.join(names)}) -> p {' '.join(names)}", **dict(zip(names[1:], shape[1:])))

        qkv = view(0, NT, 512)
        xp = view(2560, 6, XLEN)
        xs = view(2560, NT, 512)
        btok = view(2560 + NT * 512, NT, P)
        o = 2560 + 6 * XLEN
        gp = view(o, 2, GLEN)
        uc = view(o + 2 * GLEN, 2, GOUT)
        hs = view(o, 2, NLT, 256)
        o += 2 * GLEN + 2 * GOUT
        qkT = view(o, 3, NTOK)
        o += 3 * NTOK
        TMP = o
        xn = view(TMP, 2, D)
        sqs = view(TMP + 2 * D, D)
        sg = view(TMP + 3 * D, 2, NTOK)
        t1 = view(TMP, NT, 384)
        t2 = view(TMP + NT * 384, NLT, 384)
        Pm = view(TMP, QH, 512)
        PTs = view(TMP + 2048, 2, 4, P)
        LW = view(TMP, 4, 4, P)
        xdt = view(TMP + 2048, 2, 512)
        xw = view(TMP + 3072, 2, 512)
        gts = view(TMP + 4096, 2, P)
        htf = HT[:].rearrange("p a b -> p (a b)")
        off1, off2 = htf[:, 0:512], htf[:, 512:1024]
        hsc, stc = htf[:, 1024:1280], htf[:, 1536:2048].rearrange("p (a b) -> p a b", a=2)
        big = view(TMP, NT, 512)
        wtmp = view(TMP, 2, 512)
        mrow = view(0, DEPTH, 6 * D, parts=2)
        xg = view(0, 2, D)
        xgT = view(2 * D, 2, KD, P)
        hh = view(4 * D, 2, FF)
        sgate = view(4 * D + 512, 2, FF)
        hhT = view(4 * D + 1024, 2, 2, P)
        yb = view(4 * D + 1536, 2, D)
        yl = view(6 * D + 1536, 2, 2, D)
        mt = view(10 * D + 1536, 2, D)
        nrow2 = view(12 * D + 1536, D)
        cidx = sb("cidx", [P, 1], I32)
        slots = sb("slots", [P, NBLK], I32)
        gidx = sb("gidx", [P, NBLK], I32)
        svi = sb("svi", [P, 2, NT], I32)
        ovn = sb("ovn", [P, 1 + NOVF], I32)
        gcur2, scur2 = sb("gcur2", [P, 2], I32), sb("scur2", [P, 2], I32)
        gcur, scur = sb("gcur", [P, 1], I32), sb("scur", [P, 1], I32)
        wov_gu = CAT[:].rearrange("p a b -> p (a b)")[:, 0:2 * SLOT].rearrange("p (j k n) -> p j k n", j=2, k=KD)
        wov_d = HT[:].rearrange("p a b -> p (a b)")[:, 0:SLOT].rearrange("p (k n) -> p k n", k=2)
        sai = sb("sai", [P, 2, NT], I32)

        names = ("ld0 ld_par ld_rows ld_modc cst bar silu_c mod_ps mod_sb mod_st xn_ready xT_ps hT_a hT_d "
                 "pj_ps pj_sb ch_ps ch_sb ch_a pads conv_rdy convs_rdy xt_ps xt_sb uconv qk_rdy qkT_ps qkT_sb "
                 "att_s att_m att_exp att_es att_pt ptc_a ptc_d att_pv att_o kv_st st_st dt_x dt_e la_rdy cum_ps "
                 "cum_sb dec_rdy gt_ps gt_sb r_ps l_rdy w_rdy xd_rdy y_ps s_ps y_sb off_ps off_sb hs_rdy st_rdy "
                 "ut_ps ut_sb ct_ps ct_sb_a ct_sb_d wo_ps wo_sb cat_a cat_b h2_rdy h2_st h2T_ps h2T_a h2T_d lg_ps lg_sb "
                 "ge_x ge_y te_x te_y m_rdy rank_ps slot_rdy slot_init slot_st slot_ld gidx_rdy "
                 "xgT_ps xgT_sb gu_ps sgate_rdy hh_rdy hhT_ps hhT_sb y2_ps y2_sb_a y2_sb_d yg_used yst ov_go seen y_ld0 y_ld1 y_used out_st")
        S = {n: sem(n) for n in names.split()}
        for l in range(DEPTH):
            for n in "seen w gather pe x gate h hT y scatter".split():
                S[f"ov_{n}{l}"] = sem(f"ov_{n}{l}")
        full = [sem(f"ring_full{i}") for i in range(RING)]
        free = [sem(f"ring_free{i}") for i in range(RING)]
        gfull = [sem(f"gather_full{i}") for i in range(2)]
        yfree = [sem(f"scatter_done{i}") for i in range(2)]
        block = ctx.enter_context(nc.Block())

        def base(l):
            return DEPTH * MODN + l * LAYERN

        class Bars:
            def __init__(self, e):
                self.e, self.n = e, 0

            def __call__(self):
                self.n += 1
                self.e.drain().then_inc(S["bar"], 1)
                self.e.wait_ge(S["bar"], 4 * self.n)

        def cnd(t):
            return 0 if t == 0 else 1

        @block.sync
        def _(e):
            def load(q):
                if q >= RING:
                    e.wait_ge(free[q % RING], q // RING)
                e.dma_start(ring[:, q % RING, :], stream[q]).then_inc(full[q % RING], 16)

            e.dma_start(condT[:], cond).then_inc(S["ld0"], 16)
            e.dma_start(X[:], x).then_inc(S["ld0"], 16)
            e.dma_start(ropeT[:], rope).then_inc(S["ld0"], 16)
            e.dma_start(mrow, modb).then_inc(S["ld0"], 16)
            for q in range(DEPTH * MODN):
                load(q)
            for l in range(DEPTH):
                b = base(l)
                for q in range(b, b + INN + OUTN):
                    load(q)
                b += INN + OUTN
                for q in range(b, b + RING):
                    load(q)
                b += RING
                e.wait_ge(S["ov_go"], l + 1)
                some = e.value_load(ovn[0:1, 0:1], min_val=0, max_val=NOVF)
                with e.If(some > 0):
                    with e.Fori(0, NOVF) as i:
                        tile0 = e.value_load(ovn[0:1, bass.ds(i + 1, 1)], min_val=0, max_val=DEPTH * (MODN + LAYERN) - 3)
                        e.wait_ge(S[f"ov_pe{l}"], 4 * i + 1)
                        for j in range(2):
                            e.dma_start(wov_gu[:, j].rearrange("p k n -> p (k n)"),
                                        stream[bass.ds(tile0 + j, 1)].rearrange("a p n -> (a p) n")).then_inc(S[f"ov_w{l}"], 16)
                        e.dma_start(wov_d.rearrange("p k n -> p (k n)"),
                                    stream[bass.ds(tile0 + 2, 1)].rearrange("a p n -> (a p) n")).then_inc(S[f"ov_w{l}"], 16)
                with e.Fori(0, 3 * NE // RING - 1) as i:
                    for j in range(RING):
                        q = b + j
                        at = e.snap(i * RING + q)
                        e.wait_ge(free[q % RING], q // RING + i)
                        e.dma_start(ring[:, q % RING, :], stream[bass.ds(at, 1)].rearrange("a p n -> (a p) n")
                                    ).then_inc(full[q % RING], 16)

        @block.gpsimd
        def _(e):
            bar = Bars(e)
            c = S["cst"]
            for m in (ident, triF, triB, triS, ones):
                e.memset(m[:], 0.0 if m is ident else 1.0).then_inc(c, 1)
            e.memset(negF[:], 0.0).then_inc(c, 1)
            e.memset(negB[:], 0.0).then_inc(c, 1)
            e.iota(iota[:], [[1, NE]], base=0, channel_multiplier=0, allow_small_or_imprecise_dtypes=True).then_inc(c, 1)
            e.iota(svi[:], [[NTOK, 2], [P, NT]], base=0, channel_multiplier=1).then_inc(c, 1)
            e.wait_ge(c, 9)
            e.affine_select(out=ident[:], in_=ident[:], compare_op=ALU.not_equal, fill=1.0, base=0,
                            pattern=[[-1, P]], channel_multiplier=1).then_inc(c, 1)
            e.affine_select(out=triF[:], in_=triF[:], compare_op=ALU.is_ge, fill=0.0, base=0,
                            pattern=[[1, P]], channel_multiplier=-1).then_inc(c, 1)
            e.affine_select(out=triB[:], in_=triB[:], compare_op=ALU.is_ge, fill=0.0, base=0,
                            pattern=[[-1, P]], channel_multiplier=1).then_inc(c, 1)
            e.affine_select(out=triS[:], in_=triS[:], compare_op=ALU.is_gt, fill=0.0, base=0,
                            pattern=[[1, P]], channel_multiplier=-1).then_inc(c, 1)
            e.affine_select(out=negF[:], in_=negF[:], compare_op=ALU.is_ge, fill=-BIG, base=0,
                            pattern=[[1, P]], channel_multiplier=-1).then_inc(c, 1)
            e.affine_select(out=negB[:], in_=negB[:], compare_op=ALU.is_ge, fill=-BIG, base=0,
                            pattern=[[-1, P]], channel_multiplier=1).then_inc(c, 1)
            e.wait_ge(S["mod_sb"], DEPTH * 12)
            e.dma_start(mod_dram.rearrange("l c n -> c l n"), mrow).then_inc(S["mod_st"], 16)
            e.wait_ge(S["mod_st"], 16)
            bar()
            for l in range(DEPTH):
                e.dma_start(prm[:], par[l]).then_inc(S["ld_par"], 16)
                for cc in range(2):
                    for j in range(2):
                        e.dma_start(modc[:, cc, j, :], mod_dram[l, cc, j * D:(j + 1) * D].rearrange("(p k) -> p k", p=P)
                                    ).then_inc(S["ld_modc"], 16)
                for v, h in ((xp, XPAD), (gp, GPAD)):
                    for a in (0, h + CTX, 2 * h + NTOK):
                        e.memset(v[:, :, a:a + h], 0.0)
                e.drain().then_inc(S["pads"], 1)
                e.wait_ge(S["qk_rdy"], 2 * l + 1)
                e.dma_start(k_out[l], qkv[:, 0, 256:384]).then_inc(S["kv_st"], 16)
                e.dma_start(v_out[l], qkv[:, 0, 384:512]).then_inc(S["kv_st"], 16)
                e.wait_ge(S["kv_st"], 32 * (l + 1))
                bar()
                e.wait_ge(S["st_rdy"], l + 1)
                e.dma_start(st_out[l], stc).then_inc(S["st_st"], 16)
                e.wait_ge(S["st_st"], 16 * (l + 1))
                bar()
                for cc in range(2):
                    e.dma_start(RA[:, cc, :], mod_dram[l, cc:cc + 1, 2 * D:3 * D].to_broadcast((P, D))
                                ).then_inc(S["ld_rows"], 16)
                bar()
                for cc in range(2):
                    for j, dst in ((3, RB), (4, RA)):
                        e.dma_start(dst[:, cc, :], mod_dram[l, cc:cc + 1, j * D:(j + 1) * D].to_broadcast((P, D))
                                    ).then_inc(S["ld_rows"], 16)
                e.dma_start(nrow2, n2row[l:l + 1].to_broadcast((P, D))).then_inc(S["ld_rows"], 16)
                e.memset(slots[:], NOROW)
                e.drain()
                e.memset(xg, 0.0)
                e.dma_start(slot_dram.rearrange("(p n) a -> p (n a)", p=P), slots[:]).then_inc(S["slot_init"], 16)
                for t in range(NT):
                    e.wait_ge(S["h2_rdy"], NT * l + t + 1)
                    e.dma_start(h2_dram[t * P:(t + 1) * P, :], CAT[:, t, :]).then_inc(S["h2_st"], 16)
                e.wait_ge(S["slot_init"], 16 * (l + 1))
                e.wait_ge(S["slot_rdy"], l + 1)
                for k in range(2):
                    for t in range(NT):
                        e.indirect_dma_start(slot_dram, bass.IndirectOffsetOnAxis(sai[:, k, t:t + 1], 0),
                                             svi[:, k, t:t + 1], None, bounds_check=P * NBLK - 1, oob_is_err=False
                                             ).then_inc(S["slot_st"], 16)
                e.wait_ge(S["slot_st"], 160 * (l + 1))
                e.dma_start(slots[:], slot_dram.rearrange("(p n) a -> p (n a)", p=P)).then_inc(S["slot_ld"], 16)
                e.wait_ge(S["h2_st"], 16 * NT * (l + 1))
                e.wait_ge(S["gidx_rdy"], l + 1)
                bar()
                e.drain().then_inc(S["ov_go"], 1)
                for cc in range(2):
                    e.dma_start(RA[:, cc, :], mod_dram[l, cc:cc + 1, 5 * D:6 * D].to_broadcast((P, D))
                                ).then_inc(S["ld_rows"], 16)

                some = e.value_load(ovn[0:1, 0:1], min_val=0, max_val=NOVF)
                with e.If(some > 0):
                    with e.Fori(0, NOVF) as i:
                        n = i
                        e.tensor_copy(gcur[:], gidx[:, bass.ds(i + NE, 1)])
                        e.tensor_copy(scur[:], slots[:, bass.ds(i + NE, 1)])
                        e.drain()
                        e.indirect_dma_start(xg[:, 0, :], None, h2_dram, bass.IndirectOffsetOnAxis(gcur[:, 0:1], 0),
                                             bounds_check=NTOK - 1, oob_is_err=False).then_inc(S[f"ov_gather{l}"], 16)
                        e.wait_ge(S[f"ov_y{l}"], n + 2)
                        e.sem_inc(S[f"ov_seen{l}"], 1)
                        e.indirect_dma_start(yk_dram, bass.IndirectOffsetOnAxis(scur[:, 0:1], 0), yb[:, 0, :], None,
                                             bounds_check=2 * NTOK - 1, oob_is_err=False).then_inc(S[f"ov_scatter{l}"], 16)
                        e.wait_ge(S[f"ov_scatter{l}"], 16 * (n + 1))
                def gather(n, p):
                    e.tensor_copy(gcur2[:, p:p + 1], gidx[:, n:n + 1] if isinstance(n, int) else gidx[:, bass.ds(n, 1)])
                    e.drain()
                    e.indirect_dma_start(xg[:, p, :], None, h2_dram, bass.IndirectOffsetOnAxis(gcur2[:, p:p + 1], 0),
                                         bounds_check=NTOK - 1, oob_is_err=False).then_inc(gfull[p], 16)

                def pair(i, more=2):
                    for p in range(2):
                        n = 2 * i + p
                        if p < more:
                            e.wait_ge(S["xgT_ps"], n + (32 * l + 2))
                            e.sem_inc(S["seen"], 1)
                            gather(n + 3, 1 - p)
                        e.wait_ge(S["y2_sb_a"], n + (32 * l + 1))
                        e.sem_inc(S["seen"], 1)
                        e.wait_ge(S["y2_sb_d"], n + (32 * l + 1))
                        e.sem_inc(S["seen"], 1)
                        e.tensor_copy(scur2[:, p:p + 1], slots[:, n:n + 1] if isinstance(n, int) else slots[:, bass.ds(n, 1)])
                        e.drain()
                        e.indirect_dma_start(yk_dram, bass.IndirectOffsetOnAxis(scur2[:, p:p + 1], 0), yb[:, p, :], None,
                                             bounds_check=2 * NTOK - 1, oob_is_err=False).then_inc(yfree[p], 16)

                gather(0, 0)
                gather(1, 1)
                e.wait_ge(S["xgT_ps"], 32 * l + 1)
                gather(2, 0)
                pair(0)
                with e.Fori(1, NE // 2 - 2) as i:
                    pair(i)
                pair(NE // 2 - 2, 1)
                pair(NE // 2 - 1, 0)
                for i in range(2):
                    e.wait_ge(yfree[i], 16 * (NE // 2) * (l + 1))
                for t in range(NT):
                    if t >= 2:
                        e.wait_ge(S["y_used"], NT * l + t - 1)
                    for k in range(2):
                        e.dma_start(yl[:, t % 2, k, :], yk_dram[k * NTOK + t * P:k * NTOK + (t + 1) * P, :]
                                    ).then_inc(S[f"y_ld{t % 2}"], 16)
                bar()
            e.dma_start(y_out, X[:]).then_inc(S["out_st"], 16)
            e.wait_ge(S["out_st"], 16)

        @block.scalar
        def _(e):
            bar = Bars(e)
            A = e.activation
            e.wait_ge(S["ld0"], 64)
            A(condT[:], condT[:], ACT.Silu).then_inc(S["silu_c"], 1)
            bar()
            for l in range(DEPTH):
                e.sem_inc(S[f"ov_y{l}"], 1)
            for l in range(DEPTH):
                for t in range(NT):
                    e.wait_ge(S["xT_ps"], NT * l + t + 1)
                    if t == 0:
                        e.wait_ge(S["m_rdy"], 2 * l + 1)
                    for k in range(4):
                        ins = A(HT[:, k, t * P:(t + 1) * P], PS[2 * (t % 2)][:, k * P:(k + 1) * P], ACT.Identity,
                                scale=modc[:, cnd(t), 1, k:k + 1], bias=modc[:, cnd(t), 0, k:k + 1])
                    ins.then_inc(S["hT_a"], 1)
                for n in (0, 1, 4, 5, 6, 7, 8, 9):
                    e.wait_ge(S["ch_ps"], 10 * l + n + 1)
                    a, b = PS[2 * (n % 2)], PS[2 * (n % 2) + 1]
                    if n < 2:
                        A(sg[:, n, CTX:NTOK], a[:], ACT.Sigmoid)
                        ins = A(sg[:, n, 0:CTX], b[:, 0:CTX], ACT.Sigmoid)
                    else:
                        A(xp[:, n - 4, 2 * XPAD + CTX:2 * XPAD + NTOK], a[:], ACT.Copy)
                        ins = A(xp[:, n - 4, XPAD:XPAD + CTX], b[:, 0:CTX], ACT.Copy)
                    ins.then_inc(S["ch_sb"], 1)
                dtr = small(0, NT, 8)
                for n in range(15):
                    if n == 10:
                        for j in range(6):
                            e.wait_ge(S["conv_rdy"], 6 * l + j + 1)
                            A(cv[:, j, :], cv[:, j, :], ACT.Silu).then_inc(S["convs_rdy"], 1)
                    e.wait_ge(S["pj_ps"], 15 * l + n + 1)
                    t, b = n % NT, PS[4 + n % 2]
                    if n < 5:
                        ins = A(dtr[:, t, :], b[:, 0:8], ACT.Copy)
                    elif n < 10:
                        ins = A(qkv[:, t, :], b[:], ACT.Copy)
                    else:
                        ins = A(CAT[:, t, 256:768], b[:], ACT.Silu)
                    ins.then_inc(S["pj_sb"], 1)
                for n in range(7):
                    e.wait_ge(S["xt_ps"], 7 * l + n + 1)
                    b = PS[n % 2]
                    if n < 5:
                        ins = A(xs[:, n, :], b[:], ACT.Copy)
                    elif n == 5:
                        ins = A(btok[:, 0:4, :], b[:].rearrange("p (a b) -> p a b", a=4), ACT.Copy)
                    else:
                        ins = A(btok[:, 4, :], b[:, 0:P], ACT.Copy)
                    ins.then_inc(S["xt_sb"], 1)
                for t in range(NT):
                    e.wait_ge(S["qkT_ps"], NT * l + t + 1)
                    A(qkT[:, :, t * P:(t + 1) * P], PS[2 + t % 2][:, 0:384].rearrange("p (a b) -> p a b", a=3), ACT.Copy
                      ).then_inc(S["qkT_sb"], 1)
                nm, es, sums = small(44, NT, QH), small(64, NT, QH), small(84, NT, QH)
                for t in range(NT):
                    w = P if t == 0 else P * (1 + len(near(t)))
                    e.wait_ge(S["att_m"], NT * l + t + 1)
                    for h in range(QH):
                        if t:
                            e.wait_ge(S["att_pt"], 20 * l + 4 * (t - 1) + h + 1)
                        A(Pm[:, h, 0:w], PS[h][:, 0:w], ACT.Exp, bias=nm[:, t, h:h + 1], accum_out=sums[:, t, h:h + 1]
                          ).then_inc(S["att_exp"], 1)
                    A(es[:, t, :], es[:, t, :], ACT.Exp).then_inc(S["att_es"], 1)
                    for h in (0, 2):
                        n = 4 * t + h
                        e.wait_ge(S["att_pt"], 20 * l + n + 1)
                        if n >= 2:
                            e.wait_ge(S["att_pv"], 20 * l + n - 1)
                        A(PTs[:, 0, :, :].rearrange("p a b -> p (a b)")[:, 0:w], PS[4][:, 0:w], ACT.Copy).then_inc(S["ptc_a"], 1)
                bar()
                e.wait_ge(S["cat_a"], l + 1)
                A(CAT[:, :, 768:1024], CAT[:, :, 768:1024], ACT.Silu).then_inc(S["cat_b"], 1)
                e.wait_ge(S["dt_x"], l + 1)
                A(small(220, 80), small(140, 80), ACT.Exp, scale=-1.0)
                A(small(300, 16), pr("alog"), ACT.Exp).then_inc(S["dt_e"], 1)
                e.wait_ge(S["cum_sb"], l + 1)
                A(small(700, 240), small(460, 240), ACT.Exp).then_inc(S["dec_rdy"], 1)
                ncum = small(380, 2, NT, 8)
                for c in range(NT):
                    e.wait_ge(S["gt_ps"], NT * l + c + 1)
                    if c:
                        e.wait_ge(S["w_rdy"], 20 * l + 4 * c)
                    A(gts[:, 0], PS[6][:, 0:P], ACT.Copy)
                    A(gts[:, 1], PS[7][:, 0:P], ACT.Copy).then_inc(S["gt_sb"], 1)
                    for u in range(4):
                        d, g = u // 2, u % 2
                        e.wait_ge(S["r_ps"], 20 * l + 4 * c + u + 1)
                        if c and u == 0:
                            e.wait_ge(S["y_ps"], NT * l + c)
                        for j in range(4):
                            ins = A(LW[:, u, j, :], PS[u][:, j * P:(j + 1) * P], ACT.Exp, bias=ncum[:, d, c, 4 * g + j:4 * g + j + 1])
                        ins.then_inc(S["l_rdy"], 1)
                bar()
                for t in range(NT):
                    e.wait_ge(S["ct_ps"], NT * l + t + 1)
                    A(HT[:, 0:4, t * P:(t + 1) * P], PS[2 * (t % 2)][:].rearrange("p (a b) -> p a b", a=4), ACT.Copy
                      ).then_inc(S["ct_sb_a"], 1)
                bar()
                for t in range(NT):
                    e.wait_ge(S["h2T_ps"], NT * l + t + 1)
                    A(HT[:, 0:4, t * P:(t + 1) * P], PS[2 * (t % 2)][:].rearrange("p (a b) -> p a b", a=4), ACT.Copy
                      ).then_inc(S["h2T_a"], 1)
                e.wait_ge(S["ge_x"], l + 1)
                A(small(1200, NT, NG), small(1200, NT, NG), ACT.Exp).then_inc(S["ge_y"], 1)
                e.wait_ge(S["te_x"], l + 1)
                A(small(1220, NT), small(1220, NT), ACT.Exp).then_inc(S["te_y"], 1)
                bar()
                some = e.value_load(ovn[0:1, 0:1], min_val=0, max_val=NOVF)
                with e.If(some > 0):
                    with e.Fori(0, NOVF) as i:
                        n = i
                        e.wait_ge(S[f"ov_pe{l}"], 4 * n + 2)
                        for j in range(2):
                            ins = A(xgT[:, 0, 4 * j:4 * j + 4, :], PS[j][:].rearrange("p (a b) -> p a b", a=4), ACT.Copy)
                        ins.then_inc(S[f"ov_x{l}"], 1)
                        e.wait_ge(S[f"ov_pe{l}"], 4 * n + 3)
                        A(sgate[:, 0, :], PS[2][:, 0:FF], ACT.Silu).then_inc(S[f"ov_gate{l}"], 1)
                        e.wait_ge(S[f"ov_pe{l}"], 4 * n + 5)
                        for j in range(2):
                            ins = A(yb[:, 0, 512 * j:512 * j + 512], PS[5 + j][:], ACT.Copy)
                        ins.then_inc(S[f"ov_y{l}"], 1)

                def rows_in(i, p):
                    m = 2 * i + (32 * l + p)
                    e.wait_ge(S["xgT_ps"], m + 1)
                    if not isinstance(i, int) or i:
                        e.wait_ge(S["gu_ps"], m - 1)
                    A(xgT[:, p, 0:4, :], PS[0][:].rearrange("p (a b) -> p a b", a=4), ACT.Copy).then_inc(S["xgT_sb"], 1)

                def gate(i, p):
                    m = 2 * i + (32 * l + p)
                    e.wait_ge(S["gu_ps"], m + 1)
                    if not isinstance(i, int) or i:
                        e.wait_ge(S["hh_rdy"], m - 1)
                    A(sgate[:, p, :], PS[2 + p][:, 0:FF], ACT.Silu).then_inc(S["sgate_rdy"], 1)

                def result(i, p):
                    m = 2 * i + (32 * l + p)
                    e.wait_ge(S["y2_ps"], m + 1)
                    if not isinstance(i, int) or i:
                        e.wait_ge(yfree[p], 16 * i + 16 * (NE // 2) * l)
                    A(yb[:, p, 0:512], PS[5][:], ACT.Copy).then_inc(S["y2_sb_a"], 1)

                def pair(i, last=False):
                    rows_in(i, 1)
                    gate(i, 1)
                    result(i, 0)
                    if not last:
                        rows_in(i + 1, 0)
                        gate(i + 1, 0)
                    result(i, 1)

                rows_in(0, 0)
                gate(0, 0)
                pair(0)
                with e.Fori(1, NE // 2 - 1) as i:
                    pair(i)
                pair(NE // 2 - 1, True)
                bar()

        @block.vector
        def _(e):
            bar = Bars(e)
            dr = e.drain

            def rsqrt(v, a, y, yi, vi):
                e.tensor_scalar(yi, vi, 1, None, ALU.logical_shift_right); dr()
                e.tensor_scalar(yi, yi, -1.0, 1597463007.0, ALU.mult, ALU.add); dr()
                for _ in range(3):
                    e.tensor_tensor(a, y, y, ALU.mult); dr()
                    e.scalar_tensor_tensor(out=a, in0=a, scalar=-0.5, in1=v, op0=ALU.mult, op1=ALU.mult); dr()
                    e.scalar_tensor_tensor(out=y, in0=a, scalar=1.5, in1=y, op0=ALU.add, op1=ALU.mult); dr()

            def rs(n, scale, vo=1400):
                v, a, y = small(vo, n), small(vo + 50, n), small(vo + 100, n)
                e.tensor_scalar(v, v, scale, EPS, ALU.mult, ALU.add); dr()
                rsqrt(v, a, y, y.bitcast(I32), v.bitcast(I32))
                return y

            e.wait_ge(S["ld0"], 64)
            for n in range(DEPTH * 12):
                l, j = divmod(n, 12)
                e.wait_ge(S["mod_ps"], n + 1)
                m = mrow[:, l, j * 512:(j + 1) * 512]
                e.tensor_tensor(m, PS[n % 2][0:2, :], m, ALU.add).then_inc(S["mod_sb"], 1)
            bar()
            for l in range(DEPTH):
                for t in range(NT):
                    e.tensor_tensor_reduce(sqs, X[:, t, :], X[:, t, :], 1.0, 0.0, ALU.mult, ALU.add, small(1400 + t, 1))
                    dr()
                y = rs(NT, 1.0 / D)
                e.wait_ge(S["ld_par"], 16 * (l + 1))
                e.wait_ge(S["ld_modc"], 64 * (l + 1))
                for cc in range(2):
                    ins = e.scalar_tensor_tensor(out=modc[:, cc, 1, :], in0=modc[:, cc, 1, :], scalar=1.0, in1=pr("norm1"),
                                                 op0=ALU.add, op1=ALU.mult)
                dr()
                e.drain().then_inc(S["m_rdy"], 1)

                def evac1(t):
                    e.wait_ge(S["xT_ps"], NT * l + t + 1)
                    for k in range(4):
                        ins = e.tensor_scalar(HT[:, 4 + k, t * P:(t + 1) * P], PS[2 * (t % 2) + 1][:, k * P:(k + 1) * P],
                                              modc[:, cnd(t), 1, 4 + k:5 + k], modc[:, cnd(t), 0, 4 + k:5 + k], ALU.mult, ALU.add)
                    ins.then_inc(S["hT_d"], 1)

                for t in range(NT):
                    if t >= 2:
                        e.wait_ge(S["xT_ps"], NT * l + t - 1)
                    e.tensor_scalar(xn[:, t % 2, :], X[:, t, :], y[:, t:t + 1], None, ALU.mult).then_inc(S["xn_ready"], 1)
                    if t:
                        evac1(t - 1)
                evac1(NT - 1)
                for j in range(2):
                    e.wait_ge(S["ch_sb"], 8 * l + j + 1)
                    n = 2 + j
                    e.wait_ge(S["ch_ps"], 10 * l + n + 1)
                    a, b = PS[2 * (n % 2)], PS[2 * (n % 2) + 1]
                    e.tensor_tensor(gp[:, j, 2 * GPAD + CTX:2 * GPAD + NTOK], a[:], sg[:, j, CTX:NTOK], ALU.mult)
                    e.tensor_tensor(gp[:, j, GPAD:GPAD + CTX], b[:, 0:CTX], sg[:, j, 0:CTX], ALU.mult).then_inc(S["ch_a"], 1)
                dr()
                e.wait_ge(S["pads"], l + 1)
                gw, gb = pr("gw", 2, 31), pr("gb")
                for ct in range(2):
                    e.tensor_scalar(uc[:, ct, :], gp[:, ct, 0:GOUT], gw[:, ct, 0:1], gb[:, ct:ct + 1], ALU.mult, ALU.add); dr()
                    for k in range(1, 31):
                        ins = e.scalar_tensor_tensor(out=uc[:, ct, :], in0=gp[:, ct, k:k + GOUT], scalar=gw[:, ct, k:k + 1],
                                                     in1=uc[:, ct, :], op0=ALU.mult, op1=ALU.add)
                        if k < 30:
                            dr()
                    ins.then_inc(S["uconv"], 1)
                cw, cb = pr("cw", 6, 5), pr("cb")
                for n in range(6):
                    e.wait_ge(S["ch_sb"], 8 * l + 3 + n)
                    e.tensor_scalar(cv[:, n, :], xp[:, n, 0:XOUT], cw[:, n, 0:1], cb[:, n:n + 1], ALU.mult, ALU.add); dr()
                    for k in range(1, 5):
                        ins = e.scalar_tensor_tensor(out=cv[:, n, :], in0=xp[:, n, k:k + XOUT], scalar=cw[:, n, k:k + 1],
                                                     in1=cv[:, n, :], op0=ALU.mult, op1=ALU.add)
                        if k < 4:
                            dr()
                    ins.then_inc(S["conv_rdy"], 1)
                e.wait_ge(S["pj_sb"], 15 * l + 10)
                qk = qkv[:, :, 0:384]
                e.tensor_tensor(t1, qk, qk, ALU.mult); dr()
                e.tensor_reduce(small(1400, 30), t1.rearrange("p t (h d) -> p (t h) d", d=HD), AX, ALU.add); dr()
                y = rs(30, 1.0 / HD)
                for t in range(NT):
                    yt = y[:, 6 * t:6 * t + 6].unsqueeze(2).to_broadcast((P, 6, HD))
                    e.tensor_tensor(t1[:, t, :].rearrange("p (h d) -> p h d", d=HD), qkv[:, t, 0:384].rearrange("p (h d) -> p h d", d=HD),
                                    yt, ALU.mult)
                dr()
                for t in range(NT):
                    for g in range(2):
                        e.scalar_tensor_tensor(out=qkv[:, t, 128 * g:128 * g + 128].rearrange("p (k d) -> p k d", k=2),
                                               in0=t1[:, t, 0:256].rearrange("p (k g d) -> p g k d", g=2, d=HD)[:, g],
                                               scalar=HD ** -0.5,
                                               in1=pr("qw").unsqueeze(1).to_broadcast((P, 2, HD)), op0=ALU.mult, op1=ALU.mult)
                    e.tensor_tensor(qkv[:, t, 256:384].rearrange("p (k d) -> p k d", k=2),
                                    t1[:, t, 256:384].rearrange("p (k d) -> p k d", k=2),
                                    pr("kw").unsqueeze(1).to_broadcast((P, 2, HD)), ALU.mult)
                dr()
                e.drain().then_inc(S["qk_rdy"], 1)
                for t in range(1, NT):
                    q6 = qkv[:, t, 0:384].rearrange("p (h d) -> p h d", d=HD)
                    e.tensor_tensor(t1[:, t, :].rearrange("p (h d) -> p h d", d=HD), q6,
                                    ropeT[:, 0, t - 1, :].unsqueeze(1).to_broadcast((P, 6, HD)), ALU.mult)
                    halves = "p (h a b f) -> p b h a f"
                    qh = qkv[:, t, 0:384].rearrange(halves, a=2, b=2, f=16)
                    th = t2[:, t - 1, :].rearrange(halves, a=2, b=2, f=16)
                    sn = ropeT[:, 1, t - 1, :].rearrange("p (a b f) -> p b a f", b=2, f=16)
                    for b in range(2):
                        e.tensor_tensor(th[:, b], qh[:, 1 - b], sn[:, b].unsqueeze(1).to_broadcast((P, 6, 2, 16)), ALU.mult)
                dr()
                e.tensor_tensor(qkv[:, 1:NT, 0:384], t1[:, 1:NT, :], t2, ALU.add).then_inc(S["qk_rdy"], 1)

                mx, nm, es, sums, den = small(40, QH), small(44, NT, QH), small(64, NT, QH), small(84, NT, QH), small(104, QH)

                def att_max(t):
                    w = P if t == 0 else P * (1 + len(near(t)))
                    for h in range(QH):
                        e.wait_ge(S["att_s"], 20 * l + 4 * t + h + 1)
                        e.tensor_reduce(mx[:, h:h + 1], PS[h][:, 0:w], AX, ALU.max)
                    dr()
                    e.tensor_tensor(mx, mx, pr("sink"), ALU.max); dr()
                    e.tensor_scalar(nm[:, t, :], mx, -1.0, None, ALU.mult); dr()
                    e.tensor_tensor(es[:, t, :], nm[:, t, :], pr("sink"), ALU.add).then_inc(S["att_m"], 1)
                    dr()

                att_max(0)
                for t in range(NT):
                    if t + 1 < NT:
                        att_max(t + 1)
                    w = P if t == 0 else P * (1 + len(near(t)))
                    for h in (1, 3):
                        n = 4 * t + h
                        e.wait_ge(S["att_pt"], 20 * l + n + 1)
                        if n >= 2:
                            e.wait_ge(S["att_pv"], 20 * l + n - 1)
                        e.tensor_copy(PTs[:, 1, :, :].rearrange("p a b -> p (a b)")[:, 0:w], PS[5][:, 0:w]).then_inc(S["ptc_d"], 1)
                    e.wait_ge(S["att_es"], NT * l + t + 1)
                    e.tensor_tensor(den, sums[:, t, :], es[:, t, :], ALU.add); dr()
                    e.reciprocal(den, den); dr()
                    e.wait_ge(S["att_pv"], 20 * l + 4 * t + 4)
                    e.tensor_tensor(CAT[:, t, 0:256].rearrange("p (h d) -> p h d", d=HD),
                                    PS[6 + t % 2][:, 0:256].rearrange("p (h d) -> p h d", d=HD),
                                    den.unsqueeze(2).to_broadcast((P, QH, HD)), ALU.mult).then_inc(S["att_o"], 1)
                    dr()
                for t in range(NT):
                    e.wait_ge(S["ut_ps"], NT * l + t + 1)
                    e.tensor_copy(CAT[:, t, 768:1024], PS[6 + t % 2][:, 256:512]).then_inc(S["ut_sb"], 1)
                e.wait_ge(S["att_pt"], 20 * (l + 1))
                e.wait_ge(S["att_pv"], 20 * (l + 1))
                dr()
                lt = view(TMP, NT, 256)
                cu = CAT[:, :, 768:1024]
                mean = small(1200, NT, 4)
                for t in range(NT):
                    e.tensor_reduce(mean[:, t, :], CAT[:, t, 768:1024].rearrange("p (g d) -> p g d", d=HD), AX, ALU.add)
                dr()
                for t in range(NT):
                    c4 = CAT[:, t, 768:1024].rearrange("p (g d) -> p g d", d=HD)
                    e.scalar_tensor_tensor(out=c4, in0=mean[:, t, :].unsqueeze(2).to_broadcast((P, 4, HD)), scalar=-1.0 / HD, in1=c4,
                                           op0=ALU.mult, op1=ALU.add)
                dr()
                e.tensor_tensor(lt, cu, cu, ALU.mult); dr()
                e.tensor_reduce(small(1400, 20), lt.rearrange("p t (g d) -> p (t g) d", d=HD), AX, ALU.add); dr()
                y = rs(20, 1.0 / HD)
                for t in range(NT):
                    c4 = CAT[:, t, 768:1024].rearrange("p (g d) -> p g d", d=HD)
                    e.tensor_tensor(c4, c4, y[:, 4 * t:4 * t + 4].unsqueeze(2).to_broadcast((P, 4, HD)), ALU.mult)
                dr()
                e.tensor_tensor(cu, cu, pr("lnw").unsqueeze(1).to_broadcast((P, NT, 256)), ALU.mult); dr()
                e.tensor_tensor(cu, cu, pr("lnb").unsqueeze(1).to_broadcast((P, NT, 256)), ALU.add).then_inc(S["cat_a"], 1)
                bar()
                xdir, ax, ee = small(1240, 80), small(140, 80), small(220, 80)
                x4 = small(1240, 2, NT, 8)
                dtr = small(0, NT, 8)
                for d in range(2):
                    e.tensor_tensor(x4[:, d], dtr, pr("dtb")[:, 8 * d:8 * d + 8].unsqueeze(1).to_broadcast((P, NT, 8)), ALU.add)
                dr()
                e.tensor_scalar(ax, xdir, -1.0, None, ALU.mult); dr()
                e.tensor_tensor(ax, ax, xdir, ALU.max).then_inc(S["dt_x"], 1)
                e.tensor_scalar(xdir, xdir, 0.0, None, ALU.max)
                e.wait_ge(S["dt_e"], l + 1)
                dr()
                s_, z_, p_ = small(940, 80), small(1020, 80), small(1100, 80)
                e.tensor_scalar(s_, ee, 2.0, None, ALU.add); dr()
                e.reciprocal(s_, s_); dr()
                e.tensor_tensor(s_, s_, ee, ALU.mult); dr()
                e.tensor_tensor(z_, s_, s_, ALU.mult); dr()
                e.tensor_scalar(p_, z_, 1.0 / 17, None, ALU.mult); dr()
                for k in (15, 13, 11, 9, 7, 5, 3):
                    e.scalar_tensor_tensor(out=p_, in0=p_, scalar=1.0 / k, in1=z_, op0=ALU.add, op1=ALU.mult); dr()
                e.scalar_tensor_tensor(out=p_, in0=p_, scalar=1.0, in1=s_, op0=ALU.add, op1=ALU.mult); dr()
                dt, la = small(1320, 80), small(1020, 80)
                e.scalar_tensor_tensor(out=dt, in0=p_, scalar=2.0, in1=xdir, op0=ALU.mult, op1=ALU.add); dr()
                dt4, la4 = small(1320, 2, NT, 8), small(1020, 2, NT, 8)
                for d in range(2):
                    ins = e.scalar_tensor_tensor(out=la4[:, d], in0=dt4[:, d], scalar=-1.0,
                                                 in1=small(300, 2, 8)[:, d].unsqueeze(1).to_broadcast((P, NT, 8)),
                                                 op0=ALU.mult, op1=ALU.mult)
                ins.then_inc(S["la_rdy"], 1)
                e.wait_ge(S["cum_ps"], l + 1)
                e.tensor_copy(small(460, 160), PS[7][:, 0:160]); dr()
                e.tensor_scalar(small(380, 80), small(460, 80), -1.0, None, ALU.mult)
                e.tensor_tensor(small(620, 80), small(540, 80), small(460, 80), ALU.subtract).then_inc(S["cum_sb"], 1)
                e.wait_ge(S["dec_rdy"], l + 1)
                dec, cd, dte = small(700, 2, NT, 8), small(780, 2, NT, 8), small(860, 2, NT, 8)
                dsum = small(320, 8)
                e.tensor_tensor(dsum, pr("dskip")[:, 0:8], pr("dskip")[:, 8:16], ALU.add)
                e.tensor_copy(hs[:, 0, 0, :], pr("h0")[:, 0:256])
                e.tensor_copy(hs[:, 1, NLT - 1, :], pr("h0")[:, 256:512])
                dr()

                def h3(a, n=8):
                    return a.rearrange("p (h d) -> p h d", d=HD)

                def decayed(out, src, d, c):
                    for g in range(2):
                        r = slice(64 * g, 64 * g + 64)
                        e.tensor_tensor(h3(out[r]), h3(src[r]),
                                        cd[r, d, c, 4 * g:4 * g + 4].unsqueeze(2).to_broadcast((64, 4, HD)), ALU.mult)

                for c in range(NT):
                    if c:
                        e.wait_ge(S["s_ps"], NT * l + c)
                    for d in range(2):
                        e.tensor_tensor(h3(xdt[:, d, :]), h3(xs[:, c, :]), dt4[:, d, c, :].unsqueeze(2).to_broadcast((P, 8, HD)), ALU.mult)
                    dr()
                    for d in range(2):
                        ins = e.tensor_tensor(h3(xw[:, d, :]), h3(xdt[:, d, :]), dte[:, d, c, :].unsqueeze(2).to_broadcast((P, 8, HD)), ALU.mult)
                    ins.then_inc(S["xd_rdy"], 1)
                    e.tensor_tensor(h3(xs[:, c, :]), h3(xs[:, c, :]), dsum.unsqueeze(2).to_broadcast((P, 8, HD)), ALU.mult)
                    e.wait_ge(S["gt_sb"], NT * l + c + 1)
                    for u in range(4):
                        e.wait_ge(S["l_rdy"], 20 * l + 4 * c + u + 1)
                        e.tensor_tensor(LW[:, u], LW[:, u], gts[:, u % 2].unsqueeze(1).to_broadcast((P, 4, P)), ALU.mult
                                        ).then_inc(S["w_rdy"], 1)
                    e.wait_ge(S["s_ps"], NT * l + c + 1)
                    sp = PS[5]
                    if c == 0:
                        e.tensor_copy(stc.rearrange("p a b -> p (a b)"), sp[:]).then_inc(S["st_rdy"], 1)
                    else:
                        i = c - 1
                        if i < NLT - 1:
                            decayed(hsc, hs[:, 0, i, :], 0, c); dr()
                            e.tensor_tensor(hs[:, 0, i + 1, :], sp[:, 0:256], hsc, ALU.add)
                        if i:
                            e.tensor_copy(hs[:, 1, i - 1, :], sp[:, 256:512])
                    dr()
                    e.tensor_tensor(xs[:, c, :], PS[4][:], xs[:, c, :], ALU.add).then_inc(S["y_sb"], 1)
                for i in range(NLT - 1, 0, -1):
                    decayed(hsc, hs[:, 1, i, :], 1, i + 1); dr()
                    e.tensor_tensor(hs[:, 1, i - 1, :], hs[:, 1, i - 1, :], hsc, ALU.add); dr()
                e.drain().then_inc(S["hs_rdy"], 1)
                for i in range(NLT):
                    c = i + 1
                    e.wait_ge(S["off_ps"], NLT * l + i + 1)
                    for d, dst in ((0, off1), (1, off2)):
                        for g in range(2):
                            ins = e.tensor_tensor(h3(dst[:, 256 * g:256 * g + 256]), h3(PS[2 * (i % 2) + g][:, 256 * d:256 * d + 256]),
                                                  dec[:, d, c, 4 * g:4 * g + 4].unsqueeze(2).to_broadcast((P, 4, HD)), ALU.mult)
                    ins.then_inc(S["off_sb"], 1)
                    dr()
                    e.tensor_tensor(xs[:, c, :], xs[:, c, :], off1, ALU.add); dr()
                    e.tensor_tensor(xs[:, c, :], xs[:, c, :], off2, ALU.add); dr()
                cz = CAT[:, :, 256:768]
                e.wait_ge(S["st_st"], 16 * (l + 1))
                e.tensor_tensor(xs, xs, cz, ALU.mult); dr()
                e.tensor_tensor(big, xs, xs, ALU.mult); dr()
                e.tensor_reduce(small(1400, 10), big.rearrange("p t (g d) -> p (t g) d", d=256), AX, ALU.add); dr()
                y = rs(10, 1.0 / 256)
                for t in range(NT):
                    for g in range(2):
                        e.scalar_tensor_tensor(out=CAT[:, t, 256 + 256 * g:512 + 256 * g], in0=xs[:, t, 256 * g:256 * g + 256],
                                               scalar=y[:, 2 * t + g:2 * t + g + 1], in1=pr("snorm")[:, 256 * g:256 * g + 256],
                                               op0=ALU.mult, op1=ALU.mult)
                bar()
                for t in range(NT):
                    e.wait_ge(S["ct_ps"], NT * l + t + 1)
                    e.tensor_copy(HT[:, 4:8, t * P:(t + 1) * P], PS[2 * (t % 2) + 1][:].rearrange("p (a b) -> p a b", a=4)
                                  ).then_inc(S["ct_sb_d"], 1)
                e.wait_ge(S["ld_rows"], 16 * (9 * l + 2))
                for n in range(2 * NT):
                    t, hf = n % NT, n // NT
                    e.wait_ge(S["wo_ps"], 10 * l + n + 1)
                    e.tensor_tensor(wtmp[:, n % 2, :], PS[4 + n % 2][:], RA[:, cnd(t), 512 * hf:512 * hf + 512], ALU.mult
                                    ).then_inc(S["wo_sb"], 1)
                    dr()
                    e.tensor_tensor(X[:, t, 512 * hf:512 * hf + 512], X[:, t, 512 * hf:512 * hf + 512], wtmp[:, n % 2, :], ALU.add)
                bar()
                for t in range(NT):
                    e.tensor_tensor_reduce(mt[:, 0, :], X[:, t, :], X[:, t, :], 1.0, 0.0, ALU.mult, ALU.add, small(1400 + t, 1))
                    dr()
                y = rs(NT, 1.0 / D)
                e.wait_ge(S["ld_rows"], 16 * (9 * l + 7))
                for cc in range(2):
                    e.scalar_tensor_tensor(out=RA[:, cc, :], in0=RA[:, cc, :], scalar=1.0, in1=nrow2, op0=ALU.add, op1=ALU.mult)
                dr()
                e.drain().then_inc(S["m_rdy"], 1)

                def evac2(t):
                    e.wait_ge(S["h2T_ps"], NT * l + t + 1)
                    e.tensor_copy(HT[:, 4:8, t * P:(t + 1) * P], PS[2 * (t % 2) + 1][:].rearrange("p (a b) -> p a b", a=4)
                                  ).then_inc(S["h2T_d"], 1)

                for t in range(NT):
                    e.scalar_tensor_tensor(out=mt[:, t % 2, :], in0=X[:, t, :], scalar=y[:, t:t + 1], in1=RA[:, cnd(t), :],
                                           op0=ALU.mult, op1=ALU.mult); dr()
                    e.tensor_tensor(CAT[:, t, :], mt[:, t % 2, :], RB[:, cnd(t), :], ALU.add).then_inc(S["h2_rdy"], 1)
                    if t:
                        evac2(t - 1)
                evac2(NT - 1)
                lg = small(0, NT, 36)
                for t in range(NT):
                    e.wait_ge(S["lg_ps"], NT * l + t + 1)
                    e.tensor_tensor(lg[:, t, :], PS[4 + t % 2][:, 0:36], pr("rb"), ALU.add).then_inc(S["lg_sb"], 1)
                dr()
                gl, el = lg[:, :, 0:NG], lg[:, :, NG:36]

                def first_max(src, n, m, i, oh, tmp):
                    io = iota[:, 0:n].unsqueeze(1).to_broadcast((P, NT, n))
                    e.tensor_reduce(m, src, AX, ALU.max); dr()
                    e.tensor_tensor(tmp, src, m.unsqueeze(2).to_broadcast((P, NT, n)), ALU.is_equal); dr()
                    e.scalar_tensor_tensor(out=tmp, in0=tmp, scalar=-64.0, in1=io, op0=ALU.mult, op1=ALU.add); dr()
                    e.tensor_reduce(i, tmp, AX, ALU.min); dr()
                    e.tensor_scalar(i, i, 64.0, None, ALU.add); dr()
                    e.tensor_tensor(oh, i.unsqueeze(2).to_broadcast((P, NT, n)), io, ALU.is_equal); dr()

                gm, gi, m1, i1, m2, i2 = (small(180 + 5 * j, NT) for j in range(6))
                goh, gt = small(210, NT, NG), small(230, NT, NG)
                o1, o2, tm, es8 = (small(250 + 40 * j, NT, EPG) for j in range(4))
                first_max(gl, NG, gm, gi, goh, gt)
                gx = small(1200, NT, NG)
                e.tensor_tensor(gx, gl, gm.unsqueeze(2).to_broadcast((P, NT, NG)), ALU.subtract).then_inc(S["ge_x"], 1)
                tm32 = small(420, NT, NG, EPG)
                for t in range(NT):
                    e.tensor_tensor(tm32[:, t], el[:, t, :].rearrange("p (g x) -> p g x", g=NG),
                                    goh[:, t, :].unsqueeze(2).to_broadcast((P, NG, EPG)), ALU.mult)
                dr()
                for t in range(NT):
                    e.tensor_reduce(es8[:, t, :], tm32[:, t].rearrange("p g x -> p x g"), AX, ALU.add)
                dr()
                first_max(es8, EPG, m1, i1, o1, tm)
                e.scalar_tensor_tensor(out=es8, in0=o1, scalar=-BIG, in1=es8, op0=ALU.mult, op1=ALU.add); dr()
                first_max(es8, EPG, m2, i2, o2, tm)
                dx = small(1220, NT)
                e.tensor_tensor(dx, m2, m1, ALU.subtract).then_inc(S["te_x"], 1)
                M1, M2, MM = small(580, NT, NE), small(740, NT, NE), small(900, NT, NE)
                for t in range(NT):
                    for Mk, ok in ((M1, o1), (M2, o2)):
                        e.tensor_tensor(Mk[:, t, :].rearrange("p (g x) -> p g x", g=NG),
                                        goh[:, t, :].unsqueeze(2).to_broadcast((P, NG, EPG)),
                                        ok[:, t, :].unsqueeze(1).to_broadcast((P, NG, EPG)), ALU.mult)
                dr()
                e.tensor_tensor(MM, M1, M2, ALU.add).then_inc(S["lg_sb"], 1)
                e.wait_ge(S["ge_y"], l + 1)
                pg, wd = small(1225, NT), small(1230, NT)
                W1, W2 = small(1235, NT), small(1240, NT)
                e.tensor_reduce(pg, gx, AX, ALU.add); dr()
                e.wait_ge(S["te_y"], l + 1)
                e.scalar_tensor_tensor(out=wd, in0=dx, scalar=1.0, in1=pg, op0=ALU.add, op1=ALU.mult); dr()
                e.reciprocal(W1, wd); dr()
                e.tensor_tensor(W2, W1, dx, ALU.mult)
                e.wait_ge(S["rank_ps"], l + 1)
                rk, cnt = small(420, NT, NE), small(1245, NE)
                e.tensor_copy(rk, PS[6][:, 0:NT * NE].rearrange("p (t n) -> p t n", t=NT))
                e.tensor_copy(cnt, PS[6][:, NT * NE:NT * NE + NE]); dr()
                nov, cs, cs2 = small(1280, NE), small(1320, 16 + NE), small(1370, 16 + NE)
                e.tensor_scalar(nov, cnt, float(P), None, ALU.is_gt); dr()
                for j in range(2, 5):
                    e.scalar_tensor_tensor(out=nov, in0=cnt, scalar=float(P * j), in1=nov, op0=ALU.is_gt, op1=ALU.add); dr()
                e.memset(cs[:, 0:16], 0.0)
                e.memset(cs2[:, 0:16], 0.0)
                e.tensor_copy(cs[:, 16:16 + NE], nov); dr()
                a_, b_ = cs, cs2
                for j in (1, 2, 4, 8, 16):
                    e.tensor_tensor(b_[:, 16:16 + NE], a_[:, 16:16 + NE], a_[:, 16 - j:16 - j + NE], ALU.add); dr()
                    a_, b_ = b_, a_
                ovs = small(1630, NE)
                e.tensor_tensor(ovs, a_[:, 16:16 + NE], nov, ALU.subtract); dr()
                ovf, cmp = small(1662, 1 + NOVF), small(1060, 4, NE)
                for i in range(NOVF):
                    e.tensor_scalar(cmp[:, i % 4, :], a_[:, 16:16 + NE], float(i), None, ALU.is_le); dr()
                    e.tensor_reduce(ovf[:, 1 + i:2 + i], cmp[:, i % 4, :], AX, ALU.add); dr()
                e.tensor_copy(ovf[:, 0:1], a_[:, 16 + NE - 1:16 + NE])
                e.tensor_scalar(ovf[:, 1:], ovf[:, 1:], float(NE - 1), None, ALU.min); dr()
                e.tensor_scalar(ovf[:, 1:], ovf[:, 1:], 3.0, float(base(l) + INN + OUTN), ALU.mult, ALU.add); dr()
                e.tensor_copy(ovn[:], ovf)
                for k, Mk in ((0, M1), (1, M2)):
                    tt = small(0, NT, NE)
                    rk_, ek, ok_, mk, sl = (small(160 + 5 * j, NT) for j in range(5))
                    for dst, src in ((rk_, rk), (ek, iota[:].unsqueeze(1).to_broadcast((P, NT, NE))),
                                     (ok_, ovs.unsqueeze(1).to_broadcast((P, NT, NE)))):
                        e.tensor_tensor(tt, Mk, src, ALU.mult); dr()
                        e.tensor_reduce(dst, tt, AX, ALU.add); dr()
                    e.tensor_scalar(mk, rk_, float(P), None, ALU.is_ge); dr()
                    for j in range(2, 5):
                        e.scalar_tensor_tensor(out=mk, in0=rk_, scalar=float(P * j), in1=mk, op0=ALU.is_ge, op1=ALU.add); dr()
                    e.tensor_scalar(sl, mk, 0.0, None, ALU.is_gt)
                    e.tensor_tensor(ok_, ok_, ek, ALU.subtract); dr()
                    e.scalar_tensor_tensor(out=ok_, in0=ok_, scalar=float(NE - 1), in1=mk, op0=ALU.add, op1=ALU.add); dr()
                    e.tensor_tensor(ok_, ok_, sl, ALU.mult); dr()
                    e.tensor_tensor(ek, ek, ok_, ALU.add)
                    e.scalar_tensor_tensor(out=rk_, in0=mk, scalar=float(-P), in1=rk_, op0=ALU.mult, op1=ALU.add); dr()
                    e.scalar_tensor_tensor(out=rk_, in0=rk_, scalar=float(NBLK), in1=ek, op0=ALU.mult, op1=ALU.add); dr()
                    e.tensor_copy(sai[:, k, :], rk_); dr()
                e.drain().then_inc(S["slot_rdy"], 1)
                e.wait_ge(S["slot_ld"], 16 * (l + 1))
                sf, sf2 = small(0, NBLK), small(50, NBLK)
                e.tensor_copy(sf, slots[:]); dr()
                e.tensor_scalar(sf2, sf, float(NTOK), float(-NTOK), ALU.is_ge, ALU.mult); dr()
                e.tensor_tensor(sf, sf, sf2, ALU.add); dr()
                e.tensor_copy(gidx[:], sf).then_inc(S["gidx_rdy"], 1)
                bar()
                some = e.value_load(ovn[0:1, 0:1], min_val=0, max_val=NOVF)
                with e.If(some > 0):
                    with e.Fori(0, NOVF) as i:
                        n = i
                        e.wait_ge(S[f"ov_gate{l}"], n + 1)
                        e.tensor_tensor(hh[:, 0, :], PS[2][:, FF:2 * FF], sgate[:, 0, :], ALU.mult).then_inc(S[f"ov_h{l}"], 1)
                        e.wait_ge(S[f"ov_pe{l}"], 4 * n + 4)
                        e.tensor_copy(hhT[:, 0], PS[4][:, 0:256].rearrange("p (a b) -> p a b", a=2)).then_inc(S[f"ov_hT{l}"], 1)

                def rows_in(i, p):
                    m = 2 * i + (32 * l + p)
                    e.wait_ge(S["xgT_ps"], m + 1)
                    if not isinstance(i, int) or i:
                        e.wait_ge(S["gu_ps"], m - 1)
                    e.tensor_copy(xgT[:, p, 4:8, :], PS[1][:].rearrange("p (a b) -> p a b", a=4)).then_inc(S["xgT_sb"], 1)

                def gated(i, p):
                    m = 2 * i + (32 * l + p)
                    e.wait_ge(S["sgate_rdy"], m + 1)
                    if not isinstance(i, int) or i:
                        e.wait_ge(S["hhT_ps"], m - 1)
                    e.tensor_tensor(hh[:, p, :], PS[2 + p][:, FF:2 * FF], sgate[:, p, :], ALU.mult).then_inc(S["hh_rdy"], 1)

                def turned(i, p):
                    m = 2 * i + (32 * l + p)
                    e.wait_ge(S["hhT_ps"], m + 1)
                    if not isinstance(i, int) or i:
                        e.wait_ge(S["y2_ps"], m - 1)
                    e.tensor_copy(hhT[:, p], PS[4][:, 0:256].rearrange("p (a b) -> p a b", a=2)).then_inc(S["hhT_sb"], 1)

                def result(i, p):
                    m = 2 * i + (32 * l + p)
                    e.wait_ge(S["y2_ps"], m + 1)
                    if not isinstance(i, int) or i:
                        e.wait_ge(yfree[p], 16 * i + 16 * (NE // 2) * l)
                    e.tensor_copy(yb[:, p, 512:1024], PS[6][:]).then_inc(S["y2_sb_d"], 1)

                def pair(i, last=False):
                    rows_in(i, 1)
                    turned(i, 0)
                    gated(i, 1)
                    result(i, 0)
                    if not last:
                        rows_in(i + 1, 0)
                    turned(i, 1)
                    if not last:
                        gated(i + 1, 0)
                    result(i, 1)

                rows_in(0, 0)
                gated(0, 0)
                pair(0)
                with e.Fori(1, NE // 2 - 1) as i:
                    pair(i)
                pair(NE // 2 - 1, True)
                e.wait_ge(S["ld_rows"], 16 * 9 * (l + 1))
                for t in range(NT):
                    uses = (3 * l + t // 2 + 1) if t % 2 == 0 else (2 * l + t // 2 + 1)
                    e.wait_ge(S[f"y_ld{t % 2}"], 32 * uses)
                    e.tensor_scalar(mt[:, t % 2, :], yl[:, t % 2, 0, :], W1[:, t:t + 1], None, ALU.mult); dr()
                    e.scalar_tensor_tensor(out=mt[:, t % 2, :], in0=yl[:, t % 2, 1, :], scalar=W2[:, t:t + 1], in1=mt[:, t % 2, :],
                                           op0=ALU.mult, op1=ALU.add).then_inc(S["y_used"], 1)
                    dr()
                    e.tensor_tensor(mt[:, t % 2, :], mt[:, t % 2, :], RA[:, cnd(t), :], ALU.mult); dr()
                    e.tensor_tensor(X[:, t, :], X[:, t, :], mt[:, t % 2, :], ALU.add); dr()
                bar()

        @block.tensor
        def _(e):
            bar = Bars(e)

            def arrived(q):
                e.wait_ge(full[q % RING], 16 * (q // RING + 1))

            def wt(q):
                return ring[:, q % RING, :].rearrange("p (k n) -> p k n", k=KD)

            e.wait_ge(S["silu_c"], 1)
            for n in range(DEPTH * 12):
                if n >= 2:
                    e.wait_ge(S["mod_sb"], n - 1)
                for h in range(2):
                    q = 2 * n + h
                    arrived(q)
                    for k in range(KD):
                        ins = e.matmul(PS[n % 2][0:2, 256 * h:256 * h + 256], condT[:, k, :], wt(q)[:, k, :], start=(k == 0), stop=(k == KD - 1))
                        if k == KD - 1:
                            ins.then_inc(free[q % RING], 1)
                e.drain().then_inc(S["mod_ps"], 1)
            e.wait_ge(S["cst"], 15)
            bar()
            for l in range(DEPTH):
                e.sem_inc(S[f"ov_pe{l}"], 1)
            for l in range(DEPTH):
                b = base(l)
                for t in range(NT):
                    e.wait_ge(S["xn_ready"], NT * l + t + 1)
                    if t >= 2:
                        e.wait_ge(S["hT_a"], NT * l + t - 1)
                        e.wait_ge(S["hT_d"], NT * l + t - 1)
                    for k in range(KD):
                        ins = e.transpose(PS[2 * (t % 2) + k // 4][:, (k % 4) * P:(k % 4 + 1) * P], xn[:, t % 2, k * P:(k + 1) * P], ident[:])
                    ins.then_inc(S["xT_ps"], 1)
                e.wait_ge(S["hT_a"], NT * (l + 1))
                e.wait_ge(S["hT_d"], NT * (l + 1))
                e.wait_ge(S["ld_par"], 16 * (l + 1))
                wdt = pr("wdt", KD, 8)
                for n in range(10):
                    q = b + n // 2
                    arrived(q)
                    if n in (2, 3):
                        e.wait_ge(S["ch_sb"], 8 * l + n - 1)
                    elif n in (4, 5):
                        e.wait_ge(S["ch_a"], 2 * l + n - 3)
                    elif n > 5:
                        e.wait_ge(S["ch_sb"], 8 * l + n - 3)
                    lat, cx = PS[2 * (n % 2)], PS[2 * (n % 2) + 1]
                    for out, lo, w in ((lat[:], CTX, LAT), (cx[:, 0:CTX], 0, CTX)):
                        for k in range(KD):
                            ins = e.matmul(out, wt(q)[:, k, P * (n % 2):P * (n % 2) + P], HT[:, k, lo:lo + w], start=(k == 0), stop=(k == KD - 1))
                    ins.then_inc(S["ch_ps"], 1)
                    if n % 2:
                        e.drain().then_inc(free[q % RING], 1)
                for n in range(15):
                    t, bank = n % NT, PS[4 + n % 2]
                    if n >= 2:
                        e.wait_ge(S["pj_sb"], 15 * l + n - 1)
                    if n >= 5:
                        q = b + 3 + 2 * (n // NT)
                        arrived(q)
                        arrived(q + 1)
                        for h in range(2):
                            for k in range(KD):
                                ins = e.matmul(bank[:, 256 * h:256 * h + 256], HT[:, k, t * P:(t + 1) * P], wt(q + h)[:, k, :],
                                               start=(k == 0), stop=(k == KD - 1))
                        ins.then_inc(S["pj_ps"], 1)
                        if t == NT - 1:
                            for h in range(2):
                                e.drain().then_inc(free[(q + h) % RING], 1)
                    else:
                        for k in range(KD):
                            ins = e.matmul(bank[:, 0:8], HT[:, k, t * P:(t + 1) * P], wdt[:, k, :], start=(k == 0), stop=(k == KD - 1))
                        ins.then_inc(S["pj_ps"], 1)

                def at(n, t):
                    s = t * P + (0 if t == 0 else XPAD)
                    return cv[:, n, s:s + P]

                e.wait_ge(S["convs_rdy"], 6 * (l + 1))
                for n in range(7):
                    if n >= 2:
                        e.wait_ge(S["xt_sb"], 7 * l + n - 1)
                    src = [(j, n) for j in range(4)] if n < 5 else [(4, t) for t in (range(4) if n == 5 else (4,))]
                    for i, (j, t) in enumerate(src):
                        ins = e.transpose(PS[n % 2][:, i * P:(i + 1) * P], at(j, t), ident[:])
                    ins.then_inc(S["xt_ps"], 1)
                e.wait_ge(S["qk_rdy"], 2 * (l + 1))
                for t in range(NT):
                    if t >= 2:
                        e.wait_ge(S["qkT_sb"], NT * l + t - 1)
                    for j in range(3):
                        ins = e.transpose(PS[2 + t % 2][:, j * P:(j + 1) * P], qkv[:, t, j * P:(j + 1) * P], ident[:])
                    ins.then_inc(S["qkT_ps"], 1)
                e.wait_ge(S["xt_sb"], 7 * (l + 1))
                e.wait_ge(S["qkT_sb"], NT * (l + 1))
                e.wait_ge(S["pj_sb"], 15 * (l + 1))

                def att_scores(t):
                    for h in range(QH):
                        if t:
                            e.wait_ge(S["att_exp"], 20 * l + 4 * (t - 1) + h + 1)
                        kv, g = h // 2, h % 2
                        r = slice(64 * kv, 64 * kv + 64)
                        q = qkT[r, g, t * P:(t + 1) * P]
                        if t == 0:
                            ins = e.matmul(PS[h][:, 0:P], q, qkT[r, 2, 0:P], start=True, stop=True)
                        else:
                            nb = near(t)
                            w = P * len(nb)
                            e.matmul(PS[h][:, 0:P], q, pr("kctx")[r, :], start=True, stop=False, skip_group_check=True)
                            ins = e.matmul(PS[h][:, P:P + w], q, qkT[r, 2, nb[0] * P:nb[0] * P + w], start=False, stop=True, skip_group_check=True)
                            for i, j in enumerate(nb):
                                if j != t:
                                    ins = e.matmul(PS[h][:, P + i * P:P + i * P + P], ident[:], (negF if j < t else negB)[:],
                                                   start=False, stop=True, skip_group_check=True)
                        ins.then_inc(S["att_s"], 1)

                att_scores(0)
                for t in range(NT):
                    if t + 1 < NT:
                        att_scores(t + 1)
                    nb = [0] if t == 0 else [-1] + near(t)

                    def pv(h):
                        n = 4 * t + h
                        kv = h // 2
                        if h % 2 == 0:
                            e.wait_ge(S["ptc_a"], 10 * l + n // 2 + 1)
                        else:
                            e.wait_ge(S["ptc_d"], 10 * l + n // 2 + 1)
                        if t >= 2 and h == 0:
                            e.wait_ge(S["att_o"], NT * l + t - 1)
                        for i, j in enumerate(nb):
                            v = pr("vctx")[:, 64 * kv:64 * kv + 64] if j < 0 else qkv[:, j, 384 + 64 * kv:448 + 64 * kv]
                            ins = e.matmul(PS[6 + t % 2][:, 64 * h:64 * h + 64], PTs[:, h % 2, i, :], v, start=(i == 0), stop=(i == len(nb) - 1))
                        ins.then_inc(S["att_pv"], 1)

                    for h in range(QH):
                        n = 4 * t + h
                        e.wait_ge(S["att_exp"], 20 * l + n + 1)
                        if n >= 2:
                            if h % 2 == 0:
                                e.wait_ge(S["ptc_a"], 10 * l + n // 2)
                            else:
                                e.wait_ge(S["ptc_d"], 10 * l + n // 2)
                        for i in range(len(nb)):
                            ins = e.transpose(PS[4 + h % 2][:, i * P:(i + 1) * P], Pm[:, h, i * P:(i + 1) * P], ident[:])
                        ins.then_inc(S["att_pt"], 1)
                        if h:
                            pv(h - 1)
                    pv(3)
                e.wait_ge(S["uconv"], 2 * (l + 1))
                e.wait_ge(S["att_o"], NT * (l + 1))
                for t in range(NT):
                    if t >= 2:
                        e.wait_ge(S["ut_sb"], NT * l + t - 1)
                    s = t * P + (0 if t == 0 else GPAD)
                    for j in range(2):
                        ins = e.transpose(PS[6 + t % 2][:, 256 + j * P:256 + (j + 1) * P], uc[:, j, s:s + P], ident[:])
                    ins.then_inc(S["ut_ps"], 1)
                bar()
                la4 = small(1020, 2, NT, 8)
                e.wait_ge(S["la_rdy"], l + 1)
                e.matmul(PS[7][:, 0:40], triF[:], small(1020, 40), start=True, stop=True)
                e.matmul(PS[7][:, 40:80], triB[:], small(1060, 40), start=True, stop=True)
                e.matmul(PS[7][:, 80:160], ones[:], small(1020, 80), start=True, stop=True).then_inc(S["cum_ps"], 1)

                def ssd_pre(c):
                    if c:
                        e.wait_ge(S["gt_sb"], NT * l + c)
                    for g in range(2):
                        r = slice(64 * g, 64 * g + 64)
                        ins = e.matmul(PS[6 + g][:, 0:P], at(4, c)[r], at(5, c)[r], start=True, stop=True)
                    ins.then_inc(S["gt_ps"], 1)
                    for u in range(4):
                        d, g = u // 2, u % 2
                        if c:
                            e.wait_ge(S["l_rdy"], 20 * l + 4 * (c - 1) + u + 1)
                        e.matmul(PS[u][:], ident[:], (negB if d else negF)[:].unsqueeze(1).to_broadcast((P, 4, P)),
                                 start=True, stop=False, skip_group_check=True)
                        for j in range(4):
                            ins = e.matmul(PS[u][:, j * P:(j + 1) * P], la4[:, d, c, 4 * g + j:4 * g + j + 1].to_broadcast((P, P)),
                                           (triB if d else triF)[:], start=False, stop=True, skip_group_check=True)
                        ins.then_inc(S["r_ps"], 1)

                e.wait_ge(S["cum_sb"], l + 1)
                ssd_pre(0)
                for c in range(NT):
                    if c + 1 < NT:
                        ssd_pre(c + 1)
                    e.wait_ge(S["xd_rdy"], NT * l + c + 1)
                    if c:
                        e.wait_ge(S["y_sb"], NT * l + c)
                    for d in range(2):
                        for g in range(2):
                            ins = e.matmul(PS[5][64 * g:64 * g + 64, 256 * d:256 * d + 256], btok[:, c, 64 * g:64 * g + 64],
                                           xw[:, d, 256 * g:256 * g + 256], start=True, stop=True)
                    e.wait_ge(S["w_rdy"], 20 * l + 4 * c + 4)
                    for h in range(NH):
                        for d in range(2):
                            ins = e.matmul(PS[4][:, 64 * h:64 * h + 64], LW[:, 2 * d + h // 4, h % 4, :], xdt[:, d, 64 * h:64 * h + 64],
                                           start=(d == 0), stop=(d == 1))
                    e.drain().then_inc(S["y_ps"], 1)
                    e.drain().then_inc(S["s_ps"], 1)
                e.wait_ge(S["hs_rdy"], l + 1)
                for i in range(NLT):
                    if i >= 2:
                        e.wait_ge(S["off_sb"], NLT * l + i - 1)
                    for d in range(2):
                        for g in range(2):
                            r = slice(64 * g, 64 * g + 64)
                            ins = e.matmul(PS[2 * (i % 2) + g][:, 256 * d:256 * d + 256], at(5, i + 1)[r], hs[r, d, i, :], start=True, stop=True)
                    ins.then_inc(S["off_ps"], 1)
                bar()
                e.wait_ge(S["cat_b"], l + 1)

                def to_channels(signal, a, d_, src):
                    for t in range(NT):
                        if t >= 2:
                            e.wait_ge(S[a], NT * l + t - 1)
                            e.wait_ge(S[d_], NT * l + t - 1)
                        if src == "h2":
                            e.wait_ge(S["h2_rdy"], NT * l + t + 1)
                        for k in range(KD):
                            ins = e.transpose(PS[2 * (t % 2) + k // 4][:, (k % 4) * P:(k % 4 + 1) * P], CAT[:, t, k * P:(k + 1) * P], ident[:])
                        ins.then_inc(S[signal], 1)
                    e.wait_ge(S[a], NT * (l + 1))
                    e.wait_ge(S[d_], NT * (l + 1))

                to_channels("ct_ps", "ct_sb_a", "ct_sb_d", "cat")
                for n in range(2 * NT):
                    t, hf = n % NT, n // NT
                    q = b + INN + 2 * hf
                    arrived(q)
                    arrived(q + 1)
                    if n >= 2:
                        e.wait_ge(S["wo_sb"], 10 * l + n - 1)
                    for j in range(2):
                        for k in range(KD):
                            ins = e.matmul(PS[4 + n % 2][:, 256 * j:256 * j + 256], HT[:, k, t * P:(t + 1) * P], wt(q + j)[:, k, :],
                                           start=(k == 0), stop=(k == KD - 1))
                    ins.then_inc(S["wo_ps"], 1)
                    if t == NT - 1:
                        for j in range(2):
                            e.drain().then_inc(free[(q + j) % RING], 1)
                bar()
                to_channels("h2T_ps", "h2T_a", "h2T_d", "h2")
                rw = pr("rw", KD, 36)
                for t in range(NT):
                    if t >= 2:
                        e.wait_ge(S["lg_sb"], 6 * l + t - 1)
                    for k in range(KD):
                        ins = e.matmul(PS[4 + t % 2][:, 0:36], HT[:, k, t * P:(t + 1) * P], rw[:, k, :], start=(k == 0), stop=(k == KD - 1))
                    ins.then_inc(S["lg_ps"], 1)
                MM = small(900, NT, NE)
                e.wait_ge(S["lg_sb"], 6 * (l + 1))
                for t in range(NT):
                    for j in range(t + 1):
                        e.matmul(PS[6][:, NE * t:NE * t + NE], (triS if j == t else ones)[:], MM[:, j, :], start=(j == 0), stop=(j == t))
                for j in range(NT):
                    ins = e.matmul(PS[6][:, NE * NT:NE * NT + NE], ones[:], MM[:, j, :], start=(j == 0), stop=(j == NT - 1))
                ins.then_inc(S["rank_ps"], 1)
                bar()
                b2 = b + INN + OUTN

                some = e.value_load(ovn[0:1, 0:1], min_val=0, max_val=NOVF)
                with e.If(some > 0):
                    with e.Fori(0, NOVF) as i:
                        n = i
                        e.wait_ge(S[f"ov_gather{l}"], 16 * (n + 1))
                        for k in range(KD):
                            ins = e.transpose(PS[k // 4][:, (k % 4) * P:(k % 4 + 1) * P], xg[:, 0, k * P:(k + 1) * P], ident[:])
                        ins.then_inc(S[f"ov_pe{l}"], 1)
                        e.wait_ge(S[f"ov_x{l}"], n + 1)
                        e.wait_ge(S[f"ov_w{l}"], 48 * (n + 1))
                        for j in range(2):
                            for k in range(KD):
                                ins = e.matmul(PS[2][:, FF * j:FF * j + FF], xgT[:, 0, k, :], wov_gu[:, j, k, :],
                                               start=(k == 0), stop=(k == KD - 1))
                        ins.then_inc(S[f"ov_pe{l}"], 1)
                        e.wait_ge(S[f"ov_h{l}"], n + 1)
                        for k in range(2):
                            ins = e.transpose(PS[4][:, k * P:(k + 1) * P], hh[:, 0, k * P:(k + 1) * P], ident[:])
                        ins.then_inc(S[f"ov_pe{l}"], 1)
                        e.wait_ge(S[f"ov_hT{l}"], n + 1)
                        e.wait_ge(S[f"ov_y{l}"], n + 1)
                        for j in range(2):
                            for k in range(2):
                                ins = e.matmul(PS[5 + j][:], hhT[:, 0, k, :], wov_d[:, k, 512 * j:512 * j + 512],
                                               start=(k == 0), stop=(k == 1))
                        ins.then_inc(S[f"ov_pe{l}"], 1)

                def tile(i, p, j):
                    q = b2 + 3 * p + j
                    return q % RING, i + q // RING

                def rows_in(i, p):
                    m = 2 * i + (32 * l + p)
                    e.wait_ge(gfull[p], 16 * i + 16 * ((NE // 2) * l + 1))
                    if not isinstance(i, int) or i or p:
                        e.wait_ge(S["xgT_sb"], 2 * m)
                    for k in range(KD):
                        ins = e.transpose(PS[k // 4][:, (k % 4) * P:(k % 4 + 1) * P], xg[:, p, k * P:(k + 1) * P], ident[:])
                    ins.then_inc(S["xgT_ps"], 1)

                def up(i, p, j):
                    m = 2 * i + (32 * l + p)
                    if j == 0:
                        e.wait_ge(S["xgT_sb"], 2 * m + 2)
                        if not isinstance(i, int) or i:
                            e.wait_ge(S["hh_rdy"], m - 1)
                    slot, use = tile(i, p, j)
                    e.wait_ge(full[slot], 16 * use + 16)
                    w = ring[:, slot, :].rearrange("p (k n) -> p k n", k=KD)
                    for k in range(KD):
                        ins = e.matmul(PS[2 + p][:, FF * j:FF * j + FF], xgT[:, p, k, :], w[:, k, :], start=(k == 0), stop=(k == KD - 1))
                    if j:
                        ins.then_inc(S["gu_ps"], 1)
                    else:
                        ins.then_inc(free[slot], 1)

                def turn(i, p):
                    m = 2 * i + (32 * l + p)
                    e.wait_ge(S["hh_rdy"], m + 1)
                    if not isinstance(i, int) or i or p:
                        e.wait_ge(S["hhT_sb"], m)
                    for k in range(2):
                        ins = e.transpose(PS[4][:, k * P:(k + 1) * P], hh[:, p, k * P:(k + 1) * P], ident[:])
                    ins.then_inc(S["hhT_ps"], 1)

                def down(i, p, used):
                    m = 2 * i + (32 * l + p)
                    e.wait_ge(S["hhT_sb"], m + 1)
                    slot, use = tile(i, p, 2)
                    e.wait_ge(full[slot], 16 * use + 16)
                    if not isinstance(i, int) or i or p:
                        e.wait_ge(S["y2_sb_a"], m)
                        e.wait_ge(S["y2_sb_d"], m)
                    wd = ring[:, slot, :].rearrange("p (k n) -> p k n", k=2)
                    for k in range(2):
                        for j in range(2):
                            ins = e.matmul(PS[5 + j][:], hhT[:, p, k, :], wd[:, k, 512 * j:512 * j + 512], start=(k == 0), stop=(k == 1))
                            if k == 0 and j == 0 and used is not None:
                                ins.then_inc(free[used], 1)
                    ins.then_inc(free[slot], 1)
                    e.drain().then_inc(S["y2_ps"], 1)

                def pair(i, last=False):
                    rows_in(i, 1)
                    up(i, 1, 0)
                    turn(i, 0)
                    up(i, 1, 1)
                    down(i, 0, tile(0, 1, 1)[0])
                    if not last:
                        rows_in(i + 1, 0)
                        up(i + 1, 0, 0)
                        turn(i, 1)
                        up(i + 1, 0, 1)
                        down(i, 1, tile(0, 0, 1)[0])
                    else:
                        turn(i, 1)
                        down(i, 1, None)

                rows_in(0, 0)
                up(0, 0, 0)
                up(0, 0, 1)
                e.drain().then_inc(free[tile(0, 0, 1)[0]], 1)
                pair(0)
                with e.Fori(1, NE // 2 - 1) as i:
                    pair(i)
                pair(NE // 2 - 1, True)
                bar()


def near(t):
    return [j for j in (t - 1, t, t + 1) if 1 <= j < NT]


def _tiles(w):
    n = w.shape[1] // 256
    return w.reshape(KD, P, n, 256).transpose(2, 1, 0, 3).reshape(n, P, SLOT)


def _cols(v):
    return v.reshape(-1, P).T


def _rows(v):
    return np.broadcast_to(v.reshape(1, -1), (P, v.size))


def kernel(**inputs):
    import concourse.bacc as _bacc
    from concourse.bass_utils import run_bass_kernel_spmd as _run

    a = {k: np.asarray(v) for k, v in inputs.items()}
    f = np.float32
    x = np.concatenate([a["x_prompt"][0], a["x_sample"][0]]).reshape(NT, P, D).transpose(1, 0, 2)
    stream = np.empty((DEPTH * (MODN + LAYERN), P, SLOT), f)
    par = np.empty((DEPTH, P, PARN), f)
    order = np.arange(6 * D)
    order[:2 * D] = order[:2 * D].reshape(2, KD, P).transpose(0, 2, 1).ravel()
    for l in range(DEPTH):
        stream[l * MODN:(l + 1) * MODN] = _tiles(a["mod_w"][l][:, order])
        b = DEPTH * MODN + l * LAYERN
        w = a["w_in"][l]
        w = np.concatenate([w[:, 2056:2312], w[:, 1800:2056], w[:, 1024:1792], w[:, :1024]], 1)
        stream[b:b + INN] = _tiles(w)
        stream[b + INN:b + INN + OUTN] = _tiles(a["w_out"][l])
        ex = stream[b + INN + OUTN:b + LAYERN].reshape(NE, 3, P, SLOT)
        for j, n in enumerate(("expert_w_gate", "expert_w_up")):
            ex[:, j] = a[n][l].reshape(NE, KD, P, FF).transpose(0, 2, 1, 3).reshape(NE, P, SLOT)
        ex[:, 2] = a["expert_w_down"][l].reshape(NE, 2, P, D).transpose(0, 2, 1, 3).reshape(NE, P, SLOT)

        def put(name, v):
            o, n = PAR[name]
            par[l, :, o:o + n] = v.reshape(P, n)

        put("norm1", _cols(a["norm1_w"][l]))
        put("qw", _rows(a["q_norm_w"][l]))
        put("kw", _rows(a["k_norm_w"][l]))
        put("sink", _rows(a["attn_sink"][l]))
        put("cw", a["ssd_conv_w"][l].reshape(5, 6, P).transpose(2, 1, 0))
        put("cb", _cols(a["ssd_conv_b"][l]))
        put("gw", a["cm_conv_w"][l].reshape(31, 2, P).transpose(2, 1, 0))
        put("gb", _cols(a["cm_conv_b"][l]))
        put("dtb", _rows(a["ssd_dt_bias"][l]))
        put("alog", _rows(a["ssd_a_log"][l]))
        put("dskip", _rows(a["ssd_d"][l]))
        put("snorm", _rows(a["ssd_norm_w"][l]))
        put("lnw", _rows(a["cm_norm_w"][l]))
        put("lnb", _rows(a["cm_norm_b"][l]))
        put("rw", np.concatenate([a["router_group_w"][l], a["router_expert_w"][l]], 1).reshape(KD, P, 36).transpose(1, 0, 2))
        put("rb", _rows(np.concatenate([a["router_group_b"][l], a["router_expert_b"][l]])))
        put("wdt", a["w_in"][l][:, 1792:1800].reshape(KD, P, 8).transpose(1, 0, 2))
        put("kctx", a["cache_k"][0, l].reshape(P, P).T)
        put("vctx", a["cache_v"][0, l].reshape(P, P))
        put("h0", a["state_ssm"][0, l].reshape(2, 2, 4, HD, HD).transpose(1, 4, 0, 2, 3))
    cond = np.stack([a["c_ctx"], a["c"][0]]).reshape(2, KD, P).transpose(2, 1, 0)
    modb = np.broadcast_to(a["mod_b"][:, order], (2, DEPTH, 6 * D))
    pos = np.arange(LAT)
    inv = (f(10000.0) ** (-np.arange(16, dtype=f) / f(16))).astype(f)
    ang = np.stack([(pos // 64).astype(f)[:, None] * inv, (pos % 64).astype(f)[:, None] * inv], 1)
    cs, sn = np.cos(ang), np.sin(ang)
    rope = np.stack([np.stack([cs, cs], 2), np.stack([-sn, sn], 2)]).reshape(2, NLT, P, HD).transpose(2, 0, 1, 3)

    nc = _bacc.Bacc("TRN2", target_bir_lowering=False, num_devices=1)
    arrays, args = {}, []
    for name, v in (("x", x), ("stream", stream), ("par", par), ("cond", cond), ("modb", modb),
                    ("n2row", a["norm2_w"]), ("rope", rope)):
        v = np.ascontiguousarray(v, dtype=f)
        arrays[f"in_{name}"] = v
        args.append(nc.dram_tensor(f"in_{name}", v.shape, F32, kind="ExternalInput").ap())
    outs = (("y", (P, NT, D)), ("k", (DEPTH, P, 128)), ("v", (DEPTH, P, 128)), ("st", (DEPTH, P, 2, 256)))
    for name, shape in outs:
        args.append(nc.dram_tensor(f"out_{name}", shape, F32, kind="ExternalOutput").ap())
    build(nc, *args)
    r = _run(nc, [arrays], core_ids=[0]).results[0]
    y = r["out_y"].transpose(1, 0, 2).reshape(NTOK, D)
    st = r["out_st"].reshape(DEPTH, 2, HD, 2, 4, HD).transpose(0, 3, 1, 4, 5, 2).reshape(1, DEPTH, 2, NH, HD, HD)
    return (y[None, :CTX].copy(), y[None, CTX:].copy(), r["out_k"].reshape(1, DEPTH, CTX, KVH, HD),
            r["out_v"].reshape(1, DEPTH, CTX, KVH, HD), np.ascontiguousarray(st))
```

```python
from contextlib import ExitStack

import numpy as np

import concourse.bass as bass
from concourse import mybir

ALU = mybir.AluOpType
ACT = mybir.ActivationFunctionType
F32 = mybir.dt.float32
BF16 = mybir.dt.bfloat16
I32 = mybir.dt.int32
AX = mybir.AxisListType.X

P = 128
D = 1024
KD = D // P
DEPTH = 2
CTX, LAT = 128, 512
NTOK = CTX + LAT
NT = NTOK // P
NLT = LAT // P
HD = 64
NH = 8
QH, KVH = 4, 2
EPS = 1e-6
BIG = 1e30

NE, EPG, NG = 32, 8, 4
FF = 256
NOVF = (2 * NTOK - NE) // P
NBLK = NE + NOVF
NOROW = 100000

SLOT = 2048
RING = 6
AHEAD = 3
MOD0 = 2 * D // 256
MODC = 3 * D // 256
INN = 9
OUTN = 4


def modd(l):
    return D // 256 + (MOD0 if l + 1 < DEPTH else 0)


def base(l):
    return MOD0 + sum(INN + MODC + OUTN + modd(i) + 3 * NE for i in range(l))


def experts(l):
    return base(l) + INN + MODC + OUTN + modd(l)



PAR = {}
PARN = 0
for _name, _n in (("norm1", KD), ("qw", HD), ("kw", HD), ("sink", QH), ("cw", 6 * 5), ("cb", 6),
                  ("gw", 2 * 31), ("gb", 2), ("dtb", 16), ("alog", 16), ("dskip", 16),
                  ("snorm", 512), ("lnw", 256), ("lnb", 256), ("rw", KD * 36), ("rb", 36),
                  ("wdt", KD * 8), ("kctx", P), ("vctx", P), ("h0", 512)):
    PAR[_name] = (PARN, _n)
    PARN += _n
XPAD, GPAD = 2, 15
XLEN, GLEN = NTOK + 3 * XPAD, NTOK + 3 * GPAD
XOUT, GOUT = NTOK + XPAD, NTOK + GPAD


def build(nc, x, stream, par, cond, modb, n2row, rope, y_out, k_out, v_out, st_out):
    with ExitStack() as ctx:
        def sb(name, shape, dt=F32):
            return ctx.enter_context(nc.sbuf_tensor(name, shape, dt))

        def sem(name):
            return ctx.enter_context(nc.semaphore(name))

        PS = [ctx.enter_context(nc.psum_tensor(f"bank{i}", [P, 512], F32)) for i in range(8)]
        mod_dram = nc.dram_tensor("mod_rows", (2, DEPTH, 6 * D), F32, kind="Internal").ap()
        h2_dram = nc.dram_tensor("moe_in", (NTOK, D), F32, kind="Internal").ap()
        yk_dram = nc.dram_tensor("moe_out", (2 * NTOK, D), F32, kind="Internal").ap()

        X = sb("X", [P, NT, D])
        HT = sb("HT", [P, KD, NTOK])
        CAT = sb("CAT", [P, NT, D])
        ring = sb("ring", [P, RING, SLOT])
        RAB = sb("RAB", [P, 4, D])
        RA = RAB[:, 0:2, :]
        RB = RAB[:, 2:4, :]
        cv = RAB[:].rearrange("p a b -> p (a b)")[:, 0:6 * XOUT].rearrange("p (a b) -> p a b", b=XOUT)
        prm = sb("prm", [P, PARN])
        ident = sb("ident", [P, P])
        triF = sb("triF", [P, P])
        triB = sb("triB", [P, P])
        triS = sb("triS", [P, P])
        ones = sb("ones", [P, P])
        negF = sb("negF", [P, P], BF16)
        negB = sb("negB", [P, P], BF16)
        ident16 = sb("ident16", [P, P], BF16)
        iota = sb("iota", [P, P])
        ropeT = sb("ropeT", [P, 2, NLT, HD])
        condT = sb("condT", [P, KD, 2])
        modc = sb("modc", [P, 2, 2, KD])
        sm = sb("sm", [P, 1700])

        UW = 15400
        U = sb("U", [P, UW])

        def view(off, *shape, parts=P):
            n = int(np.prod(shape))
            assert off + n <= UW, (off, n)
            a = U[0:parts, off:off + n]
            if len(shape) == 1:
                return a
            names = "abcd"[:len(shape)]
            return a.rearrange(f"p ({' '.join(names)}) -> p {' '.join(names)}", **dict(zip(names[1:], shape[1:])))

        def small(off, *shape):
            n = int(np.prod(shape))
            assert off + n <= 1700
            a = sm[:, off:off + n]
            if len(shape) == 1:
                return a
            names = "abcd"[:len(shape)]
            return a.rearrange(f"p ({' '.join(names)}) -> p {' '.join(names)}", **dict(zip(names[1:], shape[1:])))

        def pr(name, *shape):
            o, n = PAR[name]
            a = prm[:, o:o + n]
            if not shape:
                return a
            names = "abcd"[:len(shape)]
            return a.rearrange(f"p ({' '.join(names)}) -> p {' '.join(names)}", **dict(zip(names[1:], shape[1:])))

        qkv = view(0, NT, 512)
        xp = view(2560, 6, XLEN)
        xs = view(2560, NT, 512)
        btok = view(2560 + NT * 512, NT, P)
        o = 2560 + 6 * XLEN
        gp = view(o, 2, GLEN)
        uc = view(o + 2 * GLEN, 2, GOUT)
        hs = view(o, 2, NLT, 256)
        o += 2 * GLEN + 2 * GOUT
        qkT = view(o, 3, NTOK)
        o += 3 * NTOK
        TMP = o
        xn = view(TMP, 2, D)
        sqs = view(TMP + 2 * D, D)
        sg = view(TMP + 3 * D, 2, NTOK)
        t1 = view(TMP, NT, 384)
        t2 = view(TMP + NT * 384, NLT, 384)
        Pm = view(TMP, QH, 512)
        PTs = view(TMP + 2048, 2, 4, P)
        LW = view(TMP, 4, 4, P)
        xdt = view(TMP + 2048, 2, 512)
        xw = view(TMP + 3072, 2, 512)
        gts = view(TMP + 4096, 2, P)
        htf = HT[:].rearrange("p a b -> p (a b)")
        off1, off2 = htf[:, 0:512], htf[:, 512:1024]
        hsc, stc = htf[:, 1024:1280], htf[:, 1536:2048].rearrange("p (a b) -> p a b", a=2)
        big = view(TMP, NT, 512)
        wtmp = view(TMP, 2, 512)
        mrow = view(0, 2 * D, parts=2)
        frow = RAB[0:2].rearrange("p a b -> p (a b)")[:, D:4 * D]
        mod_flat = mod_dram.rearrange("c l n -> c (l n)")
        modb_flat = modb.rearrange("c l n -> c (l n)")
        xg = view(0, 2, D)
        xgT = view(2 * D, 2, KD, P)
        hh = view(4 * D, 2, FF)
        sgate = view(4 * D + 512, 2, FF)
        hhT = view(4 * D + 1024, 2, 2, P)
        yb = view(4 * D + 1536, 2, D)
        yk = (CAT[:], HT[:].rearrange("p a b -> p (a b)").rearrange("p (t d) -> p t d", d=D))
        RC = view(6 * D + 1536, 2, D)
        mt = view(10 * D + 1536, 2, D)
        place = view(6 * D + 1536, 2 * NT, P)
        blockno = view(8 * D + 1536, 2 * NT, NBLK)
        nrow2 = view(12 * D + 1536, D)
        cidx = sb("cidx", [P, 1], I32)
        slots = sb("slots", [P, NBLK], I32)
        gidx = sb("gidx", [P, NBLK], I32)
        rowno = sb("rowno", [P, 2, NT])
        ovn = sb("ovn", [P, 1 + NOVF], I32)
        gcur2, scur2 = sb("gcur2", [P, 2], I32), sb("scur2", [P, 2], I32)
        gcur, scur = sb("gcur", [P, 1], I32), sb("scur", [P, 1], I32)
        wov_gu = CAT[:].rearrange("p a b -> p (a b)")[:, 0:2 * SLOT].rearrange("p (j k n) -> p j k n", j=2, k=KD)
        wov_d = HT[:].rearrange("p a b -> p (a b)")[:, 0:SLOT].rearrange("p (k n) -> p k n", k=2)

        names = ("ld0 ld_par ld_g1 ld_rows ld_g2 ld_modc cst bar silu_c mod_ps mod_sb mod_st ld_cond ld_modb fill_ps fill_sb gather_rows scatter_rows y_half x_rdy x_added sq_rdy xn_ready xT_ps hT_a hT_d "
                 "pj_ps pj_sb ch_ps ch_sb ch_a pads conv_rdy convs_rdy xt_ps xt_sb uconv qk_rdy qkT_ps qkT_sb "
                 "att_s att_m att_exp att_es att_pt ptc_a ptc_d att_pv att_o kv_st st_st dt_x dt_e la_rdy cum_ps "
                 "cum_sb dec_rdy gt_ps gt_sb r_ps l_rdy w_rdy xd_rdy y_ps s_ps y_sb off_ps off_sb hs_rdy st_rdy "
                 "ut_ps ut_sb ct_ps ct_sb_a ct_sb_d wo_ps wo_sb cat_a cat_b h2_rdy h2_st h2T_ps h2T_a h2T_d lg_ps lg_sb "
                 "ge_x ge_y te_x te_y m_rdy rank_ps slot_rdy slot_ps gidx_rdy "
                 "xgT_ps xgT_sb gu_ps sgate_rdy hh_rdy hhT_ps hhT_sb y2_ps y2_sb_a y2_sb_d yg_used ov_go seen out_st")
        S = {n: sem(n) for n in names.split()}
        for l in range(DEPTH):
            for n in "seen w gather pe x gate h hT y scatter".split():
                S[f"ov_{n}{l}"] = sem(f"ov_{n}{l}")
        full = [sem(f"ring_full{i}") for i in range(RING)]
        free = [sem(f"ring_free{i}") for i in range(RING)]
        gfull = [sem(f"gather_full{i}") for i in range(2)]
        yld = [sem(f"moe_rows_back{t}") for t in range(NT)]
        yfree = [sem(f"scatter_done{i}") for i in range(2)]
        block = ctx.enter_context(nc.Block())

        class Bars:
            def __init__(self, e):
                self.e, self.n = e, 0

            def __call__(self):
                self.n += 1
                self.e.drain().then_inc(S["bar"], 1)
                self.e.wait_ge(S["bar"], 4 * self.n)

        MODBANK = (6, 7, 4, 5, 0, 1), (0, 1, 4, 5, 2, 3)
        LATE = (4, 5, 0, 1, 2, 3)

        def before_slots(l):
            return min(4, modd(l) // 2)

        def mod_chunks(l, part):
            return sum(MODC + modd(i) for i in range(l)) // 2 + part * (MODC // 2)

        def cnd(t):
            return 0 if t == 0 else 1

        @block.sync
        def _(e):
            def load(q):
                if q >= RING:
                    e.wait_ge(free[q % RING], q // RING)
                e.dma_start(ring[:, q % RING, :], stream[q]).then_inc(full[q % RING], 16)

            e.dma_start(condT[:], cond).then_inc(S["ld_cond"], 16)
            for q in range(2):
                load(q)
            e.dma_start(mrow, modb_flat[:, 0:2 * D]).then_inc(S["ld0"], 16)
            e.dma_start(X[:], x).then_inc(S["ld0"], 16)
            e.dma_start(ropeT[:], rope).then_inc(S["ld0"], 16)
            for q in range(2, MOD0):
                load(q)
            for l in range(DEPTH):
                b = experts(l)
                for q in range(base(l) + (AHEAD if l else 0), b):
                    load(q)
                for q in range(b, b + RING):
                    load(q)
                b += RING
                e.wait_ge(S["ov_go"], l + 1)
                some = e.value_load(ovn[0:1, 0:1], min_val=0, max_val=NOVF)
                with e.If(some > 0):
                    with e.Fori(0, NOVF) as i:
                        tile0 = e.value_load(ovn[0:1, bass.ds(i + 1, 1)], min_val=0, max_val=experts(DEPTH - 1) + 3 * NE - 3)
                        e.wait_ge(S[f"ov_pe{l}"], 4 * i + 1)
                        for j in range(2):
                            e.dma_start(wov_gu[:, j].rearrange("p k n -> p (k n)"),
                                        stream[bass.ds(tile0 + j, 1)].rearrange("a p n -> (a p) n")).then_inc(S[f"ov_w{l}"], 16)
                        e.dma_start(wov_d.rearrange("p k n -> p (k n)"),
                                    stream[bass.ds(tile0 + 2, 1)].rearrange("a p n -> (a p) n")).then_inc(S[f"ov_w{l}"], 16)
                with e.Fori(0, 3 * NE // RING - 1) as i:
                    for j in range(RING):
                        q = b + j
                        at = e.snap(i * RING + q)
                        e.wait_ge(free[q % RING], q // RING + i)
                        e.dma_start(ring[:, q % RING, :], stream[bass.ds(at, 1)].rearrange("a p n -> (a p) n")
                                    ).then_inc(full[q % RING], 16)
                if l + 1 < DEPTH:
                    for q in range(base(l + 1), base(l + 1) + AHEAD):
                        load(q)
                for i in range(2):
                    e.wait_ge(yfree[i], 16 * (NE // 2) * (l + 1))
                for t in range(NT):
                    for k in range(2):
                        e.dma_start(yk[k][:, t, :], yk_dram[k * NTOK + t * P:k * NTOK + (t + 1) * P, :]
                                    ).then_inc(yld[t], 16)
            for t in range(NT):
                e.wait_ge(S["x_rdy"], NT * (DEPTH - 1) + t + 1)
                e.dma_start(y_out[:, t, :], X[:, t, :]).then_inc(S["out_st"], 16)
            e.wait_ge(S["out_st"], 16 * NT)

        @block.gpsimd
        def _(e):
            bar = Bars(e)
            c = S["cst"]
            for m in (ident, triF, triB, triS, ones, ident16):
                e.memset(m[:], 0.0 if m in (ident, ident16) else 1.0).then_inc(c, 1)
            e.memset(negF[:], 0.0).then_inc(c, 1)
            e.memset(negB[:], 0.0).then_inc(c, 1)
            e.iota(iota[:], [[1, P]], base=0, channel_multiplier=0, allow_small_or_imprecise_dtypes=True).then_inc(c, 1)
            e.iota(rowno[:], [[NTOK, 2], [P, NT]], base=1, channel_multiplier=1, allow_small_or_imprecise_dtypes=True).then_inc(c, 1)
            e.wait_ge(c, 10)
            for m in (ident, ident16):
                e.affine_select(out=m[:], in_=m[:], compare_op=ALU.not_equal, fill=1.0, base=0,
                                pattern=[[-1, P]], channel_multiplier=1).then_inc(c, 1)
            e.affine_select(out=triF[:], in_=triF[:], compare_op=ALU.is_ge, fill=0.0, base=0,
                            pattern=[[1, P]], channel_multiplier=-1).then_inc(c, 1)
            e.affine_select(out=triB[:], in_=triB[:], compare_op=ALU.is_ge, fill=0.0, base=0,
                            pattern=[[-1, P]], channel_multiplier=1).then_inc(c, 1)
            e.affine_select(out=triS[:], in_=triS[:], compare_op=ALU.is_gt, fill=0.0, base=0,
                            pattern=[[1, P]], channel_multiplier=-1).then_inc(c, 1)
            e.affine_select(out=negF[:], in_=negF[:], compare_op=ALU.is_ge, fill=-BIG, base=0,
                            pattern=[[1, P]], channel_multiplier=-1).then_inc(c, 1)
            e.affine_select(out=negB[:], in_=negB[:], compare_op=ALU.is_ge, fill=-BIG, base=0,
                            pattern=[[-1, P]], channel_multiplier=1).then_inc(c, 1)
            bar()
            e.wait_ge(S["mod_sb"], MOD0 // 2)
            e.dma_start(mod_flat[:, 0:2 * D], mrow).then_inc(S["mod_st"], 16)
            e.wait_ge(S["mod_st"], 16)

            def layer_vectors(l):
                e.dma_start(prm[:], par[l]).then_inc(S["ld_par"], 16)
                for cc in range(2):
                    for j in range(2):
                        e.dma_start(modc[:, cc, j, :], mod_dram[cc, l, j * D:(j + 1) * D].rearrange("(p k) -> p k", p=P)
                                    ).then_inc(S["ld_modc"], 16)

            def mod_at(l, part, tiles):
                at = l * 6 * D + (2 if part == 0 else 5) * D
                return slice(at, at + 256 * tiles), slice(0, 256 * tiles)

            def biases(l, part, tiles):
                src, dst = mod_at(l, part, tiles)
                e.dma_start(frow[:, dst], modb_flat[:, src]).then_inc(S["ld_modb"], 16)

            def rows_out(l, part, tiles):
                dst, src = mod_at(l, part, tiles)
                e.wait_ge(S["fill_sb"], mod_chunks(l, part) + tiles // 2)
                e.dma_start(mod_flat[:, dst], frow[:, src]).then_inc(S["mod_st"], 16)
                e.wait_ge(S["mod_st"], 16 * (2 * l + part + 2))

            layer_vectors(0)
            for l in range(DEPTH):
                for v, h in ((xp, XPAD), (gp, GPAD)):
                    for a in (0, h + CTX, 2 * h + NTOK):
                        e.memset(v[:, :, a:a + h], 0.0)
                e.drain().then_inc(S["pads"], 1)
                e.wait_ge(S["qk_rdy"], 2 * l + 1)
                e.dma_start(k_out[l], qkv[:, 0, 256:384]).then_inc(S["kv_st"], 16)
                e.dma_start(v_out[l], qkv[:, 0, 384:512]).then_inc(S["kv_st"], 16)
                e.wait_ge(S["kv_st"], 32 * (l + 1))
                bar()
                e.wait_ge(S["st_rdy"], l + 1)
                e.dma_start(st_out[l], stc).then_inc(S["st_st"], 16)
                e.wait_ge(S["st_st"], 16 * (l + 1))
                bar()
                biases(l, 0, MODC)
                rows_out(l, 0, MODC)
                for cc in range(2):
                    e.dma_start(RA[:, cc, :], mod_dram[cc:cc + 1, l, 2 * D:3 * D].to_broadcast((P, D))
                                ).then_inc(S["ld_g1"], 16)
                for cc in range(2):
                    for j, dst in ((3, RB), (4, RC)):
                        e.dma_start(dst[:, cc, :], mod_dram[cc:cc + 1, l, j * D:(j + 1) * D].to_broadcast((P, D))
                                    ).then_inc(S["ld_rows"], 16)
                e.dma_start(nrow2, n2row[l:l + 1].to_broadcast((P, D))).then_inc(S["ld_rows"], 16)
                e.memset(xg, 0.0)
                for t in range(NT):
                    e.wait_ge(S["h2_rdy"], NT * l + t + 1)
                    e.dma_start(h2_dram[t * P:(t + 1) * P, :], CAT[:, t, :]).then_inc(S["h2_st"], 16)
                biases(l, 1, modd(l))
                e.wait_ge(S["h2_st"], 16 * NT * (l + 1))
                e.wait_ge(S["gidx_rdy"], l + 1)
                bar()
                e.drain().then_inc(S["ov_go"], 1)
                some = e.value_load(ovn[0:1, 0:1], min_val=0, max_val=NOVF)
                with e.If(some > 0):
                    with e.Fori(0, NOVF) as i:
                        n = i
                        e.tensor_copy(gcur[:], gidx[:, bass.ds(i + NE, 1)])
                        e.tensor_copy(scur[:], slots[:, bass.ds(i + NE, 1)])
                        e.drain()
                        e.indirect_dma_start(xg[:, 0, :], None, h2_dram, bass.IndirectOffsetOnAxis(gcur[:, 0:1], 0),
                                             bounds_check=NTOK - 1, oob_is_err=False).then_inc(S[f"ov_gather{l}"], 16)
                        e.wait_ge(S[f"ov_y{l}"], n + 2)
                        e.sem_inc(S[f"ov_seen{l}"], 1)
                        e.indirect_dma_start(yk_dram, bass.IndirectOffsetOnAxis(scur[:, 0:1], 0), yb[:, 0, :], None,
                                             bounds_check=2 * NTOK - 1, oob_is_err=False).then_inc(S[f"ov_scatter{l}"], 16)
                        e.wait_ge(S[f"ov_scatter{l}"], 16 * (n + 1))
                def gather(n, p):
                    e.tensor_copy(gcur2[:, p:p + 1], gidx[:, n:n + 1] if isinstance(n, int) else gidx[:, bass.ds(n, 1)]
                                  ).then_inc(S["gather_rows"], 1)
                    e.wait_ge(S["gather_rows"], n + (32 * l + 1))
                    e.sem_inc(S["seen"], 1)
                    e.indirect_dma_start(xg[:, p, :], None, h2_dram, bass.IndirectOffsetOnAxis(gcur2[:, p:p + 1], 0),
                                         bounds_check=NTOK - 1, oob_is_err=False).then_inc(gfull[p], 16)

                def pair(i, more=2):
                    for p in range(2):
                        n = 2 * i + p
                        if p < more:
                            e.wait_ge(S["xgT_ps"], n + (32 * l + 2))
                            e.sem_inc(S["seen"], 1)
                            gather(n + 3, 1 - p)
                        e.wait_ge(S["y2_sb_a"], n + (32 * l + 1))
                        e.sem_inc(S["seen"], 1)
                        e.wait_ge(S["y2_sb_d"], n + (32 * l + 1))
                        e.sem_inc(S["seen"], 1)
                        e.tensor_copy(scur2[:, p:p + 1], slots[:, n:n + 1] if isinstance(n, int) else slots[:, bass.ds(n, 1)]
                                      ).then_inc(S["scatter_rows"], 1)
                        e.wait_ge(S["scatter_rows"], n + (32 * l + 1))
                        e.sem_inc(S["seen"], 1)
                        e.indirect_dma_start(yk_dram, bass.IndirectOffsetOnAxis(scur2[:, p:p + 1], 0), yb[:, p, :], None,
                                             bounds_check=2 * NTOK - 1, oob_is_err=False).then_inc(yfree[p], 16)

                gather(0, 0)
                gather(1, 1)
                rows_out(l, 1, modd(l))
                for cc in range(2):
                    e.dma_start(RA[:, cc, :], mod_dram[cc:cc + 1, l, 5 * D:6 * D].to_broadcast((P, D))
                                ).then_inc(S["ld_g2"], 16)
                if l + 1 < DEPTH:
                    layer_vectors(l + 1)
                e.wait_ge(S["xgT_ps"], 32 * l + 1)
                gather(2, 0)
                pair(0)
                with e.Fori(1, NE // 2 - 2) as i:
                    pair(i)
                pair(NE // 2 - 2, 1)
                pair(NE // 2 - 1, 0)
                bar()

        @block.scalar
        def _(e):
            bar = Bars(e)
            A = e.activation
            e.wait_ge(S["ld_cond"], 16)
            A(condT[:], condT[:], ACT.Silu).then_inc(S["silu_c"], 1)
            bar()

            for l in range(DEPTH):
                e.sem_inc(S[f"ov_y{l}"], 1)
            for l in range(DEPTH):
                for t in range(NT):
                    e.wait_ge(S["xT_ps"], NT * l + t + 1)
                    if t == 0:
                        e.wait_ge(S["m_rdy"], l + 1)
                    for k in range(4):
                        ins = A(HT[:, k, t * P:(t + 1) * P], PS[2 * (t % 2)][:, k * P:(k + 1) * P], ACT.Identity,
                                scale=modc[:, cnd(t), 1, k:k + 1], bias=modc[:, cnd(t), 0, k:k + 1])
                    ins.then_inc(S["hT_a"], 1)
                for n in (0, 1, 4, 5, 6, 7, 8, 9):
                    e.wait_ge(S["ch_ps"], 10 * l + n + 1)
                    a, b = PS[2 * (n % 2)], PS[2 * (n % 2) + 1]
                    if n < 2:
                        A(sg[:, n, CTX:NTOK], a[:], ACT.Sigmoid)
                        ins = A(sg[:, n, 0:CTX], b[:, 0:CTX], ACT.Sigmoid)
                    else:
                        A(xp[:, n - 4, 2 * XPAD + CTX:2 * XPAD + NTOK], a[:], ACT.Copy)
                        ins = A(xp[:, n - 4, XPAD:XPAD + CTX], b[:, 0:CTX], ACT.Copy)
                    ins.then_inc(S["ch_sb"], 1)
                dtr = small(0, NT, 8)
                for n in range(15):
                    if n == 10:
                        for j in range(6):
                            e.wait_ge(S["conv_rdy"], 6 * l + j + 1)
                            A(cv[:, j, :], cv[:, j, :], ACT.Silu).then_inc(S["convs_rdy"], 1)
                        e.wait_ge(S["dt_x"], l + 1)
                        A(small(220, 80), small(140, 80), ACT.Exp, scale=-1.0)
                        A(small(300, 16), pr("alog"), ACT.Exp).then_inc(S["dt_e"], 1)
                    e.wait_ge(S["pj_ps"], 15 * l + n + 1)
                    t, b = n % NT, PS[4 + n % 2]
                    if n < 5:
                        ins = A(dtr[:, t, :], b[:, 0:8], ACT.Copy)
                    elif n < 10:
                        ins = A(qkv[:, t, :], b[:], ACT.Copy)
                    else:
                        ins = A(CAT[:, t, 256:768], b[:], ACT.Silu)
                    ins.then_inc(S["pj_sb"], 1)
                for n in range(7):
                    e.wait_ge(S["xt_ps"], 7 * l + n + 1)
                    b = PS[n % 2]
                    if n < 5:
                        ins = A(xs[:, n, :], b[:], ACT.Copy)
                    elif n == 5:
                        ins = A(btok[:, 0:4, :], b[:].rearrange("p (a b) -> p a b", a=4), ACT.Copy)
                    else:
                        ins = A(btok[:, 4, :], b[:, 0:P], ACT.Copy)
                    ins.then_inc(S["xt_sb"], 1)
                for t in range(NT):
                    e.wait_ge(S["qkT_ps"], NT * l + t + 1)
                    A(qkT[:, :, t * P:(t + 1) * P], PS[2 + t % 2][:, 0:384].rearrange("p (a b) -> p a b", a=3), ACT.Copy
                      ).then_inc(S["qkT_sb"], 1)
                e.wait_ge(S["cat_a"], l + 1)
                A(CAT[:, :, 768:1024], CAT[:, :, 768:1024], ACT.Silu).then_inc(S["cat_b"], 1)
                e.wait_ge(S["cum_sb"], l + 1)
                A(small(700, 240), small(460, 240), ACT.Exp).then_inc(S["dec_rdy"], 1)
                nm, es, sums = small(44, NT, QH), small(64, NT, QH), small(84, NT, QH)
                for t in range(NT):
                    w = P if t == 0 else P * (1 + len(near(t)))
                    e.wait_ge(S["att_m"], NT * l + t + 1)
                    for h in range(QH):
                        if t:
                            e.wait_ge(S["att_pt"], 20 * l + 4 * (t - 1) + h + 1)
                        A(Pm[:, h, 0:w], PS[h][:, 0:w], ACT.Exp, bias=nm[:, t, h:h + 1], accum_out=sums[:, t, h:h + 1]
                          ).then_inc(S["att_exp"], 1)
                    A(es[:, t, :], es[:, t, :], ACT.Exp).then_inc(S["att_es"], 1)
                    for h in (0, 2):
                        n = 4 * t + h
                        e.wait_ge(S["att_pt"], 20 * l + n + 1)
                        if n >= 2:
                            e.wait_ge(S["att_pv"], 20 * l + n - 1)
                        A(PTs[:, 0, :, :].rearrange("p a b -> p (a b)")[:, 0:w], PS[4][:, 0:w], ACT.Copy).then_inc(S["ptc_a"], 1)
                bar()
                ncum = small(380, 2, NT, 8)
                for c in range(NT):
                    e.wait_ge(S["gt_ps"], NT * l + c + 1)
                    if c:
                        e.wait_ge(S["w_rdy"], 20 * l + 4 * c)
                    A(gts[:, 0], PS[6][:, 0:P], ACT.Copy)
                    A(gts[:, 1], PS[7][:, 0:P], ACT.Copy).then_inc(S["gt_sb"], 1)
                    for u in range(4):
                        d, g = u // 2, u % 2
                        e.wait_ge(S["r_ps"], 20 * l + 4 * c + u + 1)
                        if c and u == 0:
                            e.wait_ge(S["y_ps"], NT * l + c)
                        for j in range(4):
                            ins = A(LW[:, u, j, :], PS[u][:, j * P:(j + 1) * P], ACT.Exp, bias=ncum[:, d, c, 4 * g + j:4 * g + j + 1])
                        ins.then_inc(S["l_rdy"], 1)
                bar()
                for t in range(NT):
                    e.wait_ge(S["ct_ps"], NT * l + t + 1)
                    A(HT[:, 0:4, t * P:(t + 1) * P], PS[2 * (t % 2)][:].rearrange("p (a b) -> p a b", a=4), ACT.Copy
                      ).then_inc(S["ct_sb_a"], 1)
                for n in range(2 * NT):
                    t, hf = n % NT, n // NT
                    e.wait_ge(S["x_added"], 10 * l + n + 1)
                    A(view(TMP + 1024, 512), X[:, t, 512 * hf:512 * hf + 512], ACT.Square, accum_out=small(1600 + n, 1))
                    e.drain()
                e.drain().then_inc(S["sq_rdy"], 1)
                for t in range(NT):
                    e.wait_ge(S["h2T_ps"], NT * l + t + 1)
                    A(HT[:, 0:4, t * P:(t + 1) * P], PS[2 * (t % 2)][:].rearrange("p (a b) -> p a b", a=4), ACT.Copy
                      ).then_inc(S["h2T_a"], 1)
                e.wait_ge(S["ge_x"], l + 1)
                A(small(1200, NT, NG), small(1200, NT, NG), ACT.Exp).then_inc(S["ge_y"], 1)
                e.wait_ge(S["te_x"], l + 1)
                A(small(1220, NT), small(1220, NT), ACT.Exp).then_inc(S["te_y"], 1)
                bar()
                some = e.value_load(ovn[0:1, 0:1], min_val=0, max_val=NOVF)
                with e.If(some > 0):
                    with e.Fori(0, NOVF) as i:
                        n = i
                        e.wait_ge(S[f"ov_pe{l}"], 4 * n + 2)
                        for j in range(2):
                            ins = A(xgT[:, 0, 4 * j:4 * j + 4, :], PS[j][:].rearrange("p (a b) -> p a b", a=4), ACT.Copy)
                        ins.then_inc(S[f"ov_x{l}"], 1)
                        e.wait_ge(S[f"ov_pe{l}"], 4 * n + 3)
                        A(sgate[:, 0, :], PS[2][:, 0:FF], ACT.Silu).then_inc(S[f"ov_gate{l}"], 1)
                        e.wait_ge(S[f"ov_pe{l}"], 4 * n + 5)
                        for j in range(2):
                            ins = A(yb[:, 0, 512 * j:512 * j + 512], PS[5 + j][:], ACT.Copy)
                        ins.then_inc(S[f"ov_y{l}"], 1)

                def rows_in(i, p):
                    m = 2 * i + (32 * l + p)
                    e.wait_ge(S["xgT_ps"], m + 1)
                    if not isinstance(i, int) or i:
                        e.wait_ge(S["gu_ps"], m - 1)
                    A(xgT[:, p, 0:4, :], PS[0][:].rearrange("p (a b) -> p a b", a=4), ACT.Copy).then_inc(S["xgT_sb"], 1)

                def gate(i, p):
                    m = 2 * i + (32 * l + p)
                    e.wait_ge(S["gu_ps"], m + 1)
                    if not isinstance(i, int) or i:
                        e.wait_ge(S["hh_rdy"], m - 1)
                    A(sgate[:, p, :], PS[2 + p][:, 0:FF], ACT.Silu).then_inc(S["sgate_rdy"], 1)

                def result(i, p):
                    m = 2 * i + (32 * l + p)
                    e.wait_ge(S["y2_ps"], m + 1)
                    if not isinstance(i, int) or i:
                        e.wait_ge(yfree[p], 16 * i + 16 * (NE // 2) * l)
                    A(yb[:, p, 0:512], PS[5][:], ACT.Copy).then_inc(S["y2_sb_a"], 1)

                def pair(i, last=False):
                    gate(i, 1)
                    if not last:
                        rows_in(i + 1, 0)
                    result(i, 0)
                    if not last:
                        gate(i + 1, 0)
                        rows_in(i + 1, 1)
                    result(i, 1)

                rows_in(0, 0)
                gate(0, 0)
                rows_in(0, 1)
                pair(0)
                with e.Fori(1, NE // 2 - 1) as i:
                    pair(i)
                pair(NE // 2 - 1, True)
                def squares(t):
                    if l + 1 < DEPTH:
                        e.wait_ge(S["x_rdy"], NT * l + t + 1)
                        A(nrow2, X[:, t, :], ACT.Square, accum_out=small(1400 + t, 1))
                        e.drain()

                for t in range(NT):
                    e.wait_ge(yld[t], 32 * (l + 1))
                    if t >= 2:
                        e.wait_ge(S["x_rdy"], NT * l + t - 1)
                    A(mt[:, t % 2, :], yk[0][:, t, :], ACT.Copy, scale=small(1235, NT)[:, t:t + 1]).then_inc(S["y_half"], 1)
                    if t:
                        squares(t - 1)
                squares(NT - 1)
                bar()

        @block.vector
        def _(e):
            bar = Bars(e)
            dr = e.drain

            def rsqrt(v, a, y, yi, vi):
                e.tensor_scalar(yi, vi, 1, None, ALU.logical_shift_right); dr()
                e.tensor_scalar(yi, yi, -1.0, 1597463007.0, ALU.mult, ALU.add); dr()
                for _ in range(3):
                    e.tensor_tensor(a, y, y, ALU.mult); dr()
                    e.scalar_tensor_tensor(out=a, in0=a, scalar=-0.5, in1=v, op0=ALU.mult, op1=ALU.mult); dr()
                    e.scalar_tensor_tensor(out=y, in0=a, scalar=1.5, in1=y, op0=ALU.add, op1=ALU.mult); dr()

            def rs(n, scale, vo=1400):
                v, a, y = small(vo, n), small(vo + 50, n), small(vo + 100, n)
                e.tensor_scalar(v, v, scale, EPS, ALU.mult, ALU.add); dr()
                rsqrt(v, a, y, y.bitcast(I32), v.bitcast(I32))
                return y

            e.wait_ge(S["ld0"], 48)
            for t in range(NT):
                e.tensor_tensor_reduce(sqs, X[:, t, :], X[:, t, :], 1.0, 0.0, ALU.mult, ALU.add, small(1400 + t, 1))
                dr()

            def scaled(t):
                e.tensor_scalar(xn[:, t % 2, :], X[:, t, :], small(1500, NT)[:, t:t + 1], None, ALU.mult).then_inc(S["xn_ready"], 1)

            def modulation(l, part, n, j):
                e.wait_ge(S["ld_modb"], 16 * (2 * l + part + 1))
                e.wait_ge(S["fill_ps"], mod_chunks(l, part) + n + 1)
                m = frow[:, 512 * j:512 * j + 512]
                e.tensor_tensor(m, PS[MODBANK[part][j]][0:2, :], m, ALU.add).then_inc(S["fill_sb"], 1)

            rs(NT, 1.0 / D)
            scaled(0)
            scaled(1)
            for n in range(MOD0 // 2):
                e.wait_ge(S["mod_ps"], n + 1)
                m = mrow[:, n * 512:(n + 1) * 512]
                e.tensor_tensor(m, PS[n % 2][0:2, :], m, ALU.add).then_inc(S["mod_sb"], 1)
            bar()
            for l in range(DEPTH):
                if l:
                    rs(NT, 1.0 / D)
                    scaled(0)
                    scaled(1)
                e.wait_ge(S["ld_par"], 16 * (l + 1))
                e.wait_ge(S["ld_modc"], 64 * (l + 1))
                for cc in range(2):
                    ins = e.scalar_tensor_tensor(out=modc[:, cc, 1, :], in0=modc[:, cc, 1, :], scalar=1.0, in1=pr("norm1"),
                                                 op0=ALU.add, op1=ALU.mult)
                dr()
                e.drain().then_inc(S["m_rdy"], 1)

                def evac1(t):
                    e.wait_ge(S["xT_ps"], NT * l + t + 1)
                    for k in range(4):
                        ins = e.tensor_scalar(HT[:, 4 + k, t * P:(t + 1) * P], PS[2 * (t % 2) + 1][:, k * P:(k + 1) * P],
                                              modc[:, cnd(t), 1, 4 + k:5 + k], modc[:, cnd(t), 0, 4 + k:5 + k], ALU.mult, ALU.add)
                    ins.then_inc(S["hT_d"], 1)

                for t in range(NT):
                    evac1(t)
                    if t + 2 < NT:
                        scaled(t + 2)
                for j in range(2):
                    e.wait_ge(S["ch_sb"], 8 * l + j + 1)
                    n = 2 + j
                    e.wait_ge(S["ch_ps"], 10 * l + n + 1)
                    a, b = PS[2 * (n % 2)], PS[2 * (n % 2) + 1]
                    e.tensor_tensor(gp[:, j, 2 * GPAD + CTX:2 * GPAD + NTOK], a[:], sg[:, j, CTX:NTOK], ALU.mult)
                    e.tensor_tensor(gp[:, j, GPAD:GPAD + CTX], b[:, 0:CTX], sg[:, j, 0:CTX], ALU.mult).then_inc(S["ch_a"], 1)
                dr()
                e.wait_ge(S["pads"], l + 1)
                gw, gb = pr("gw", 2, 31), pr("gb")
                for ct in range(2):
                    e.tensor_scalar(uc[:, ct, :], gp[:, ct, 0:GOUT], gw[:, ct, 0:1], gb[:, ct:ct + 1], ALU.mult, ALU.add); dr()
                    for k in range(1, 31):
                        ins = e.scalar_tensor_tensor(out=uc[:, ct, :], in0=gp[:, ct, k:k + GOUT], scalar=gw[:, ct, k:k + 1],
                                                     in1=uc[:, ct, :], op0=ALU.mult, op1=ALU.add)
                        if k < 30:
                            dr()
                    ins.then_inc(S["uconv"], 1)
                cw, cb = pr("cw", 6, 5), pr("cb")
                for n in range(6):
                    e.wait_ge(S["ch_sb"], 8 * l + 3 + n)
                    e.tensor_scalar(cv[:, n, :], xp[:, n, 0:XOUT], cw[:, n, 0:1], cb[:, n:n + 1], ALU.mult, ALU.add); dr()
                    for k in range(1, 5):
                        ins = e.scalar_tensor_tensor(out=cv[:, n, :], in0=xp[:, n, k:k + XOUT], scalar=cw[:, n, k:k + 1],
                                                     in1=cv[:, n, :], op0=ALU.mult, op1=ALU.add)
                        if k < 4:
                            dr()
                    ins.then_inc(S["conv_rdy"], 1)
                e.wait_ge(S["pj_sb"], 15 * l + 5)
                xdir, ax, ee = small(1240, 80), small(140, 80), small(220, 80)
                x4 = small(1240, 2, NT, 8)
                dtr = small(0, NT, 8)
                for d in range(2):
                    e.tensor_tensor(x4[:, d], dtr, pr("dtb")[:, 8 * d:8 * d + 8].unsqueeze(1).to_broadcast((P, NT, 8)), ALU.add)
                dr()
                e.tensor_scalar(ax, xdir, -1.0, None, ALU.mult); dr()
                e.tensor_tensor(ax, ax, xdir, ALU.max).then_inc(S["dt_x"], 1)
                e.tensor_scalar(xdir, xdir, 0.0, None, ALU.max)
                e.wait_ge(S["pj_sb"], 15 * l + 10)
                qk = qkv[:, :, 0:384]
                e.tensor_tensor(t1, qk, qk, ALU.mult); dr()
                e.tensor_reduce(small(1400, 30), t1.rearrange("p t (h d) -> p (t h) d", d=HD), AX, ALU.add); dr()
                y = rs(30, 1.0 / HD)
                for t in range(NT):
                    yt = y[:, 6 * t:6 * t + 6].unsqueeze(2).to_broadcast((P, 6, HD))
                    e.tensor_tensor(t1[:, t, :].rearrange("p (h d) -> p h d", d=HD), qkv[:, t, 0:384].rearrange("p (h d) -> p h d", d=HD),
                                    yt, ALU.mult)
                dr()
                for t in range(NT):
                    for g in range(2):
                        e.scalar_tensor_tensor(out=qkv[:, t, 128 * g:128 * g + 128].rearrange("p (k d) -> p k d", k=2),
                                               in0=t1[:, t, 0:256].rearrange("p (k g d) -> p g k d", g=2, d=HD)[:, g],
                                               scalar=HD ** -0.5,
                                               in1=pr("qw").unsqueeze(1).to_broadcast((P, 2, HD)), op0=ALU.mult, op1=ALU.mult)
                    e.tensor_tensor(qkv[:, t, 256:384].rearrange("p (k d) -> p k d", k=2),
                                    t1[:, t, 256:384].rearrange("p (k d) -> p k d", k=2),
                                    pr("kw").unsqueeze(1).to_broadcast((P, 2, HD)), ALU.mult)
                dr()
                e.drain().then_inc(S["qk_rdy"], 1)
                for t in range(1, NT):
                    q6 = qkv[:, t, 0:384].rearrange("p (h d) -> p h d", d=HD)
                    e.tensor_tensor(t1[:, t, :].rearrange("p (h d) -> p h d", d=HD), q6,
                                    ropeT[:, 0, t - 1, :].unsqueeze(1).to_broadcast((P, 6, HD)), ALU.mult)
                    halves = "p (h a b f) -> p b h a f"
                    qh = qkv[:, t, 0:384].rearrange(halves, a=2, b=2, f=16)
                    th = t2[:, t - 1, :].rearrange(halves, a=2, b=2, f=16)
                    sn = ropeT[:, 1, t - 1, :].rearrange("p (a b f) -> p b a f", b=2, f=16)
                    for b in range(2):
                        e.tensor_tensor(th[:, b], qh[:, 1 - b], sn[:, b].unsqueeze(1).to_broadcast((P, 6, 2, 16)), ALU.mult)
                dr()
                e.tensor_tensor(qkv[:, 1:NT, 0:384], t1[:, 1:NT, :], t2, ALU.add).then_inc(S["qk_rdy"], 1)

                e.wait_ge(S["dt_e"], l + 1)
                dr()
                s_, z_, p_ = small(940, 80), small(1020, 80), small(1100, 80)
                e.tensor_scalar(s_, ee, 2.0, None, ALU.add); dr()
                e.reciprocal(s_, s_); dr()
                e.tensor_tensor(s_, s_, ee, ALU.mult); dr()
                e.tensor_tensor(z_, s_, s_, ALU.mult); dr()
                e.tensor_scalar(p_, z_, 1.0 / 17, None, ALU.mult); dr()
                for k in (15, 13, 11, 9, 7, 5, 3):
                    e.scalar_tensor_tensor(out=p_, in0=p_, scalar=1.0 / k, in1=z_, op0=ALU.add, op1=ALU.mult); dr()
                e.scalar_tensor_tensor(out=p_, in0=p_, scalar=1.0, in1=s_, op0=ALU.add, op1=ALU.mult); dr()
                dt, la = small(1320, 80), small(1020, 80)
                e.scalar_tensor_tensor(out=dt, in0=p_, scalar=2.0, in1=xdir, op0=ALU.mult, op1=ALU.add); dr()
                dt4, la4 = small(1320, 2, NT, 8), small(1020, 2, NT, 8)
                for d in range(2):
                    ins = e.scalar_tensor_tensor(out=la4[:, d], in0=dt4[:, d], scalar=-1.0,
                                                 in1=small(300, 2, 8)[:, d].unsqueeze(1).to_broadcast((P, NT, 8)),
                                                 op0=ALU.mult, op1=ALU.mult)
                ins.then_inc(S["la_rdy"], 1)
                for j in range(3):
                    e.wait_ge(S["ut_ps"], 3 * l + j + 1)
                    w = min(2, NT - 2 * j)
                    e.tensor_copy(CAT[:, 2 * j:2 * j + w, 768:1024], PS[j][:, 0:256 * w].rearrange("p (t c) -> p t c", t=w)
                                  ).then_inc(S["ut_sb"], 1)
                dr()
                lt = view(TMP, NT, 256)
                cu = CAT[:, :, 768:1024]
                mean = small(1200, NT, 4)
                for t in range(NT):
                    e.tensor_reduce(mean[:, t, :], CAT[:, t, 768:1024].rearrange("p (g d) -> p g d", d=HD), AX, ALU.add)
                dr()
                for t in range(NT):
                    c4 = CAT[:, t, 768:1024].rearrange("p (g d) -> p g d", d=HD)
                    e.scalar_tensor_tensor(out=c4, in0=mean[:, t, :].unsqueeze(2).to_broadcast((P, 4, HD)), scalar=-1.0 / HD, in1=c4,
                                           op0=ALU.mult, op1=ALU.add)
                dr()
                e.tensor_tensor(lt, cu, cu, ALU.mult); dr()
                e.tensor_reduce(small(1400, 20), lt.rearrange("p t (g d) -> p (t g) d", d=HD), AX, ALU.add); dr()
                y = rs(20, 1.0 / HD)
                for t in range(NT):
                    c4 = CAT[:, t, 768:1024].rearrange("p (g d) -> p g d", d=HD)
                    e.tensor_tensor(c4, c4, y[:, 4 * t:4 * t + 4].unsqueeze(2).to_broadcast((P, 4, HD)), ALU.mult)
                dr()
                e.tensor_tensor(cu, cu, pr("lnw").unsqueeze(1).to_broadcast((P, NT, 256)), ALU.mult); dr()
                e.tensor_tensor(cu, cu, pr("lnb").unsqueeze(1).to_broadcast((P, NT, 256)), ALU.add).then_inc(S["cat_a"], 1)
                e.wait_ge(S["cum_ps"], l + 1)
                e.tensor_copy(small(460, 160), PS[7][:, 0:160]); dr()
                e.tensor_scalar(small(380, 80), small(460, 80), -1.0, None, ALU.mult)
                e.tensor_tensor(small(620, 80), small(540, 80), small(460, 80), ALU.subtract).then_inc(S["cum_sb"], 1)

                mx, nm, es, sums, den = small(40, QH), small(44, NT, QH), small(64, NT, QH), small(84, NT, QH), small(104, QH)

                def att_max(t):
                    w = P if t == 0 else P * (1 + len(near(t)))
                    for h in range(QH):
                        e.wait_ge(S["att_s"], 20 * l + 4 * t + h + 1)
                        e.tensor_reduce(mx[:, h:h + 1], PS[h][:, 0:w], AX, ALU.max)
                    dr()
                    e.tensor_tensor(mx, mx, pr("sink"), ALU.max); dr()
                    e.tensor_scalar(nm[:, t, :], mx, -1.0, None, ALU.mult); dr()
                    e.tensor_tensor(es[:, t, :], nm[:, t, :], pr("sink"), ALU.add).then_inc(S["att_m"], 1)
                    dr()

                att_max(0)
                for t in range(NT):
                    if t + 1 < NT:
                        att_max(t + 1)
                    w = P if t == 0 else P * (1 + len(near(t)))
                    for h in (1, 3):
                        n = 4 * t + h
                        e.wait_ge(S["att_pt"], 20 * l + n + 1)
                        if n >= 2:
                            e.wait_ge(S["att_pv"], 20 * l + n - 1)
                        e.tensor_copy(PTs[:, 1, :, :].rearrange("p a b -> p (a b)")[:, 0:w], PS[5][:, 0:w]).then_inc(S["ptc_d"], 1)
                    e.wait_ge(S["att_es"], NT * l + t + 1)
                    e.tensor_tensor(den, sums[:, t, :], es[:, t, :], ALU.add); dr()
                    e.reciprocal(den, den); dr()
                    e.wait_ge(S["att_pv"], 20 * l + 4 * t + 4)
                    e.tensor_tensor(CAT[:, t, 0:256].rearrange("p (h d) -> p h d", d=HD),
                                    PS[6 + t % 2][:, 0:256].rearrange("p (h d) -> p h d", d=HD),
                                    den.unsqueeze(2).to_broadcast((P, QH, HD)), ALU.mult).then_inc(S["att_o"], 1)
                    dr()
                bar()
                e.wait_ge(S["dec_rdy"], l + 1)
                dec, cd, dte = small(700, 2, NT, 8), small(780, 2, NT, 8), small(860, 2, NT, 8)
                dsum = small(320, 8)
                e.tensor_tensor(dsum, pr("dskip")[:, 0:8], pr("dskip")[:, 8:16], ALU.add)
                e.tensor_copy(hs[:, 0, 0, :], pr("h0")[:, 0:256])
                e.tensor_copy(hs[:, 1, NLT - 1, :], pr("h0")[:, 256:512])
                dr()

                def h3(a, n=8):
                    return a.rearrange("p (h d) -> p h d", d=HD)

                def decayed(out, src, d, c):
                    for g in range(2):
                        r = slice(64 * g, 64 * g + 64)
                        e.tensor_tensor(h3(out[r]), h3(src[r]),
                                        cd[r, d, c, 4 * g:4 * g + 4].unsqueeze(2).to_broadcast((64, 4, HD)), ALU.mult)

                for c in range(NT):
                    if c:
                        e.wait_ge(S["s_ps"], NT * l + c)
                    for d in range(2):
                        e.tensor_tensor(h3(xdt[:, d, :]), h3(xs[:, c, :]), dt4[:, d, c, :].unsqueeze(2).to_broadcast((P, 8, HD)), ALU.mult)
                    dr()
                    for d in range(2):
                        ins = e.tensor_tensor(h3(xw[:, d, :]), h3(xdt[:, d, :]), dte[:, d, c, :].unsqueeze(2).to_broadcast((P, 8, HD)), ALU.mult)
                    ins.then_inc(S["xd_rdy"], 1)
                    e.tensor_tensor(h3(xs[:, c, :]), h3(xs[:, c, :]), dsum.unsqueeze(2).to_broadcast((P, 8, HD)), ALU.mult)
                    e.wait_ge(S["gt_sb"], NT * l + c + 1)
                    for u in range(4):
                        e.wait_ge(S["l_rdy"], 20 * l + 4 * c + u + 1)
                        e.tensor_tensor(LW[:, u], LW[:, u], gts[:, u % 2].unsqueeze(1).to_broadcast((P, 4, P)), ALU.mult
                                        ).then_inc(S["w_rdy"], 1)
                    e.wait_ge(S["s_ps"], NT * l + c + 1)
                    sp = PS[5]
                    if c == 0:
                        e.tensor_copy(stc.rearrange("p a b -> p (a b)"), sp[:]).then_inc(S["st_rdy"], 1)
                    else:
                        i = c - 1
                        if i < NLT - 1:
                            decayed(hsc, hs[:, 0, i, :], 0, c); dr()
                            e.tensor_tensor(hs[:, 0, i + 1, :], sp[:, 0:256], hsc, ALU.add)
                        if i:
                            e.tensor_copy(hs[:, 1, i - 1, :], sp[:, 256:512])
                    dr()
                    e.tensor_tensor(xs[:, c, :], PS[4][:], xs[:, c, :], ALU.add).then_inc(S["y_sb"], 1)
                for i in range(NLT - 1, 0, -1):
                    decayed(hsc, hs[:, 1, i, :], 1, i + 1); dr()
                    e.tensor_tensor(hs[:, 1, i - 1, :], hs[:, 1, i - 1, :], hsc, ALU.add); dr()
                e.drain().then_inc(S["hs_rdy"], 1)
                for i in range(NLT):
                    c = i + 1
                    e.wait_ge(S["off_ps"], NLT * l + i + 1)
                    for d, dst in ((0, off1), (1, off2)):
                        for g in range(2):
                            ins = e.tensor_tensor(h3(dst[:, 256 * g:256 * g + 256]), h3(PS[2 * (i % 2) + g][:, 256 * d:256 * d + 256]),
                                                  dec[:, d, c, 4 * g:4 * g + 4].unsqueeze(2).to_broadcast((P, 4, HD)), ALU.mult)
                    ins.then_inc(S["off_sb"], 1)
                    dr()
                    e.tensor_tensor(xs[:, c, :], xs[:, c, :], off1, ALU.add); dr()
                    e.tensor_tensor(xs[:, c, :], xs[:, c, :], off2, ALU.add); dr()
                cz = CAT[:, :, 256:768]
                e.wait_ge(S["st_st"], 16 * (l + 1))
                e.tensor_tensor(xs, xs, cz, ALU.mult); dr()
                e.tensor_tensor(big, xs, xs, ALU.mult); dr()
                e.tensor_reduce(small(1400, 10), big.rearrange("p t (g d) -> p (t g) d", d=256), AX, ALU.add); dr()
                y = rs(10, 1.0 / 256)
                for t in range(NT):
                    for g in range(2):
                        e.scalar_tensor_tensor(out=CAT[:, t, 256 + 256 * g:512 + 256 * g], in0=xs[:, t, 256 * g:256 * g + 256],
                                               scalar=y[:, 2 * t + g:2 * t + g + 1], in1=pr("snorm")[:, 256 * g:256 * g + 256],
                                               op0=ALU.mult, op1=ALU.mult)
                bar()
                late = list(enumerate(LATE))
                for n, j in late[:2]:
                    modulation(l, 0, n, j)
                for t in range(NT):
                    e.wait_ge(S["ct_ps"], NT * l + t + 1)
                    e.tensor_copy(HT[:, 4:8, t * P:(t + 1) * P], PS[2 * (t % 2) + 1][:].rearrange("p (a b) -> p a b", a=4)
                                  ).then_inc(S["ct_sb_d"], 1)
                for n, j in late[2:]:
                    modulation(l, 0, n, j)
                e.wait_ge(S["ld_g1"], 32 * (l + 1))
                for n in range(2 * NT):
                    t, hf = n % NT, n // NT
                    e.wait_ge(S["wo_ps"], 10 * l + n + 1)
                    e.tensor_tensor(wtmp[:, n % 2, :], PS[4 + n % 2][:], RA[:, cnd(t), 512 * hf:512 * hf + 512], ALU.mult
                                    ).then_inc(S["wo_sb"], 1)
                    dr()
                    e.tensor_tensor(X[:, t, 512 * hf:512 * hf + 512], X[:, t, 512 * hf:512 * hf + 512], wtmp[:, n % 2, :], ALU.add
                                    ).then_inc(S["x_added"], 1)
                    if n == 5:
                        e.wait_ge(S["ld_rows"], 80 * (l + 1))
                        for cc in range(2):
                            e.scalar_tensor_tensor(out=RC[:, cc, :], in0=RC[:, cc, :], scalar=1.0, in1=nrow2, op0=ALU.add, op1=ALU.mult)
                e.wait_ge(S["sq_rdy"], l + 1)
                e.tensor_tensor(small(1400, NT), small(1600, NT), small(1600 + NT, NT), ALU.add); dr()
                y = rs(NT, 1.0 / D)

                def evac2(t):
                    e.wait_ge(S["h2T_ps"], NT * l + t + 1)
                    e.tensor_copy(HT[:, 4:8, t * P:(t + 1) * P], PS[2 * (t % 2) + 1][:].rearrange("p (a b) -> p a b", a=4)
                                  ).then_inc(S["h2T_d"], 1)

                for t in range(NT):
                    e.scalar_tensor_tensor(out=mt[:, t % 2, :], in0=X[:, t, :], scalar=y[:, t:t + 1], in1=RC[:, cnd(t), :],
                                           op0=ALU.mult, op1=ALU.mult); dr()
                    e.tensor_tensor(CAT[:, t, :], mt[:, t % 2, :], RB[:, cnd(t), :], ALU.add).then_inc(S["h2_rdy"], 1)
                    if t:
                        evac2(t - 1)
                evac2(NT - 1)
                lg = small(0, NT, 36)
                for t in range(NT):
                    e.wait_ge(S["lg_ps"], NT * l + t + 1)
                    e.tensor_tensor(lg[:, t, :], PS[4 + t % 2][:, 0:36], pr("rb"), ALU.add).then_inc(S["lg_sb"], 1)
                dr()
                gl, el = lg[:, :, 0:NG], lg[:, :, NG:36]

                def first_max(src, n, m, i, oh, tmp):
                    io = iota[:, 0:n].unsqueeze(1).to_broadcast((P, NT, n))
                    e.tensor_reduce(m, src, AX, ALU.max); dr()
                    e.tensor_tensor(tmp, src, m.unsqueeze(2).to_broadcast((P, NT, n)), ALU.is_equal); dr()
                    e.scalar_tensor_tensor(out=tmp, in0=tmp, scalar=-64.0, in1=io, op0=ALU.mult, op1=ALU.add); dr()
                    e.tensor_reduce(i, tmp, AX, ALU.min); dr()
                    e.tensor_scalar(i, i, 64.0, None, ALU.add); dr()
                    e.tensor_tensor(oh, i.unsqueeze(2).to_broadcast((P, NT, n)), io, ALU.is_equal); dr()

                gm, gi, m1, i1, m2, i2 = (small(180 + 5 * j, NT) for j in range(6))
                goh, gt = small(210, NT, NG), small(230, NT, NG)
                o1, o2, tm, es8 = (small(250 + 40 * j, NT, EPG) for j in range(4))
                first_max(gl, NG, gm, gi, goh, gt)
                gx = small(1200, NT, NG)
                e.tensor_tensor(gx, gl, gm.unsqueeze(2).to_broadcast((P, NT, NG)), ALU.subtract).then_inc(S["ge_x"], 1)
                tm32 = small(420, NT, NG, EPG)
                for t in range(NT):
                    e.tensor_tensor(tm32[:, t], el[:, t, :].rearrange("p (g x) -> p g x", g=NG),
                                    goh[:, t, :].unsqueeze(2).to_broadcast((P, NG, EPG)), ALU.mult)
                dr()
                for t in range(NT):
                    e.tensor_reduce(es8[:, t, :], tm32[:, t].rearrange("p g x -> p x g"), AX, ALU.add)
                dr()
                first_max(es8, EPG, m1, i1, o1, tm)
                e.scalar_tensor_tensor(out=es8, in0=o1, scalar=-BIG, in1=es8, op0=ALU.mult, op1=ALU.add); dr()
                first_max(es8, EPG, m2, i2, o2, tm)
                dx = small(1220, NT)
                e.tensor_tensor(dx, m2, m1, ALU.subtract).then_inc(S["te_x"], 1)
                M1, M2, MM = small(580, NT, NE), small(740, NT, NE), small(900, NT, NE)
                for t in range(NT):
                    for Mk, ok in ((M1, o1), (M2, o2)):
                        e.tensor_tensor(Mk[:, t, :].rearrange("p (g x) -> p g x", g=NG),
                                        goh[:, t, :].unsqueeze(2).to_broadcast((P, NG, EPG)),
                                        ok[:, t, :].unsqueeze(1).to_broadcast((P, NG, EPG)), ALU.mult)
                dr()
                e.tensor_tensor(MM, M1, M2, ALU.add).then_inc(S["lg_sb"], 1)
                e.wait_ge(S["ge_y"], l + 1)
                pg, wd = small(1225, NT), small(1230, NT)
                W1, W2 = small(1235, NT), small(1240, NT)
                e.tensor_reduce(pg, gx, AX, ALU.add); dr()
                e.wait_ge(S["te_y"], l + 1)
                e.scalar_tensor_tensor(out=wd, in0=dx, scalar=1.0, in1=pg, op0=ALU.add, op1=ALU.mult); dr()
                e.reciprocal(W1, wd); dr()
                e.tensor_tensor(W2, W1, dx, ALU.mult)
                e.wait_ge(S["rank_ps"], l + 1)
                rk, cnt = small(420, NT, NE), small(1245, NE)
                e.tensor_copy(rk, PS[6][:, 0:NT * NE].rearrange("p (t n) -> p t n", t=NT))
                e.tensor_copy(cnt, PS[6][:, NT * NE:NT * NE + NE]); dr()
                nov, cs, cs2 = small(1280, NE), small(1320, 16 + NE), small(1370, 16 + NE)
                e.tensor_scalar(nov, cnt, float(P), None, ALU.is_gt); dr()
                for j in range(2, 5):
                    e.scalar_tensor_tensor(out=nov, in0=cnt, scalar=float(P * j), in1=nov, op0=ALU.is_gt, op1=ALU.add); dr()
                e.memset(cs[:, 0:16], 0.0)
                e.memset(cs2[:, 0:16], 0.0)
                e.tensor_copy(cs[:, 16:16 + NE], nov); dr()
                a_, b_ = cs, cs2
                for j in (1, 2, 4, 8, 16):
                    e.tensor_tensor(b_[:, 16:16 + NE], a_[:, 16:16 + NE], a_[:, 16 - j:16 - j + NE], ALU.add); dr()
                    a_, b_ = b_, a_
                ovs = small(1630, NE)
                e.tensor_tensor(ovs, a_[:, 16:16 + NE], nov, ALU.subtract); dr()
                Mb, tt = small(580, 2, NT, NE), mt[:, 0, 0:2 * NT * NE].rearrange("p (k t n) -> p k t n", k=2, t=NT)
                rk_, ek, ok_, mk, sl = (small(160 + 10 * j, 2, NT) for j in range(5))
                bc = (P, 2, NT, NE)
                for dst, src in ((rk_, rk.unsqueeze(1)), (ek, iota[:, 0:NE].unsqueeze(1).unsqueeze(1)), (ok_, ovs.unsqueeze(1).unsqueeze(1))):
                    e.tensor_tensor(tt, Mb, src.to_broadcast(bc), ALU.mult); dr()
                    e.tensor_reduce(dst, tt, AX, ALU.add); dr()
                e.tensor_scalar(mk, rk_, float(P), None, ALU.is_ge); dr()
                for j in range(2, 5):
                    e.scalar_tensor_tensor(out=mk, in0=rk_, scalar=float(P * j), in1=mk, op0=ALU.is_ge, op1=ALU.add); dr()
                e.tensor_scalar(sl, mk, 0.0, None, ALU.is_gt)
                e.tensor_tensor(ok_, ok_, ek, ALU.subtract); dr()
                e.scalar_tensor_tensor(out=ok_, in0=ok_, scalar=float(NE - 1), in1=mk, op0=ALU.add, op1=ALU.add)
                e.scalar_tensor_tensor(out=rk_, in0=mk, scalar=float(-P), in1=rk_, op0=ALU.mult, op1=ALU.add); dr()
                e.tensor_tensor(ok_, ok_, sl, ALU.mult); dr()
                e.tensor_tensor(ek, ek, ok_, ALU.add); dr()
                e.tensor_tensor(place, iota[:].unsqueeze(1).to_broadcast((P, 2 * NT, P)),
                                small(160, 2 * NT).unsqueeze(2).to_broadcast((P, 2 * NT, P)), ALU.is_equal)
                e.tensor_tensor(blockno, iota[:, 0:NBLK].unsqueeze(1).to_broadcast((P, 2 * NT, NBLK)),
                                small(170, 2 * NT).unsqueeze(2).to_broadcast((P, 2 * NT, NBLK)), ALU.is_equal); dr()
                e.tensor_tensor(blockno, blockno, rowno[:].rearrange("p k t -> p (k t)").unsqueeze(2).to_broadcast((P, 2 * NT, NBLK)),
                                ALU.mult).then_inc(S["slot_rdy"], 1)
                ovf, cmp = small(1662, 1 + NOVF), mt[:, 1, 0:NOVF * NE].rearrange("p (i n) -> p i n", i=NOVF)
                e.tensor_tensor(cmp, a_[:, 16:16 + NE].unsqueeze(1).to_broadcast((P, NOVF, NE)),
                                iota[:, 0:NOVF].unsqueeze(2).to_broadcast((P, NOVF, NE)), ALU.is_le)
                e.tensor_copy(ovf[:, 0:1], a_[:, 16 + NE - 1:16 + NE]); dr()
                e.tensor_reduce(ovf[:, 1:], cmp, AX, ALU.add); dr()
                e.tensor_scalar(ovf[:, 1:], ovf[:, 1:], float(NE - 1), None, ALU.min); dr()
                e.tensor_scalar(ovf[:, 1:], ovf[:, 1:], 3.0, float(experts(l)), ALU.mult, ALU.add); dr()
                e.tensor_copy(ovn[:], ovf)
                for j in range(before_slots(l)):
                    modulation(l, 1, j, j)
                e.wait_ge(S["slot_ps"], l + 1)
                sf, sf2 = small(0, NBLK), small(50, NBLK)
                e.tensor_scalar(sf2, PS[6][:, 0:NBLK], 0.0, float(NOROW), ALU.is_equal, ALU.mult); dr()
                e.scalar_tensor_tensor(out=sf, in0=PS[6][:, 0:NBLK], scalar=-1.0, in1=sf2, op0=ALU.add, op1=ALU.add); dr()
                e.tensor_copy(slots[:], sf)
                e.tensor_scalar(sf2, sf, float(NTOK), float(-NTOK), ALU.is_ge, ALU.mult); dr()
                e.tensor_tensor(sf, sf, sf2, ALU.add); dr()
                e.tensor_copy(gidx[:], sf).then_inc(S["gidx_rdy"], 1)
                for j in range(before_slots(l), modd(l) // 2):
                    modulation(l, 1, j, j)
                bar()
                some = e.value_load(ovn[0:1, 0:1], min_val=0, max_val=NOVF)
                with e.If(some > 0):
                    with e.Fori(0, NOVF) as i:
                        n = i
                        e.wait_ge(S[f"ov_gate{l}"], n + 1)
                        e.tensor_tensor(hh[:, 0, :], PS[2][:, FF:2 * FF], sgate[:, 0, :], ALU.mult).then_inc(S[f"ov_h{l}"], 1)
                        e.wait_ge(S[f"ov_pe{l}"], 4 * n + 4)
                        e.tensor_copy(hhT[:, 0], PS[4][:, 0:256].rearrange("p (a b) -> p a b", a=2)).then_inc(S[f"ov_hT{l}"], 1)

                def rows_in(i, p):
                    m = 2 * i + (32 * l + p)
                    e.wait_ge(S["xgT_ps"], m + 1)
                    if not isinstance(i, int) or i:
                        e.wait_ge(S["gu_ps"], m - 1)
                    e.tensor_copy(xgT[:, p, 4:8, :], PS[1][:].rearrange("p (a b) -> p a b", a=4)).then_inc(S["xgT_sb"], 1)

                def gated(i, p):
                    m = 2 * i + (32 * l + p)
                    e.wait_ge(S["sgate_rdy"], m + 1)
                    if not isinstance(i, int) or i:
                        e.wait_ge(S["hhT_ps"], m - 1)
                    e.tensor_tensor(hh[:, p, :], PS[2 + p][:, FF:2 * FF], sgate[:, p, :], ALU.mult).then_inc(S["hh_rdy"], 1)

                def turned(i, p):
                    m = 2 * i + (32 * l + p)
                    e.wait_ge(S["hhT_ps"], m + 1)
                    if not isinstance(i, int) or i:
                        e.wait_ge(S["y2_ps"], m - 1)
                    e.tensor_copy(hhT[:, p], PS[4][:, 0:256].rearrange("p (a b) -> p a b", a=2)).then_inc(S["hhT_sb"], 1)

                def result(i, p):
                    m = 2 * i + (32 * l + p)
                    e.wait_ge(S["y2_ps"], m + 1)
                    if not isinstance(i, int) or i:
                        e.wait_ge(yfree[p], 16 * i + 16 * (NE // 2) * l)
                    e.tensor_copy(yb[:, p, 512:1024], PS[6][:]).then_inc(S["y2_sb_d"], 1)

                def pair(i, last=False):
                    turned(i, 0)
                    gated(i, 1)
                    if not last:
                        rows_in(i + 1, 0)
                    result(i, 0)
                    turned(i, 1)
                    if not last:
                        gated(i + 1, 0)
                        rows_in(i + 1, 1)
                    result(i, 1)

                rows_in(0, 0)
                gated(0, 0)
                rows_in(0, 1)
                pair(0)
                with e.Fori(1, NE // 2 - 1) as i:
                    pair(i)
                pair(NE // 2 - 1, True)
                e.wait_ge(S["ld_g2"], 32 * (l + 1))
                for t in range(NT):
                    e.wait_ge(yld[t], 32 * (l + 1))
                    e.wait_ge(S["y_half"], NT * l + t + 1)
                    e.scalar_tensor_tensor(out=mt[:, t % 2, :], in0=yk[1][:, t, :], scalar=W2[:, t:t + 1], in1=mt[:, t % 2, :],
                                           op0=ALU.mult, op1=ALU.add)
                    dr()
                    e.tensor_tensor(mt[:, t % 2, :], mt[:, t % 2, :], RA[:, cnd(t), :], ALU.mult); dr()
                    e.tensor_tensor(X[:, t, :], X[:, t, :], mt[:, t % 2, :], ALU.add).then_inc(S["x_rdy"], 1)
                bar()

        @block.tensor
        def _(e):
            bar = Bars(e)

            def arrived(q):
                e.wait_ge(full[q % RING], 16 * (q // RING + 1))

            def wt(q):
                return ring[:, q % RING, :].rearrange("p (k n) -> p k n", k=KD)

            e.wait_ge(S["silu_c"], 1)
            for n in range(MOD0 // 2):
                if n >= 2:
                    e.wait_ge(S["mod_sb"], n - 1)
                for h in range(2):
                    q = 2 * n + h
                    arrived(q)
                    for k in range(KD):
                        ins = e.matmul(PS[n % 2][0:2, 256 * h:256 * h + 256], condT[:, k, :], wt(q)[:, k, :], start=(k == 0), stop=(k == KD - 1))
                        if k == KD - 1:
                            ins.then_inc(free[q % RING], 1)
                e.drain().then_inc(S["mod_ps"], 1)
            e.wait_ge(S["cst"], 17)
            bar()

            def mod_rows(part, q0, lo, hi):
                for j in range(lo, hi):
                    for h in range(2):
                        q = q0 + 2 * j + h
                        arrived(q)
                        for k in range(KD):
                            ins = e.matmul(PS[MODBANK[part][j]][0:2, 256 * h:256 * h + 256], condT[:, k, :], wt(q)[:, k, :],
                                           start=(k == 0), stop=(k == KD - 1))
                        ins.then_inc(free[q % RING], 1)
                    if part:
                        e.drain().then_inc(S["fill_ps"], 1)

            for l in range(DEPTH):
                e.sem_inc(S[f"ov_pe{l}"], 1)
            for l in range(DEPTH):
                b = base(l)
                for t in range(NT):
                    e.wait_ge(S["xn_ready"], NT * l + t + 1)
                    if t >= 2:
                        e.wait_ge(S["hT_a"], NT * l + t - 1)
                        e.wait_ge(S["hT_d"], NT * l + t - 1)
                    for k in range(KD):
                        ins = e.transpose(PS[2 * (t % 2) + k // 4][:, (k % 4) * P:(k % 4 + 1) * P], xn[:, t % 2, k * P:(k + 1) * P], ident[:])
                    ins.then_inc(S["xT_ps"], 1)
                e.wait_ge(S["hT_a"], NT * (l + 1))
                e.wait_ge(S["hT_d"], NT * (l + 1))
                e.wait_ge(S["ld_par"], 16 * (l + 1))
                wdt = pr("wdt", KD, 8)
                for n in range(10):
                    q = b + n // 2
                    arrived(q)
                    if n in (2, 3):
                        e.wait_ge(S["ch_sb"], 8 * l + n - 1)
                    elif n in (4, 5):
                        e.wait_ge(S["ch_a"], 2 * l + n - 3)
                    elif n > 5:
                        e.wait_ge(S["ch_sb"], 8 * l + n - 3)
                    lat, cx = PS[2 * (n % 2)], PS[2 * (n % 2) + 1]
                    for out, lo, w in ((lat[:], CTX, LAT), (cx[:, 0:CTX], 0, CTX)):
                        for k in range(KD):
                            ins = e.matmul(out, wt(q)[:, k, P * (n % 2):P * (n % 2) + P], HT[:, k, lo:lo + w], start=(k == 0), stop=(k == KD - 1))
                    ins.then_inc(S["ch_ps"], 1)
                    if n % 2:
                        e.drain().then_inc(free[q % RING], 1)
                for n in range(15):
                    t, bank = n % NT, PS[4 + n % 2]
                    if n == 12:
                        e.wait_ge(S["uconv"], 2 * (l + 1))
                        e.wait_ge(S["ch_sb"], 8 * (l + 1))
                        for u in range(NT):
                            s = u * P + (0 if u == 0 else GPAD)
                            for j in range(2):
                                ins = e.transpose(PS[u // 2][:, 256 * (u % 2) + j * P:256 * (u % 2) + (j + 1) * P], uc[:, j, s:s + P], ident[:])
                            if u % 2 or u == NT - 1:
                                ins.then_inc(S["ut_ps"], 1)
                    if n >= 2:
                        e.wait_ge(S["pj_sb"], 15 * l + n - 1)
                    if n >= 5:
                        q = b + 3 + 2 * (n // NT)
                        arrived(q)
                        arrived(q + 1)
                        for h in range(2):
                            for k in range(KD):
                                ins = e.matmul(bank[:, 256 * h:256 * h + 256], HT[:, k, t * P:(t + 1) * P], wt(q + h)[:, k, :],
                                               start=(k == 0), stop=(k == KD - 1))
                        ins.then_inc(S["pj_ps"], 1)
                        if t == NT - 1:
                            for h in range(2):
                                e.drain().then_inc(free[(q + h) % RING], 1)
                    else:
                        for k in range(KD):
                            ins = e.matmul(bank[:, 0:8], HT[:, k, t * P:(t + 1) * P], wdt[:, k, :], start=(k == 0), stop=(k == KD - 1))
                        ins.then_inc(S["pj_ps"], 1)

                e.wait_ge(S["la_rdy"], l + 1)
                e.matmul(PS[7][:, 0:40], triF[:], small(1020, 40), start=True, stop=True)
                e.matmul(PS[7][:, 40:80], triB[:], small(1060, 40), start=True, stop=True)
                e.matmul(PS[7][:, 80:160], ones[:], small(1020, 80), start=True, stop=True).then_inc(S["cum_ps"], 1)

                def at(n, t):
                    s = t * P + (0 if t == 0 else XPAD)
                    return cv[:, n, s:s + P]

                e.wait_ge(S["convs_rdy"], 6 * (l + 1))
                e.wait_ge(S["ut_sb"], 3 * (l + 1))
                for n in range(7):
                    if n >= 2:
                        e.wait_ge(S["xt_sb"], 7 * l + n - 1)
                    src = [(j, n) for j in range(4)] if n < 5 else [(4, t) for t in (range(4) if n == 5 else (4,))]
                    for i, (j, t) in enumerate(src):
                        ins = e.transpose(PS[n % 2][:, i * P:(i + 1) * P], at(j, t), ident[:])
                    ins.then_inc(S["xt_ps"], 1)
                e.wait_ge(S["qk_rdy"], 2 * (l + 1))
                for t in range(NT):
                    if t >= 2:
                        e.wait_ge(S["qkT_sb"], NT * l + t - 1)
                    for j in range(3):
                        ins = e.transpose(PS[2 + t % 2][:, j * P:(j + 1) * P], qkv[:, t, j * P:(j + 1) * P], ident[:])
                    ins.then_inc(S["qkT_ps"], 1)
                e.wait_ge(S["xt_sb"], 7 * (l + 1))
                e.wait_ge(S["qkT_sb"], NT * (l + 1))
                e.wait_ge(S["cum_sb"], l + 1)
                e.wait_ge(S["pj_sb"], 15 * (l + 1))

                def att_scores(t):
                    for h in range(QH):
                        if t:
                            e.wait_ge(S["att_exp"], 20 * l + 4 * (t - 1) + h + 1)
                        kv, g = h // 2, h % 2
                        r = slice(64 * kv, 64 * kv + 64)
                        q = qkT[r, g, t * P:(t + 1) * P]
                        if t == 0:
                            ins = e.matmul(PS[h][:, 0:P], q, qkT[r, 2, 0:P], start=True, stop=True)
                        else:
                            nb = near(t)
                            w = P * len(nb)
                            e.matmul(PS[h][:, 0:P], q, pr("kctx")[r, :], start=True, stop=False, skip_group_check=True)
                            ins = e.matmul(PS[h][:, P:P + w], q, qkT[r, 2, nb[0] * P:nb[0] * P + w], start=False, stop=True, skip_group_check=True)
                            for i, j in enumerate(nb):
                                if j != t:
                                    ins = e.matmul(PS[h][:, P + i * P:P + i * P + P], ident16[:], (negF if j < t else negB)[:],
                                                   start=False, stop=True, skip_group_check=True)
                        ins.then_inc(S["att_s"], 1)

                att_scores(0)
                for t in range(NT):
                    if t + 1 < NT:
                        att_scores(t + 1)
                    nb = [0] if t == 0 else [-1] + near(t)

                    def pv(h):
                        n = 4 * t + h
                        kv = h // 2
                        if h % 2 == 0:
                            e.wait_ge(S["ptc_a"], 10 * l + n // 2 + 1)
                        else:
                            e.wait_ge(S["ptc_d"], 10 * l + n // 2 + 1)
                        if t >= 2 and h == 0:
                            e.wait_ge(S["att_o"], NT * l + t - 1)
                        for i, j in enumerate(nb):
                            v = pr("vctx")[:, 64 * kv:64 * kv + 64] if j < 0 else qkv[:, j, 384 + 64 * kv:448 + 64 * kv]
                            ins = e.matmul(PS[6 + t % 2][:, 64 * h:64 * h + 64], PTs[:, h % 2, i, :], v, start=(i == 0), stop=(i == len(nb) - 1))
                        ins.then_inc(S["att_pv"], 1)

                    for h in range(QH):
                        n = 4 * t + h
                        e.wait_ge(S["att_exp"], 20 * l + n + 1)
                        if n >= 2:
                            if h % 2 == 0:
                                e.wait_ge(S["ptc_a"], 10 * l + n // 2)
                            else:
                                e.wait_ge(S["ptc_d"], 10 * l + n // 2)
                        for i in range(len(nb)):
                            ins = e.transpose(PS[4 + h % 2][:, i * P:(i + 1) * P], Pm[:, h, i * P:(i + 1) * P], ident[:])
                        ins.then_inc(S["att_pt"], 1)
                        if h:
                            pv(h - 1)
                    pv(3)
                bar()
                la4 = small(1020, 2, NT, 8)

                def ssd_pre(c):
                    if c:
                        e.wait_ge(S["gt_sb"], NT * l + c)
                    for g in range(2):
                        r = slice(64 * g, 64 * g + 64)
                        ins = e.matmul(PS[6 + g][:, 0:P], at(4, c)[r], at(5, c)[r], start=True, stop=True)
                    ins.then_inc(S["gt_ps"], 1)
                    for u in range(4):
                        d, g = u // 2, u % 2
                        if c:
                            e.wait_ge(S["l_rdy"], 20 * l + 4 * (c - 1) + u + 1)
                        e.matmul(PS[u][:], ident16[:], (negB if d else negF)[:].unsqueeze(1).to_broadcast((P, 4, P)),
                                 start=True, stop=False, skip_group_check=True)
                        for j in range(4):
                            ins = e.matmul(PS[u][:, j * P:(j + 1) * P], la4[:, d, c, 4 * g + j:4 * g + j + 1].to_broadcast((P, P)),
                                           (triB if d else triF)[:], start=False, stop=True, skip_group_check=True)
                        ins.then_inc(S["r_ps"], 1)

                ssd_pre(0)
                for c in range(NT):
                    if c + 1 < NT:
                        ssd_pre(c + 1)
                    e.wait_ge(S["xd_rdy"], NT * l + c + 1)
                    if c:
                        e.wait_ge(S["y_sb"], NT * l + c)
                    for d in range(2):
                        for g in range(2):
                            ins = e.matmul(PS[5][64 * g:64 * g + 64, 256 * d:256 * d + 256], btok[:, c, 64 * g:64 * g + 64],
                                           xw[:, d, 256 * g:256 * g + 256], start=True, stop=True)
                    e.wait_ge(S["w_rdy"], 20 * l + 4 * c + 4)
                    for h in range(NH):
                        for d in range(2):
                            ins = e.matmul(PS[4][:, 64 * h:64 * h + 64], LW[:, 2 * d + h // 4, h % 4, :], xdt[:, d, 64 * h:64 * h + 64],
                                           start=(d == 0), stop=(d == 1))
                    e.drain().then_inc(S["y_ps"], 1)
                    e.drain().then_inc(S["s_ps"], 1)
                e.wait_ge(S["gt_sb"], NT * (l + 1))
                mod_rows(0, b + INN, 0, 2)
                e.wait_ge(S["hs_rdy"], l + 1)
                for i in range(NLT):
                    if i >= 2:
                        e.wait_ge(S["off_sb"], NLT * l + i - 1)
                    for d in range(2):
                        for g in range(2):
                            r = slice(64 * g, 64 * g + 64)
                            ins = e.matmul(PS[2 * (i % 2) + g][:, 256 * d:256 * d + 256], at(5, i + 1)[r], hs[r, d, i, :], start=True, stop=True)
                    ins.then_inc(S["off_ps"], 1)
                e.wait_ge(S["y_sb"], NT * (l + 1))
                mod_rows(0, b + INN, 2, 4)
                e.wait_ge(S["off_sb"], NLT * l + 3)
                mod_rows(0, b + INN, 4, 6)
                bar()
                e.drain().then_inc(S["fill_ps"], MODC // 2)
                e.wait_ge(S["cat_b"], l + 1)
                e.wait_ge(S["fill_sb"], mod_chunks(l, 0) + 2)

                def to_channels(signal, a, d_, src):
                    for t in range(NT):
                        if t >= 2:
                            e.wait_ge(S[a], NT * l + t - 1)
                            e.wait_ge(S[d_], NT * l + t - 1)
                        if src == "h2":
                            e.wait_ge(S["h2_rdy"], NT * l + t + 1)
                        for k in range(KD):
                            ins = e.transpose(PS[2 * (t % 2) + k // 4][:, (k % 4) * P:(k % 4 + 1) * P], CAT[:, t, k * P:(k + 1) * P], ident[:])
                        ins.then_inc(S[signal], 1)
                    e.wait_ge(S[a], NT * (l + 1))
                    e.wait_ge(S[d_], NT * (l + 1))

                to_channels("ct_ps", "ct_sb_a", "ct_sb_d", "cat")
                e.wait_ge(S["fill_sb"], mod_chunks(l, 0) + MODC // 2)
                for n in range(2 * NT):
                    t, hf = n % NT, n // NT
                    q = b + INN + MODC + 2 * hf
                    arrived(q)
                    arrived(q + 1)
                    if n >= 2:
                        e.wait_ge(S["wo_sb"], 10 * l + n - 1)
                    for j in range(2):
                        for k in range(KD):
                            ins = e.matmul(PS[4 + n % 2][:, 256 * j:256 * j + 256], HT[:, k, t * P:(t + 1) * P], wt(q + j)[:, k, :],
                                           start=(k == 0), stop=(k == KD - 1))
                    ins.then_inc(S["wo_ps"], 1)
                    if t == NT - 1:
                        for j in range(2):
                            e.drain().then_inc(free[(q + j) % RING], 1)
                to_channels("h2T_ps", "h2T_a", "h2T_d", "h2")
                rw = pr("rw", KD, 36)
                for t in range(NT):
                    if t >= 2:
                        e.wait_ge(S["lg_sb"], 6 * l + t - 1)
                    for k in range(KD):
                        ins = e.matmul(PS[4 + t % 2][:, 0:36], HT[:, k, t * P:(t + 1) * P], rw[:, k, :], start=(k == 0), stop=(k == KD - 1))
                    ins.then_inc(S["lg_ps"], 1)
                MM = small(900, NT, NE)
                mod_rows(1, b + INN + MODC + OUTN, 0, 1)
                e.wait_ge(S["lg_sb"], 6 * (l + 1))
                for t in range(NT):
                    for j in range(t + 1):
                        e.matmul(PS[6][:, NE * t:NE * t + NE], (triS if j == t else ones)[:], MM[:, j, :], start=(j == 0), stop=(j == t))
                for j in range(NT):
                    ins = e.matmul(PS[6][:, NE * NT:NE * NT + NE], ones[:], MM[:, j, :], start=(j == 0), stop=(j == NT - 1))
                ins.then_inc(S["rank_ps"], 1)
                mod_rows(1, b + INN + MODC + OUTN, 1, before_slots(l))
                e.wait_ge(S["slot_rdy"], l + 1)
                for j in range(2 * NT):
                    ins = e.matmul(PS[6][:, 0:NBLK], place[:, j, :], blockno[:, j, :], start=(j == 0), stop=(j == 2 * NT - 1))
                ins.then_inc(S["slot_ps"], 1)
                mod_rows(1, b + INN + MODC + OUTN, before_slots(l), modd(l) // 2)
                e.wait_ge(S["fill_sb"], mod_chunks(l, 1) + modd(l) // 2)
                bar()
                b2 = experts(l)

                some = e.value_load(ovn[0:1, 0:1], min_val=0, max_val=NOVF)
                with e.If(some > 0):
                    with e.Fori(0, NOVF) as i:
                        n = i
                        e.wait_ge(S[f"ov_gather{l}"], 16 * (n + 1))
                        for k in range(KD):
                            ins = e.transpose(PS[k // 4][:, (k % 4) * P:(k % 4 + 1) * P], xg[:, 0, k * P:(k + 1) * P], ident[:])
                        ins.then_inc(S[f"ov_pe{l}"], 1)
                        e.wait_ge(S[f"ov_x{l}"], n + 1)
                        e.wait_ge(S[f"ov_w{l}"], 48 * (n + 1))
                        for j in range(2):
                            for k in range(KD):
                                ins = e.matmul(PS[2][:, FF * j:FF * j + FF], xgT[:, 0, k, :], wov_gu[:, j, k, :],
                                               start=(k == 0), stop=(k == KD - 1))
                        ins.then_inc(S[f"ov_pe{l}"], 1)
                        e.wait_ge(S[f"ov_h{l}"], n + 1)
                        for k in range(2):
                            ins = e.transpose(PS[4][:, k * P:(k + 1) * P], hh[:, 0, k * P:(k + 1) * P], ident[:])
                        ins.then_inc(S[f"ov_pe{l}"], 1)
                        e.wait_ge(S[f"ov_hT{l}"], n + 1)
                        e.wait_ge(S[f"ov_y{l}"], n + 1)
                        for j in range(2):
                            for k in range(2):
                                ins = e.matmul(PS[5 + j][:], hhT[:, 0, k, :], wov_d[:, k, 512 * j:512 * j + 512],
                                               start=(k == 0), stop=(k == 1))
                        ins.then_inc(S[f"ov_pe{l}"], 1)

                def tile(i, p, j):
                    q = b2 + 3 * p + j
                    return q % RING, i + q // RING

                def rows_in(i, p):
                    m = 2 * i + (32 * l + p)
                    e.wait_ge(gfull[p], 16 * i + 16 * ((NE // 2) * l + 1))
                    if not isinstance(i, int) or i or p:
                        e.wait_ge(S["xgT_sb"], 2 * m)
                    for k in range(KD):
                        ins = e.transpose(PS[k // 4][:, (k % 4) * P:(k % 4 + 1) * P], xg[:, p, k * P:(k + 1) * P], ident[:])
                    ins.then_inc(S["xgT_ps"], 1)

                def up(i, p, j, used=None):
                    m = 2 * i + (32 * l + p)
                    if j == 0:
                        e.wait_ge(S["xgT_sb"], 2 * m + 2)
                        if not isinstance(i, int) or i:
                            e.wait_ge(S["hh_rdy"], m - 1)
                    slot, use = tile(i, p, j)
                    e.wait_ge(full[slot], 16 * use + 16)
                    w = ring[:, slot, :].rearrange("p (k n) -> p k n", k=KD)
                    for k in range(KD):
                        ins = e.matmul(PS[2 + p][:, FF * j:FF * j + FF], xgT[:, p, k, :], w[:, k, :], start=(k == 0), stop=(k == KD - 1))
                        if k == 0 and used is not None:
                            ins.then_inc(free[used], 1)
                    if j:
                        ins.then_inc(S["gu_ps"], 1)
                    else:
                        ins.then_inc(free[slot], 1)

                def turn(i, p):
                    m = 2 * i + (32 * l + p)
                    e.wait_ge(S["hh_rdy"], m + 1)
                    if not isinstance(i, int) or i or p:
                        e.wait_ge(S["hhT_sb"], m)
                    for k in range(2):
                        ins = e.transpose(PS[4][:, k * P:(k + 1) * P], hh[:, p, k * P:(k + 1) * P], ident[:])
                    ins.then_inc(S["hhT_ps"], 1)

                def down(i, p, used):
                    m = 2 * i + (32 * l + p)
                    e.wait_ge(S["hhT_sb"], m + 1)
                    slot, use = tile(i, p, 2)
                    e.wait_ge(full[slot], 16 * use + 16)
                    if not isinstance(i, int) or i or p:
                        e.wait_ge(S["y2_sb_a"], m)
                        e.wait_ge(S["y2_sb_d"], m)
                    wd = ring[:, slot, :].rearrange("p (k n) -> p k n", k=2)
                    for k in range(2):
                        for j in range(2):
                            ins = e.matmul(PS[5 + j][:], hhT[:, p, k, :], wd[:, k, 512 * j:512 * j + 512], start=(k == 0), stop=(k == 1))
                            if k == 0 and j == 0 and used is not None:
                                ins.then_inc(free[used], 1)
                    ins.then_inc(S["y2_ps"], 1)

                def pair(i, last=False):
                    up(i, 1, 0, None if isinstance(i, int) and i == 0 else tile(0, 1, 2)[0])
                    turn(i, 0)
                    up(i, 1, 1)
                    if not last:
                        rows_in(i + 1, 0)
                    down(i, 0, tile(0, 1, 1)[0])
                    if not last:
                        up(i + 1, 0, 0, tile(0, 0, 2)[0])
                        turn(i, 1)
                        up(i + 1, 0, 1)
                        rows_in(i + 1, 1)
                        down(i, 1, tile(0, 0, 1)[0])
                    else:
                        turn(i, 1)
                        down(i, 1, tile(0, 0, 2)[0])
                        e.drain().then_inc(free[tile(0, 1, 2)[0]], 1)

                rows_in(0, 0)
                up(0, 0, 0)
                up(0, 0, 1)
                e.drain().then_inc(free[tile(0, 0, 1)[0]], 1)
                rows_in(0, 1)
                pair(0)
                with e.Fori(1, NE // 2 - 1) as i:
                    pair(i)
                pair(NE // 2 - 1, True)
                bar()


def near(t):
    return [j for j in (t - 1, t, t + 1) if 1 <= j < NT]


def _tiles(w):
    n = w.shape[1] // 256
    return w.reshape(KD, P, n, 256).transpose(2, 1, 0, 3).reshape(n, P, SLOT)


def _cols(v):
    return v.reshape(-1, P).T


def _rows(v):
    return np.broadcast_to(v.reshape(1, -1), (P, v.size))


def kernel(**inputs):
    import concourse.bacc as _bacc
    from concourse.bass_utils import run_bass_kernel_spmd as _run

    a = {k: np.asarray(v) for k, v in inputs.items()}
    f = np.float32
    x = np.concatenate([a["x_prompt"][0], a["x_sample"][0]]).reshape(NT, P, D).transpose(1, 0, 2)
    stream = np.empty((experts(DEPTH - 1) + 3 * NE, P, SLOT), f)
    par = np.empty((DEPTH, P, PARN), f)
    order = np.arange(6 * D)
    order[:2 * D] = order[:2 * D].reshape(2, KD, P).transpose(0, 2, 1).ravel()
    for l in range(DEPTH):
        b = base(l)
        mod = _tiles(a["mod_w"][l][:, order])
        first = b - MOD0 if l == 0 else experts(l - 1) - MOD0
        stream[first:first + MOD0] = mod[:MOD0]
        stream[b + INN:b + INN + MODC] = mod[MOD0:MOD0 + MODC]
        b2 = b + INN + MODC + OUTN
        stream[b2:b2 + D // 256] = mod[MOD0 + MODC:]
        w = a["w_in"][l]
        w = np.concatenate([w[:, 2056:2312], w[:, 1800:2056], w[:, 1024:1792], w[:, :1024]], 1)
        stream[b:b + INN] = _tiles(w)
        stream[b2 - OUTN:b2] = _tiles(a["w_out"][l])
        ex = stream[experts(l):experts(l) + 3 * NE].reshape(NE, 3, P, SLOT)
        for j, n in enumerate(("expert_w_gate", "expert_w_up")):
            ex[:, j] = a[n][l].reshape(NE, KD, P, FF).transpose(0, 2, 1, 3).reshape(NE, P, SLOT)
        ex[:, 2] = a["expert_w_down"][l].reshape(NE, 2, P, D).transpose(0, 2, 1, 3).reshape(NE, P, SLOT)

        def put(name, v):
            o, n = PAR[name]
            par[l, :, o:o + n] = v.reshape(P, n)

        put("norm1", _cols(a["norm1_w"][l]))
        put("qw", _rows(a["q_norm_w"][l]))
        put("kw", _rows(a["k_norm_w"][l]))
        put("sink", _rows(a["attn_sink"][l]))
        put("cw", a["ssd_conv_w"][l].reshape(5, 6, P).transpose(2, 1, 0))
        put("cb", _cols(a["ssd_conv_b"][l]))
        put("gw", a["cm_conv_w"][l].reshape(31, 2, P).transpose(2, 1, 0))
        put("gb", _cols(a["cm_conv_b"][l]))
        put("dtb", _rows(a["ssd_dt_bias"][l]))
        put("alog", _rows(a["ssd_a_log"][l]))
        put("dskip", _rows(a["ssd_d"][l]))
        put("snorm", _rows(a["ssd_norm_w"][l]))
        put("lnw", _rows(a["cm_norm_w"][l]))
        put("lnb", _rows(a["cm_norm_b"][l]))
        put("rw", np.concatenate([a["router_group_w"][l], a["router_expert_w"][l]], 1).reshape(KD, P, 36).transpose(1, 0, 2))
        put("rb", _rows(np.concatenate([a["router_group_b"][l], a["router_expert_b"][l]])))
        put("wdt", a["w_in"][l][:, 1792:1800].reshape(KD, P, 8).transpose(1, 0, 2))
        put("kctx", a["cache_k"][0, l].reshape(P, P).T)
        put("vctx", a["cache_v"][0, l].reshape(P, P))
        put("h0", a["state_ssm"][0, l].reshape(2, 2, 4, HD, HD).transpose(1, 4, 0, 2, 3))
    cond = np.stack([a["c_ctx"], a["c"][0]]).reshape(2, KD, P).transpose(2, 1, 0)
    modb = np.broadcast_to(a["mod_b"][:, order], (2, DEPTH, 6 * D))
    pos = np.arange(LAT)
    inv = (f(10000.0) ** (-np.arange(16, dtype=f) / f(16))).astype(f)
    ang = np.stack([(pos // 64).astype(f)[:, None] * inv, (pos % 64).astype(f)[:, None] * inv], 1)
    cs, sn = np.cos(ang), np.sin(ang)
    rope = np.stack([np.stack([cs, cs], 2), np.stack([-sn, sn], 2)]).reshape(2, NLT, P, HD).transpose(2, 0, 1, 3)

    nc = _bacc.Bacc("TRN2", target_bir_lowering=False, num_devices=1)
    arrays, args = {}, []
    for name, v in (("x", x), ("stream", stream), ("par", par), ("cond", cond), ("modb", modb),
                    ("n2row", a["norm2_w"]), ("rope", rope)):
        v = np.ascontiguousarray(v, dtype=f)
        arrays[f"in_{name}"] = v
        args.append(nc.dram_tensor(f"in_{name}", v.shape, F32, kind="ExternalInput").ap())
    outs = (("y", (P, NT, D)), ("k", (DEPTH, P, 128)), ("v", (DEPTH, P, 128)), ("st", (DEPTH, P, 2, 256)))
    for name, shape in outs:
        args.append(nc.dram_tensor(f"out_{name}", shape, F32, kind="ExternalOutput").ap())
    build(nc, *args)
    r = _run(nc, [arrays], core_ids=[0]).results[0]
    y = r["out_y"].transpose(1, 0, 2).reshape(NTOK, D)
    st = r["out_st"].reshape(DEPTH, 2, HD, 2, 4, HD).transpose(0, 3, 1, 4, 5, 2).reshape(1, DEPTH, 2, NH, HD, HD)
    return (y[None, :CTX].copy(), y[None, CTX:].copy(), r["out_k"].reshape(1, DEPTH, CTX, KVH, HD),
            r["out_v"].reshape(1, DEPTH, CTX, KVH, HD), np.ascontiguousarray(st))
```
